# Optimizing a Trainium2 kernel written in Bass

```python
import jax
import jax.numpy as jnp
from jax import lax
import numpy as np
import math
import jax, jax.numpy as jnp

D_MODEL = 1024
BATCH = 1
SEQ = 256
DEPTH = 2

CTX_LEN = 256
GRID_W = 64
N_HEADS = 16
HEAD_DIM = D_MODEL // N_HEADS
D_FF = 2816
N_MIXERS = 2
NA_KH_MAX = 8
NA_KW = 16
NA_QC = 16
NA_KBW = 2 * NA_KW
CONV_W = 3
ROPE_BASE = 10000.0
N_MOD = 9
N_NA_LAYERS = (DEPTH + N_MIXERS - 1) // N_MIXERS
N_CONV_LAYERS = DEPTH // N_MIXERS
DN_ALPHA = (2.0 * DEPTH) ** 0.25
DN_BETA = (8.0 * DEPTH) ** -0.25
LN_EPS = 1e-6


def layer_norm(x, g, b):
    xf = x.astype(jnp.float32)
    mu = jnp.mean(xf, axis=-1, keepdims=True)
    var = jnp.mean(jnp.square(xf - mu), axis=-1, keepdims=True)
    return ((xf - mu) * lax.rsqrt(var + LN_EPS)).astype(x.dtype) * g + b

def modulate(x, shift, scale):
    return x * (1 + scale) + shift

def post_norm_update(x, y, gate, res_w, g, b):
    return layer_norm(DN_ALPHA * x + res_w * gate * y, g, b)

def swiglu_ffn(h, w_in, w_out):
    a, u = jnp.split(h @ w_in, 2, axis=-1)
    return (jax.nn.silu(a) * u) @ w_out

def half_step_ffn(x, shift, scale, gate, w_in, w_out, g, b):
    y = swiglu_ffn(modulate(x, shift, scale), w_in, w_out)
    return post_norm_update(x, y, gate, 0.5, g, b)

def axial_rope_tables(n_tok):
    t = np.arange(n_tok)
    n_freq = HEAD_DIM // 4
    inv_freq = ROPE_BASE ** (-np.arange(n_freq) / n_freq)
    ang_row = (t // GRID_W)[:, None] * inv_freq[None]
    ang_col = (t % GRID_W)[:, None] * inv_freq[None]
    return (jnp.asarray(np.cos(ang_row), jnp.float32), jnp.asarray(np.sin(ang_row), jnp.float32),
            jnp.asarray(np.cos(ang_col), jnp.float32), jnp.asarray(np.sin(ang_col), jnp.float32))

def _rotate(x, cos, sin):
    x1, x2 = jnp.split(x, 2, axis=-1)
    cos = cos[None, :, None, :].astype(x.dtype)
    sin = sin[None, :, None, :].astype(x.dtype)
    return jnp.concatenate([x1 * cos - x2 * sin, x2 * cos + x1 * sin], axis=-1)

def apply_axial_rope(x, tables):
    cos_r, sin_r, cos_c, sin_c = tables
    half = HEAD_DIM // 2
    return jnp.concatenate([_rotate(x[..., :half], cos_r, sin_r),
                            _rotate(x[..., half:], cos_c, sin_c)], axis=-1)

def neighbourhood_attention(hx, hc, w_qkv, w_out, rpb, rope, with_ctx_queries):
    B, S, D = hx.shape
    rows = S // GRID_W
    kh = min(NA_KH_MAX, rows)
    ncb = GRID_W // NA_QC
    nk = kh * NA_KBW
    scale = HEAD_DIM ** -0.5

    qkv = (hx @ w_qkv).reshape(B, S, 3, N_HEADS, HEAD_DIM)
    q = apply_axial_rope(qkv[:, :, 0], rope)
    k = apply_axial_rope(qkv[:, :, 1], rope)
    v = qkv[:, :, 2]
    qkv_c = (hc @ w_qkv).reshape(B, hc.shape[1], 3, N_HEADS, HEAD_DIM)
    q_c, k_c, v_c = qkv_c[:, :, 0], qkv_c[:, :, 1], qkv_c[:, :, 2]

    q_col = np.arange(ncb)[:, None] * NA_QC + np.arange(NA_QC)[None]
    win_c0 = np.clip(q_col - NA_KW // 2, 0, GRID_W - NA_KW)
    blk_c0 = np.clip(np.arange(ncb) * NA_QC - NA_KW // 2, 0, GRID_W - NA_KBW)
    key_col = blk_c0[:, None] + np.arange(NA_KBW)[None]
    col_ok = (key_col[:, None, :] >= win_c0[..., None]) & (key_col[:, None, :] < win_c0[..., None] + NA_KW)
    mask = jnp.asarray(np.broadcast_to(col_ok[:, :, None, :], (ncb, NA_QC, kh, NA_KBW)).reshape(ncb, NA_QC, nk))
    dx_idx = np.clip(key_col[:, None, :] - q_col[..., None] + NA_KW - 1, 0, 2 * NA_KW - 2)
    dx_b = np.broadcast_to(dx_idx[:, :, None, :], (ncb, NA_QC, kh, NA_KBW))

    k_grid = k.reshape(B, rows, GRID_W, N_HEADS, HEAD_DIM)
    v_grid = v.reshape(B, rows, GRID_W, N_HEADS, HEAD_DIM)
    q_rows = jnp.moveaxis(q.reshape(B, rows, ncb, NA_QC, N_HEADS, HEAD_DIM), 1, 0)

    def row_block(args):
        r, q_r = args
        rs = jnp.clip(r - kh // 2, 0, rows - kh)
        k_rows = lax.dynamic_slice_in_dim(k_grid, rs, kh, axis=1)
        v_rows = lax.dynamic_slice_in_dim(v_grid, rs, kh, axis=1)
        k_blk = jnp.moveaxis(k_rows[:, :, key_col], 2, 1).reshape(B, ncb, nk, N_HEADS, HEAD_DIM)
        v_blk = jnp.moveaxis(v_rows[:, :, key_col], 2, 1).reshape(B, ncb, nk, N_HEADS, HEAD_DIM)
        dy_idx = rs + jnp.arange(kh) - r + NA_KH_MAX - 1
        bias = rpb[:, dy_idx[None, None, :, None], dx_b].reshape(N_HEADS, ncb, NA_QC, nk)
        s_win = jnp.einsum('bjqhd,bjkhd->bhjqk', q_r, k_blk).astype(jnp.float32) * scale
        s_win = jnp.where(mask, s_win + bias.astype(jnp.float32)[None], -jnp.inf)
        s_ctx = jnp.einsum('bjqhd,bchd->bhjqc', q_r, k_c).astype(jnp.float32) * scale
        p = jax.nn.softmax(jnp.concatenate([s_win, s_ctx], axis=-1), axis=-1).astype(v.dtype)
        return (jnp.einsum('bhjqk,bjkhd->bjqhd', p[..., :nk], v_blk)
                + jnp.einsum('bhjqc,bchd->bjqhd', p[..., nk:], v_c))

    o = lax.map(row_block, (jnp.arange(rows), q_rows))
    y_lat = jnp.moveaxis(o, 0, 1).reshape(B, S, D) @ w_out

    y_ctx = None
    if with_ctx_queries:
        s = jnp.einsum('bqhd,bkhd->bhqk', q_c, k_c).astype(jnp.float32) * scale
        p = jax.nn.softmax(s, axis=-1).astype(v_c.dtype)
        y_ctx = jnp.einsum('bhqk,bkhd->bqhd', p, v_c).reshape(B, hc.shape[1], D) @ w_out
    return y_lat, y_ctx

def short_conv_mixer(h, w_in, conv_w, w_out):
    b_gate, c_gate, hv = jnp.split(h @ w_in, 3, axis=-1)
    u = c_gate * hv
    n = u.shape[1]
    pad = CONV_W // 2
    up = jnp.pad(u, ((0, 0), (pad, pad), (0, 0)))
    y = conv_w[0] * up[:, 0:n]
    for j in range(1, CONV_W):
        y = y + conv_w[j] * up[:, j:j + n]
    return (b_gate * y) @ w_out

def first_inputs(seed: int = 0) -> dict:
    key = jax.random.key(seed)
    ks = jax.random.split(key, 16)
    D, F = D_MODEL, D_FF

    def nrm(k, shape, s):
        return jax.random.normal(k, shape, jnp.float32) * s

    return {
        "x": nrm(ks[0], (BATCH, SEQ, D), 1.0),
        "c": nrm(ks[1], (BATCH, D), 1.0),
        "ctx": nrm(ks[2], (BATCH, CTX_LEN, D), 1.0),
        "c_ctx": nrm(ks[3], (D,), 1.0),
        "ada_w": nrm(ks[4], (DEPTH, D, N_MOD * D), 0.5 * D ** -0.5),
        "ada_b": nrm(ks[5], (DEPTH, N_MOD * D), 0.02),
        "ln_g": 1.0 + nrm(ks[6], (DEPTH, 3, D), 0.02),
        "ln_b": nrm(ks[7], (DEPTH, 3, D), 0.02),
        "ffn_w_in": nrm(ks[8], (DEPTH, 2, D, 2 * F), D ** -0.5),
        "ffn_w_out": nrm(ks[9], (DEPTH, 2, F, D), DN_BETA * F ** -0.5),
        "na_w_qkv": nrm(ks[10], (N_NA_LAYERS, D, 3 * D), D ** -0.5),
        "na_w_out": nrm(ks[11], (N_NA_LAYERS, D, D), DN_BETA * D ** -0.5),
        "na_rpb": nrm(ks[12], (N_NA_LAYERS, N_HEADS, 2 * NA_KH_MAX - 1, 2 * NA_KW - 1), 0.1),
        "sc_w_in": nrm(ks[13], (N_CONV_LAYERS, D, 3 * D), D ** -0.5),
        "sc_conv": nrm(ks[14], (N_CONV_LAYERS, CONV_W, D), CONV_W ** -0.5),
        "sc_w_out": nrm(ks[15], (N_CONV_LAYERS, D, D), DN_BETA * D ** -0.5),
    }

def first_block(x, c, ctx, c_ctx, ada_w, ada_b, ln_g, ln_b, ffn_w_in, ffn_w_out,
              na_w_qkv, na_w_out, na_rpb, sc_w_in, sc_conv, sc_w_out):
    B, S, D = x.shape
    rope = axial_rope_tables(S)
    last_na = max(range(0, DEPTH, N_MIXERS))
    s_c = jax.nn.silu(c)
    s_cc = jax.nn.silu(c_ctx)
    for i in range(DEPTH):
        ctx_in = i <= last_na
        ctx_out = i < last_na
        j = i // N_MIXERS
        m = (s_c @ ada_w[i] + ada_b[i]).reshape(B, N_MOD, 1, D)
        mc = (s_cc @ ada_w[i] + ada_b[i]).reshape(N_MOD, D)

        x = half_step_ffn(x, m[:, 0], m[:, 1], m[:, 2], ffn_w_in[i, 0], ffn_w_out[i, 0], ln_g[i, 0], ln_b[i, 0])
        if ctx_in:
            ctx = half_step_ffn(ctx, mc[0], mc[1], mc[2], ffn_w_in[i, 0], ffn_w_out[i, 0], ln_g[i, 0], ln_b[i, 0])

        hx = modulate(x, m[:, 3], m[:, 4])
        y_ctx = None
        if i % N_MIXERS == 0:
            hc = modulate(ctx, mc[3], mc[4])
            y_lat, y_ctx = neighbourhood_attention(hx, hc, na_w_qkv[j], na_w_out[j], na_rpb[j], rope, ctx_out)
        else:
            y_lat = short_conv_mixer(hx, sc_w_in[j], sc_conv[j], sc_w_out[j])
            if ctx_out:
                y_ctx = short_conv_mixer(modulate(ctx, mc[3], mc[4]), sc_w_in[j], sc_conv[j], sc_w_out[j])
        x = post_norm_update(x, y_lat, m[:, 5], 1.0, ln_g[i, 1], ln_b[i, 1])
        if ctx_out:
            ctx = post_norm_update(ctx, y_ctx, mc[5], 1.0, ln_g[i, 1], ln_b[i, 1])

        x = half_step_ffn(x, m[:, 6], m[:, 7], m[:, 8], ffn_w_in[i, 1], ffn_w_out[i, 1], ln_g[i, 2], ln_b[i, 2])
        if ctx_out:
            ctx = half_step_ffn(ctx, mc[6], mc[7], mc[8], ffn_w_in[i, 1], ffn_w_out[i, 1], ln_g[i, 2], ln_b[i, 2])
    return x


N_META = 16
CHUNK = 128
PAD = CHUNK
ROPE_THETA = 10000.0
EPS = 1e-6
LB_FLOOR = 1e-30
RET_HEADS = 4
RET_DK = 128
RET_DV = 256
HG_HEADS = 8
HG_DK = 128
HG_DV = 128
DA_HEADS = 8
DA_DH = 64
DA_DV = 2 * DA_DH
N_BRANCH = 3
BRANCH_WIDTH = 1024
Q_BLOCK = 128
MASK_VALUE = -1e30
RET_QK_W = RET_HEADS * RET_DK
RET_V_W = RET_HEADS * RET_DV
HG_K_W = HG_HEADS * HG_DK
HG_V_W = HG_HEADS * HG_DV
DA_QK_W = DA_HEADS * 2 * DA_DH
DA_V_W = DA_HEADS * DA_DV
IN_SPLITS = (RET_QK_W, RET_QK_W, RET_V_W, RET_V_W, HG_K_W, HG_K_W, HG_V_W, HG_V_W, DA_QK_W, DA_QK_W, DA_V_W, N_BRANCH * D_MODEL)
IN_WIDTH = sum(IN_SPLITS)
F32 = jnp.float32


def _rms(x):
    xf = x.astype(F32)
    return xf * lax.rsqrt(jnp.mean(xf * xf, axis=-1, keepdims=True) + EPS)

def rms_norm(x, g):
    return (_rms(x) * g.astype(F32)).astype(x.dtype)

def rope(x, pos):
    d = x.shape[-1]
    inv = ROPE_THETA ** (-jnp.arange(0, d, 2, dtype=F32) / d)
    ang = pos.astype(F32)[:, None] * inv[None, :]
    cos = jnp.cos(ang)[None, :, None, :]
    sin = jnp.sin(ang)[None, :, None, :]
    x1, x2 = jnp.split(x, 2, axis=-1)
    return jnp.concatenate([x1 * cos - x2 * sin, x2 * cos + x1 * sin], axis=-1)

def to_chunks(x):
    b, l = x.shape[:2]
    return jnp.swapaxes(x.reshape((b, l // CHUNK, CHUNK) + x.shape[2:]), 0, 1)

def from_chunks(x):
    n, b = x.shape[:2]
    return jnp.swapaxes(x, 0, 1).reshape((b, n * CHUNK) + x.shape[3:])

def retention(q, k, v, gate, valid, pos):
    b = q.shape[0]
    q = rope(q, pos)
    k = jnp.where(valid[None, :, None, None], rope(k, pos) * RET_DK ** -0.5, 0.0)
    log_g = jnp.log1p(-jnp.exp2(-5.0 - jnp.arange(RET_HEADS, dtype=F32)))
    idx = jnp.arange(CHUNK, dtype=F32)
    gap = idx[:, None] - idx[None, :]
    intra = jnp.where(gap >= 0, jnp.exp(log_g[:, None, None] * jnp.maximum(gap, 0.0)), 0.0)
    q_dec = jnp.exp(log_g[:, None] * (idx[None, :] + 1.0))
    k_dec = jnp.exp(log_g[:, None] * (CHUNK - 1.0 - idx[None, :]))
    c_dec = jnp.exp(log_g * CHUNK)[None, :, None, None]

    def step(state, xs):
        qc, kc, vc = xs
        s = jnp.einsum('bqhd,bkhd->bhqk', qc, kc) * intra[None]
        o = jnp.einsum('bhqk,bkhe->bqhe', s, vc) + jnp.einsum('bqhd,hq,bhde->bqhe', qc, q_dec, state)
        state = c_dec * state + jnp.einsum('bkhd,hk,bkhe->bhde', kc, k_dec, vc)
        return state, o

    s0 = jnp.zeros((b, RET_HEADS, RET_DK, RET_DV), F32)
    _, o = lax.scan(step, s0, (to_chunks(q), to_chunks(k), to_chunks(v)))
    o = _rms(from_chunks(o)) * jax.nn.silu(gate)
    return o.reshape(b, -1, RET_V_W)

def hgrn2(q, f_logit, inp, gate, lb, valid):
    b = q.shape[0]
    lbh = lb.reshape(HG_HEADS, HG_DK)
    log_f = jnp.logaddexp(jnp.log(jnp.maximum(lbh, LB_FLOOR)), jnp.log1p(-lbh) + jax.nn.log_sigmoid(f_logit))
    k = (1.0 - lbh) * jax.nn.sigmoid(-f_logit)
    v = jnp.where(valid[None, :, None, None], inp, 0.0)
    causal = jnp.tril(jnp.ones((CHUNK, CHUNK), bool))[None, :, :, None, None]

    def step(state, xs):
        qc, kc, vc, lfc = xs
        cb = jnp.cumsum(lfc, axis=1)
        rel = cb[:, :, None] - cb[:, None, :]
        dec = jnp.where(causal, jnp.exp(jnp.where(causal, rel, 0.0)), 0.0)
        a = jnp.einsum('bqhd,bkhd,bqkhd->bhqk', qc, kc, dec)
        o = jnp.einsum('bhqk,bkhe->bqhe', a, vc) + jnp.einsum('bqhd,bhde->bqhe', qc * jnp.exp(cb), state)
        c_end = cb[:, -1]
        state = jnp.exp(c_end)[..., None] * state + jnp.einsum('bkhd,bkhe->bhde', kc * jnp.exp(c_end[:, None] - cb), vc)
        return state, o

    s0 = jnp.zeros((b, HG_HEADS, HG_DK, HG_DV), F32)
    _, o = lax.scan(step, s0, (to_chunks(q), to_chunks(k), to_chunks(v), to_chunks(log_f)))
    o = _rms(from_chunks(o)) * jax.nn.silu(gate)
    return o.reshape(b, -1, HG_V_W)

def diff_attention(q, k, v, lam_p, subln_g, lambda_init, valid, pos):
    b, l = q.shape[:2]
    lp = lam_p.astype(F32)
    lam = jnp.exp(jnp.sum(lp[0] * lp[1])) - jnp.exp(jnp.sum(lp[2] * lp[3])) + lambda_init
    q = rope(q.reshape(b, l, 2 * DA_HEADS, DA_DH), pos).reshape(b, l, DA_HEADS, 2, DA_DH) * DA_DH ** -0.5
    k = rope(k.reshape(b, l, 2 * DA_HEADS, DA_DH), pos).reshape(b, l, DA_HEADS, 2, DA_DH)
    n_blk = l // Q_BLOCK
    q_blocks = jnp.swapaxes(q.reshape(b, n_blk, Q_BLOCK, DA_HEADS, 2, DA_DH), 0, 1)
    key_pos = jnp.arange(l)

    def block(args):
        qb, bi = args
        s = jnp.einsum('bqhmd,bkhmd->bhmqk', qb, k)
        q_pos = bi * Q_BLOCK + jnp.arange(Q_BLOCK)
        allowed = (key_pos[None, :] <= q_pos[:, None]) & valid[None, :]
        p = jax.nn.softmax(jnp.where(allowed, s, MASK_VALUE), axis=-1)
        w = p[:, :, 0] - lam * p[:, :, 1]
        return jnp.einsum('bhqk,bkhe->bqhe', w, v)

    o = lax.map(block, (q_blocks, jnp.arange(n_blk)))
    o = jnp.swapaxes(o, 0, 1).reshape(b, l, DA_HEADS, DA_DV)
    o = _rms(o) * subln_g.astype(F32) * (1.0 - lambda_init)
    return o.reshape(b, l, DA_V_W)

def mixer(hn, w_in, w_branch, w_out, lb, lam_p, subln_g, lambda_init, valid, pos):
    b, l, _ = hn.shape
    proj = (hn @ w_in).astype(F32)
    offs = [int(o) for o in np.cumsum(IN_SPLITS)[:-1]]
    rq, rk, rv, rg, hq, hf, hi, hg, dq, dk, dv, mg = jnp.split(proj, offs, axis=-1)
    o_ret = retention(rq.reshape(b, l, RET_HEADS, RET_DK), rk.reshape(b, l, RET_HEADS, RET_DK),
                      rv.reshape(b, l, RET_HEADS, RET_DV), rg.reshape(b, l, RET_HEADS, RET_DV), valid, pos)
    o_hg = hgrn2(hq.reshape(b, l, HG_HEADS, HG_DK), hf.reshape(b, l, HG_HEADS, HG_DK),
                 hi.reshape(b, l, HG_HEADS, HG_DV), hg.reshape(b, l, HG_HEADS, HG_DV), lb, valid)
    o_da = diff_attention(dq.reshape(b, l, DA_HEADS, 2, DA_DH), dk.reshape(b, l, DA_HEADS, 2, DA_DH),
                          dv.reshape(b, l, DA_HEADS, DA_DV), lam_p, subln_g, lambda_init, valid, pos)
    branches = jnp.stack([o_ret, o_hg, o_da], axis=2)
    y_b = jnp.einsum('blnc,ncd->blnd', branches, w_branch.astype(F32))
    gates = jax.nn.sigmoid(mg.reshape(b, l, N_BRANCH, D_MODEL))
    y = jnp.sum(gates * y_b, axis=2)
    return y.astype(hn.dtype) @ w_out

def conv_ffn(hn, w_ffn_in, conv_w, conv_b, w_ffn_out, valid):
    l = hn.shape[1]
    u = jnp.where(valid[None, :, None], hn @ w_ffn_in, 0.0)
    up = jnp.pad(u, ((0, 0), (CONV_W - 1, 0), (0, 0)))
    c = conv_b + sum(conv_w[j] * up[:, j:j + l] for j in range(CONV_W))
    gate, val = jnp.split(c, 2, axis=-1)
    return (jax.nn.silu(gate) * val) @ w_ffn_out

def second_inputs(seed: int = 0) -> dict:
    key = jax.random.key(seed)
    ks = jax.random.split(key, 16)

    def nrm(k, shape, scale):
        return jax.random.normal(k, shape, F32) * scale

    return {
        'x': nrm(ks[0], (BATCH, SEQ, D_MODEL), 1.0),
        'meta': nrm(ks[1], (N_META, D_MODEL), 1.0),
        'norm_mix_g': 1.0 + nrm(ks[2], (DEPTH, D_MODEL), 0.02),
        'w_in': nrm(ks[3], (DEPTH, D_MODEL, IN_WIDTH), D_MODEL ** -0.5),
        'w_branch': nrm(ks[4], (DEPTH, N_BRANCH, BRANCH_WIDTH, D_MODEL), BRANCH_WIDTH ** -0.5),
        'w_out': nrm(ks[5], (DEPTH, D_MODEL, D_MODEL), D_MODEL ** -0.5),
        'hg_lb': nrm(ks[6], (DEPTH, HG_K_W), 0.1),
        'da_lambda': nrm(ks[7], (DEPTH, 4, DA_DH), 0.1),
        'da_subln_g': 1.0 + nrm(ks[8], (DEPTH, DA_DV), 0.02),
        'norm_ffn_g': 1.0 + nrm(ks[9], (DEPTH, D_MODEL), 0.02),
        'w_ffn_in': nrm(ks[10], (DEPTH, D_MODEL, 2 * D_FF), D_MODEL ** -0.5),
        'ffn_conv_w': nrm(ks[11], (DEPTH, CONV_W, 2 * D_FF), CONV_W ** -0.5),
        'ffn_conv_b': nrm(ks[12], (DEPTH, 2 * D_FF), 0.01),
        'w_ffn_out': nrm(ks[13], (DEPTH, D_FF, D_MODEL), D_FF ** -0.5),
        'norm_final_g': 1.0 + nrm(ks[14], (D_MODEL,), 0.02),
    }

def second_block(x, meta, norm_mix_g, w_in, w_branch, w_out, hg_lb, da_lambda, da_subln_g,
              norm_ffn_g, w_ffn_in, ffn_conv_w, ffn_conv_b, w_ffn_out, norm_final_g):
    b, s, d = x.shape
    l = PAD + s
    h = jnp.concatenate([jnp.zeros((b, PAD - N_META, d), x.dtype),
                         jnp.broadcast_to(meta[None].astype(x.dtype), (b, N_META, d)), x], axis=1)
    t = jnp.arange(l)
    valid = t >= PAD - N_META
    pos = t - (PAD - N_META)
    lb_soft = jax.nn.softmax(hg_lb.astype(F32), axis=0)
    lbs = jnp.cumsum(lb_soft, axis=0) - lb_soft[0]
    for li in range(DEPTH):
        lambda_init = 0.8 - 0.6 * math.exp(-0.3 * li)
        h = h + mixer(rms_norm(h, norm_mix_g[li]), w_in[li], w_branch[li], w_out[li], lbs[li],
                      da_lambda[li], da_subln_g[li], lambda_init, valid, pos)
        h = h + conv_ffn(rms_norm(h, norm_ffn_g[li]), w_ffn_in[li], ffn_conv_w[li], ffn_conv_b[li],
                         w_ffn_out[li], valid)
    h = rms_norm(h, norm_final_g)
    return h[:, PAD:]


def setup_inputs(seed=0):
    out = dict(first_inputs(seed))
    for name, value in second_inputs(seed + 1).items():
        if name != "x":
            out[name + "_2"] = value
    return out


def reference(
    x, c, ctx, c_ctx, ada_w, ada_b, ln_g, ln_b, ffn_w_in, ffn_w_out, na_w_qkv, na_w_out, na_rpb,
    sc_w_in, sc_conv, sc_w_out, meta_2, norm_mix_g_2, w_in_2, w_branch_2, w_out_2, hg_lb_2,
    da_lambda_2, da_subln_g_2, norm_ffn_g_2, w_ffn_in_2, ffn_conv_w_2, ffn_conv_b_2,
    w_ffn_out_2, norm_final_g_2,
):
    x = first_block(
        x, c, ctx, c_ctx, ada_w, ada_b, ln_g, ln_b, ffn_w_in, ffn_w_out, na_w_qkv, na_w_out,
        na_rpb, sc_w_in, sc_conv, sc_w_out,
    )
    return second_block(
        x, meta_2, norm_mix_g_2, w_in_2, w_branch_2, w_out_2, hg_lb_2, da_lambda_2,
        da_subln_g_2, norm_ffn_g_2, w_ffn_in_2, ffn_conv_w_2, ffn_conv_b_2, w_ffn_out_2,
        norm_final_g_2,
    )


_drawn_inputs = setup_inputs


def setup_inputs(seed=0):
    import zlib

    import numpy as np

    out = dict(_drawn_inputs(seed))
    spreads = {}
    factors = {'na_rpb': 26.951,
     'hg_lb_2': 13.119,
     'da_subln_g_2': 4.827,
     'norm_ffn_g_2': 2.842,
     'ffn_conv_b_2': 5.51,
     'norm_final_g_2': 8.114}
    for name, (base, spread) in spreads.items():
        noise = np.random.default_rng([zlib.crc32(name.encode()), seed]).standard_normal(out[name].shape)
        drawn = base * np.exp(spread * noise) if base else spread * noise
        out[name] = jnp.asarray(drawn.astype(out[name].dtype))
    for name, factor in factors.items():
        out[name] = (out[name] * factor).astype(out[name].dtype)
    return out
```

```python
from contextlib import ExitStack
import math

import numpy as np

import concourse.bass as bass
from concourse import mybir

F32 = mybir.dt.float32
F32R = mybir.dt.float32r
I32 = mybir.dt.int32
ALU = mybir.AluOpType
ACT = mybir.ActivationFunctionType
AX = mybir.AxisListType

P = 128
D = 1024
KT = D // P
F = 2816
FT = F // P
SEQ = 256
CTX = 256
N_META = 16
T1 = SEQ + CTX
T2 = N_META + SEQ
DEPTH = 2
PW = 512
NH, HD = 16, 64
GRID_W, GRID_H = 64, SEQ // 64
RH = 4
HH = 8
DH = 8
ALPHA = (2.0 * DEPTH) ** 0.25
EPS = 1e-6
IN_W = 13312
CHUNKS = ((0, 128), (128, 128), (256, 16))
LEVELS = (1, 2, 4, 8, 16, 32, 64)
NEG = -1e30

COLS = {}
_at = 0
for _name, _n in (("c", 2 * KT), ("ada_b", DEPTH * 9 * KT), ("ln_g", DEPTH * 3 * KT), ("ln_b", DEPTH * 3 * KT),
                  ("mix_g", DEPTH * KT), ("ffn_g", DEPTH * KT), ("final_g", KT), ("sc_w", 3 * KT),
                  ("conv_w", DEPTH * 3 * 2 * FT), ("conv_b", DEPTH * 2 * FT), ("hg_lb", DEPTH * KT),
                  ("subln", DEPTH), ("lam", DEPTH * 4)):
    COLS[_name] = _at
    _at += _n
NCOL = _at

C1 = {"ident": 0, "pair": 128, "rot": 132, "cos": 260, "sin": 516, "colmask": 772}
NC1 = 836
C2 = {"rot_r": 0, "rot_d": 128, "cos_r": 256, "sin_r": 528, "cos_d": 800, "sin_d": 1072,
      "gap": 1344, "dmask": 2160, "reset": 2976, "levels": 3248}
NC2 = 3248 + 8 * 128


def rotation(half, width):
    r = np.zeros((P, P), np.float32)
    for base in range(0, P, width):
        for d in range(half):
            r[base + half + d, base + d] = -1.0
            r[base + d, base + half + d] = 1.0
    return r


def first_constants():
    out = np.zeros((P, NC1), np.float32)
    out[:, 0:128] = np.eye(P)
    out[0:2, 128] = 1.0
    out[2:4, 129] = 1.0
    out[:, C1["rot"]:C1["rot"] + P] = rotation(HD // 4, HD // 2)
    t = np.arange(SEQ)
    inv = 10000.0 ** (-np.arange(HD // 4) / (HD // 4))
    for p in range(P):
        d = p % HD
        pos = (t // GRID_W) if d < HD // 2 else (t % GRID_W)
        ang = pos * inv[d % (HD // 4)]
        out[p, C1["cos"]:C1["cos"] + SEQ] = np.cos(ang)
        out[p, C1["sin"]:C1["sin"] + SEQ] = np.sin(ang)
    for p in range(P):
        start = min(max(p % GRID_W - 8, 0), GRID_W - 16)
        row = np.full(GRID_W, NEG, np.float32)
        row[start:start + 16] = 0.0
        out[p, C1["colmask"]:] = row
    return out


def second_constants():
    out = np.zeros((P, NC2), np.float32)
    out[:, 0:P] = rotation(64, 128)
    out[:, P:2 * P] = rotation(32, 64)
    pos = np.arange(T2, dtype=np.float32)
    for key, dim in (("_r", 128), ("_d", 64)):
        inv = (np.float32(10000.0) ** (-np.arange(0, dim, 2, dtype=np.float32) / np.float32(dim))).astype(np.float32)
        ang = inv[np.arange(P) % (dim // 2)][:, None] * pos[None, :]
        out[:, C2["cos" + key]:C2["cos" + key] + T2] = np.cos(ang)
        out[:, C2["sin" + key]:C2["sin" + key] + T2] = np.sin(ang)
    for n, (t0, w) in enumerate(CHUNKS):
        k = t0 + np.arange(w)
        gap = pos[None, :] - k[:, None]
        out[:w, C2["gap"] + n * T2:C2["gap"] + (n + 1) * T2] = np.where(gap >= 0, gap, 1e6)
        out[:w, C2["dmask"] + n * T2:C2["dmask"] + (n + 1) * T2] = np.where(-gap >= 0, 0.0, NEG)
    reset = np.ones(T2, np.float32)
    reset[[t0 for t0, _ in CHUNKS]] = 0.0
    out[:, C2["reset"]:C2["reset"] + T2] = reset
    i = np.arange(P)
    masks = [i[:, None] == i[None, :]]
    for s in LEVELS:
        same = (i[:, None] // (2 * s)) == (i[None, :] // (2 * s))
        masks.append(same & (i[:, None] % (2 * s) < s) & (i[None, :] % (2 * s) >= s))
    for n, m in enumerate(masks):
        out[:, C2["levels"] + n * P:C2["levels"] + (n + 1) * P] = m
    return out


def gemm_steps(w):
    steps = []

    def add(name, groups, src, layer=0, t0=0, T=SEQ, panels=((0, 8),), halves=False, unroll=False):
        steps.append(dict(name=name, groups=groups, src=src, layer=layer, t0=t0, T=T, panels=panels,
                          halves=halves, unroll=unroll))

    def plain(ap, col0=0):
        v = ap.rearrange("(k p) n -> p k n", p=P)

        def src(i, k0, nk):
            if nk == 2:
                return [v[:, k0 + x, bass.ds(col0 + PW * i, PW)] for x in range(2)]
            return [v[:, k0, bass.ds(col0 + PW * i + x * PW // 2, PW // 2)] for x in range(2)]
        return src

    def paired(ap, first, second):
        v = ap.rearrange("(k p) n -> p k n", p=P)

        def src(i, k0, nk):
            return [v[:, k0:k0 + nk, bass.ds(at + 256 * i, 256)] for at in (first, second)]
        return src

    deep = ((0, 7), (7, 7), (14, 8))
    for layer in range(DEPTH):
        add("ada", 9 * D // PW, plain(w["ada_w"][layer]), layer)
    for layer in range(DEPTH):
        for r in range(3):
            T = T1 if (layer, r) == (0, 0) else SEQ
            if r != 1:
                half = 0 if r == 0 else 1
                add("glu", FT // 2, paired(w["ffn_w_in"][layer, half], 0, F), layer, T=T, halves=True)
                add("res", 2, plain(w["ffn_w_out"][layer, half]), layer, T=T, panels=deep)
                steps[-1]["r"] = r
            elif layer == 0:
                add("q", 2, plain(w["na_w_qkv"][0], 0), layer)
                add("k", 2, plain(w["na_w_qkv"][0], D), layer, T=T1)
                add("v", 2, plain(w["na_w_qkv"][0], 2 * D), layer, T=T1)
                add("res", 2, plain(w["na_w_out"][0]), layer)
                steps[-1]["r"] = r
            else:
                add("cgate", 4, paired(w["sc_w_in"][0], D, 2 * D), layer, halves=True)
                add("bgate", 2, plain(w["sc_w_in"][0], 0), layer)
                add("res", 2, plain(w["sc_w_out"][0]), layer)
                steps[-1]["r"] = r
            steps[-1]["norm"] = True
    for layer in range(DEPTH):
        w_in = w["w_in_2"][layer]
        for n, kinds in enumerate(((("store", 4, 0, 0), ("gate", 2, 2048, 16)),
                                   (("store", 2, 3072, 0), ("forget", 2, 4096, 8), ("store", 2, 5120, 24),
                                    ("gate", 2, 6144, 32)),
                                   (("store", 6, 7168, 0),))):
            for kind, groups, col, tile in kinds:
                add(kind, groups, plain(w_in, col), layer, T=T2)
                steps[-1]["tile"] = tile
                steps[-1]["after_rms"] = col == 0
            steps[-1]["mixer"] = n
            add("mgate", 2, plain(w_in, 10240 + n * D), layer, T=T2)
            add("branch", 2, plain(w["w_branch_2"][layer, n]), layer, T=T2)
            steps[-1]["n"] = n
        add("add", 2, plain(w["w_out_2"][layer]), layer, T=T2)
        steps[-1]["rms"] = ("ffn_g", layer)
        add("conv", FT // 2, paired(w["w_ffn_in_2"][layer], 0, F), layer, T=T2, halves=True)
        steps[-1]["after_rms"] = True
        add("add", 2, plain(w["w_ffn_out_2"][layer]), layer, T=T2, panels=deep, unroll=(layer == DEPTH - 1))
        steps[-1]["rms"] = ("mix_g", layer + 1) if layer + 1 < DEPTH else ("final_g", 0)
    g = G = 0
    for s in steps:
        s["g0"], s["G0"] = g, G
        g += s["groups"] * len(s["panels"])
        G += s["groups"]
    steps[-1]["last"] = True
    return steps


RPB_W = 128


def two_block_kernel(nc, w, tokens, meta, cols_d, const1_d, const2_d, rpb_d, rpb_skew, out_d):
    steps = gemm_steps(w)
    ctx = ExitStack()
    with ctx:
        def sem(name):
            return ctx.enter_context(nc.semaphore(name))

        base = 16512
        arena = nc.sbuf_usable_end - 64

        class Region:
            def __init__(self, at):
                self.at = at

            def take(self, name, shape, dt=F32):
                off = (self.at + 31) // 32 * 32
                size = 4 * int(np.prod(shape[1:]))
                self.at = off + size
                assert self.at <= arena, (name, self.at, arena)
                return nc.alloc_sbuf_tensor_at(name, shape, dt, offset=off)

        R = Region(base)
        raw = R.take("raw", [P, 4, 2, PW])
        high = R.take("high", [P, 4, 2, PW], F32R)
        low = R.take("low", [P, 4, 2, PW], F32R)
        X = R.take("X", [P, KT, T1])
        cols = R.take("cols", [P, NCOL])
        con1 = R.take("con1", [P, NC1])
        ones = R.take("ones", [P, P])
        mod = R.take("mod", [P, DEPTH, 2, 9 * KT])
        small = R.take("small", [P, 40 * KT])
        RS = R.take("RS", [P, 2, T1])
        epsc = R.take("epsc", [P, 2])
        dst = R.take("dst", [P, 4, 4])
        common_end = R.at

        A = Region(common_end)
        XH = A.take("XH", [P, KT, T1], F32R)
        XL = A.take("XL", [P, KT, T1], F32R)
        inner = A.at
        GH = A.take("GH", [P, FT, T1], F32R)
        GL = A.take("GL", [P, FT, T1], F32R)
        A2 = Region(inner)
        TC = A2.take("TC", [P, KT, T1])
        TQ = A2.take("TQ", [P, KT, T1])
        E1 = Region(A.at)
        SG = E1.take("SG", [P, 2, T1])
        GB = E1.take("GB", [P, 2, T1])
        e1_end = E1.at
        A3 = Region(inner)
        SC4 = A3.take("SC4", [P, KT, P], F32R)
        adarow = A3.take("adarow", [P, PW])
        scf = A3.take("scf", [P, 4 * 2 * KT])
        A4 = Region(inner)
        NQ = A4.take("NQ", [P, KT, SEQ])
        NK = A4.take("NK", [P, KT, T1])
        NV = A4.take("NV", [P, 4, D])
        NVT = A4.take("NVT", [P, KT, T1])
        TB = A4.take("TB", [P, NH, 6, GRID_W])
        NT = Region(A4.at - 4 * NH * 6 * GRID_W - 4 * KT * T1)
        SB = NT.take("SB", [P, 4, T1])
        PT = NT.take("PT", [P, 2, T1])
        ROT = A4.take("ROT", [P, 2, SEQ])
        nst = A4.take("nst", [P, 4, 4])
        A5 = Region(inner + 2 * 4 * FT * T1 // 2)
        UP = A5.take("UP", [P, KT, SEQ + 2])
        CV = A5.take("CV", [P, KT, SEQ])
        A5.at = max(A5.at, e1_end)

        con2 = Region(arena // 32 * 32 - 4 * NC2 - 32).take("con2", [P, NC2])
        B = Region(common_end)
        H = B.take("H", [P, KT, T2])
        NHh = B.take("NHh", [P, KT, T2], F32R)
        NHl = B.take("NHl", [P, KT, T2], F32R)
        b_inner = B.at
        Y = B.take("Y", [P, KT, T2])
        oh_at = B.at
        OH = B.take("OH", [P, KT, T2], F32R)
        ol_at = B.at
        OL = B.take("OL", [P, KT, T2], F32R)
        VT = B.take("VT", [P, 3, D])
        SX = B.take("SX", [P, 2, 2, T2])
        SY = B.take("SY", [P, 2, 2, T2])
        MI = B.take("MI", [P, 24, T2])
        MJ = B.take("MJ", [P, 8, T2])
        MG = B.take("MG", [P, 8, T2])
        assert B.at <= arena - 4 * NC2 - 96
        QB = Region(oh_at).take("QB", [P, KT, T2])
        AM = Region(ol_at).take("AM", [P, KT, T2])
        B2 = Region(b_inner)
        G2H = B2.take("G2H", [P, FT, T2], F32R)
        G2L = B2.take("G2L", [P, FT, T2], F32R)
        CB = B2.take("CB", [P, 4, T2])
        SG2 = B2.take("SG2", [P, 4, T2])
        assert B2.at <= arena - 4 * NC2 - 96
        TN = Region(b_inner).take("TN", [P, KT, T2])

        PS = ctx.enter_context(nc.psum_tensor("PS", [P, 8, PW], F32))

        s_tokens = sem("tokens_loaded")
        s_out = sem("output_written")
        s_skew_out = sem("bias_skew_written")
        s_bias = sem("bias_loaded")
        s_ones = sem("ones_set")
        s_raw = [sem(f"raw_quarter{q}_loaded") for q in range(4)]
        s_high = sem("high_quarters")
        s_low = sem("low_quarters")
        s_half = sem("panel_halves_multiplied")
        s_pair0 = sem("first_pair_multiplied")
        s_free = sem("pairs_evacuated")
        s_act = sem("act_epilogue")
        s_mid = sem("dve_epilogue_steps")
        s_gb = sem("conv_hidden_ready")
        s_hh = sem("hidden_high")
        s_hl = sem("hidden_low")
        s_adarow = sem("ada_row_ready")
        s_silu = sem("silu_c_steps")
        s_sc4 = sem("silu_c_ready")
        s_comp = sem("columns_ready")
        s_sum = sem("row_sums")
        s_cen = sem("centred_halves")
        s_sq = sem("squared_halves")
        s_var = sem("square_sums")
        s_ln = sem("log_taken")
        s_rdev = sem("rdev_ready")
        s_modd = sem("modulated_tiles")
        s_xh = sem("x_high_pairs")
        s_xl = sem("x_low_halves")
        s_res = sem("residual_ready")
        s_chain = sem("dve_chain")
        s_pchain = sem("pool_chain")

        ACTS = {"glu": 2, "cgate": 2, "gate": 2, "forget": 4, "mgate": 2, "conv": 6}
        MIDS = {"glu": 2, "cgate": 6, "conv": 8}
        HIDS = {"glu": 2, "bgate": 2, "conv": 2}
        act = mid = hid = gb = yad = 0
        for s in steps:
            s["act0"], s["mid0"], s["hid0"], s["gb0"], s["yad0"] = act, mid, hid, gb, yad
            act += ACTS.get(s["name"], 0) * s["groups"]
            mid += MIDS.get(s["name"], 0) * s["groups"]
            hid += HIDS.get(s["name"], 0) * s["groups"]
            gb += (2 if s["name"] == "conv" else 0) * s["groups"]
            yad += 2 * s["groups"] if s["name"] == "branch" and s["n"] else 0

        COLOF = {False: (0, 128, 256, 384), True: (0, 256, 128, 384)}

        def groups_of(eng, s):
            if s["unroll"] or s["groups"] == 2:
                yield from range(s["groups"])
            else:
                with eng.Fori(0, s["groups"]) as i:
                    yield i

        def groups_behind(eng, s, body, epilogue):
            body(0)
            if s["unroll"] or s["groups"] == 2:
                for i in range(1, s["groups"]):
                    body(i)
                    epilogue(i - 1)
            else:
                with eng.Fori(1, s["groups"]) as i:
                    body(i)
                    epilogue(i - 1)
            epilogue(s["groups"] - 1)

        def is_last(s, i, pi):
            return bool(s.get("last")) and s["unroll"] and i == s["groups"] - 1 and pi == len(s["panels"]) - 1

        def col(name, n=0, w=1):
            return cols[:, bass.ds(COLS[name] + n, w)]

        def flat(ap):
            return ap.rearrange("p a t -> p (a t)")

        def bc(ap, n):
            return bass.AP(ap.tensor, ap.offset, [ap.ap[0], [0, n], *ap.ap[1:]])

        def sm(name, c=0):
            names = ("ag", "ag_", "gate", "gate_", "xg", "xb", "ab", "ab_", "lbm0", "lbm1", "olb0", "olb1",
                     "sub", "lam", "t0", "t1", "t2", "t3")
            at = names.index(name + "_" * c) * KT
            return small[:, at:at + KT]

        def smcol(name, n, c=0, w=1):
            names = ("ag", "ag_", "gate", "gate_", "xg", "xb", "ab", "ab_", "lbm0", "lbm1", "olb0", "olb1",
                     "sub", "lam", "t0", "t1", "t2", "t3")
            return small[:, bass.ds(names.index(name + "_" * c) * KT + n, w)]

        def bank(G, j, n=1):
            return PS[:, bass.ds((G % 2) * 4 + j, n), :]

        def ones_sum(dst, src, n):
            for k in range(n):
                last = nc.tensor.matmul(dst, ones[:], src[:, k, :], start=(k == 0), stop=(k == n - 1))
            return last

        def gate_room(s, n):
            return MI[:, bass.ds(16 + n, 2), :] if s["name"] == "gate" and s["tile"] == 16 else MG[:, bass.ds(n, 2), :]

        s_nvt = sem("na_values_transposed")
        s_nvc = sem("na_values_copied")
        s_nrot = sem("na_rotated")
        s_nr1 = sem("na_sin_part")
        s_nr2 = sem("na_roped")
        s_ns = sem("na_scores")
        s_na = sem("na_biased")
        s_nm = sem("na_max")
        s_ne = sem("na_exp")
        s_nr = sem("na_sum_inverse")
        s_nw = sem("na_probs")
        s_nt = sem("na_probs_transposed")
        s_nc = sem("na_probs_copied")
        s_no = sem("na_heads_out")
        s_no_high = sem("na_out_high")
        s_no_low = sem("na_out_low")
        s_vt = sem("values_transposed")
        s_vc = sem("values_copied")
        s_rot = sem("rotated")
        s_rope1 = sem("sin_part")
        s_rope2 = sem("roped")
        s_dec = sem("decay_ready")
        s_rs = sem("ret_scores")
        s_rd = sem("ret_scores_decayed")
        s_lamp = sem("lambda_products")
        s_lams = sem("lambda_sums")
        s_lame = sem("lambda_exps")
        s_ds = sem("da_scores")
        s_dm = sem("da_masked")
        s_dx = sem("da_max")
        s_de = sem("da_exp")
        s_dw = sem("da_weights")
        s_dt = sem("da_weights_transposed")
        s_dp = sem("da_values_summed")
        s_dc = sem("da_weights_copied")
        s_hd = sem("hg_dve")
        s_ha = sem("hg_act")
        s_hp = sem("hg_pool")
        s_ht = sem("hg_pe")
        s_o = sem("head_out")
        s_osq = sem("head_squared")
        s_oms = sem("head_square_sum")
        s_oln = sem("head_log")
        s_ord = sem("head_rdev")
        s_ot = sem("head_gated")
        s_oth = sem("head_high")
        s_tail_low = sem("head_low")
        s_yadd = sem("y_added")
        s_yh = sem("y_high")
        s_yl = sem("y_low")
        s_rsq = sem("rms_squares")
        s_rsum = sem("rms_sums")
        s_rln = sem("rms_log")
        s_rrd = sem("rms_rdev")
        s_modd_final = sem("rms_scaled_final")
        s_rmod = sem("rms_scaled")
        s_rxh = sem("rms_high_pairs")
        s_rxl = sem("rms_low_halves")
        s_meta = sem("meta_loaded")

        ident = con1[:, 0:P]

        def tail_first(layer, n):
            return layer * 20 + (0, 4, 12)[n]

        def tail_count(layer, n):
            return layer * 20 + (4, 12, 20)[n]

        def cc(name, w=T2, at=0):
            return con2[:, C2[name] + at:C2[name] + at + w]

        def out_bank(n, h):
            return 2 + 2 * (h % 2) if n == 0 else 5 + h % 2

        def tail_act_square(act, n, hh, h):
            ne = 2 if n == 0 else 1
            act.wait_ge(s_o, hh + 1)
            if hh >= 2:
                act.wait_ge(s_oms, hh - 1)
            b = out_bank(n, h)
            nc.scalar.activation(SX[:, hh % 2, 0:ne, :], PS[:, b:b + ne, 0:T2], ACT.Square).then_inc(s_osq, 1)

        def tail_pe(pe, n, hh, h):
            ne = 2 if n == 0 else 1
            pe.wait_ge(s_osq, hh + 1)
            if hh >= 1:
                pe.wait_ge(s_oln, hh)
            ones_sum(PS[:, 7, 0:T2], SX[:, hh % 2], ne).then_inc(s_oms, 1)

        def tail_act_rdev(act, n, hh, h):
            act.wait_ge(s_oms, hh + 1)
            if hh >= 2:
                act.wait_ge(s_ot, hh - 1)
            rs = RS[:, hh % 2, 0:T2]
            nc.scalar.activation(rs, PS[:, 7, 0:T2], ACT.Ln, bias=epsc[:, 0:1],
                                 scale=1.0 / (256 if n == 0 else 128)).then_inc(s_oln, 1)
            act.wait_ge(s_oln, hh + 1)
            nc.scalar.activation(rs, rs, ACT.Exp, scale=-0.5).then_inc(s_ord, 1)

        def tail_act_high(act, n, hh, h):
            ne = 2 if n == 0 else 1
            act.wait_ge(s_ot, hh + 1)
            nc.scalar.copy(OH[:, h * ne:(h + 1) * ne, :], SY[:, hh % 2, 0:ne, :]).then_inc(s_oth, 1)

        def tail_dve(dve, link, n, hh, h):
            tail_dve_gate(dve, link, n, hh, h)
            tail_dve_low(dve, n, hh, h)

        def tail_dve_gate(dve, link, n, hh, h):
            ne = 2 if n == 0 else 1
            b = out_bank(n, h)
            dve.wait_ge(s_ord, hh + 1)
            rs, sy = RS[:, hh % 2, 0:T2], SY[:, hh % 2, 0:ne, :]
            if n == 2:
                nc.vector.scalar_tensor_tensor(sy[:, 0, :], PS[:, b, 0:T2], sm("sub")[:, 0:1], rs,
                                               ALU.mult, ALU.mult).then_inc(s_ot, 1)
            else:
                link(nc.vector.tensor_tensor(sy, PS[:, b:b + ne, 0:T2], bc(rs, ne), ALU.mult))
                gate = MI[:, 16 + 2 * h:18 + 2 * h, :] if n == 0 else MG[:, h:h + 1, :]
                nc.vector.tensor_tensor(sy, sy, gate, ALU.mult).then_inc(s_ot, 1)

        def tail_dve_low(dve, n, hh, h):
            ne = 2 if n == 0 else 1
            sy = SY[:, hh % 2, 0:ne, :]
            dve.wait_ge(s_oth, hh + 1)
            t = slice(h * ne, (h + 1) * ne)
            nc.vector.tensor_tensor(OL[:, t, :], sy, OH[:, t, :].bitcast(F32), ALU.subtract).then_inc(s_tail_low, 1)

        def values_pe(pe, src, m):
            for n, (t0, wd) in enumerate(CHUNKS):
                for f in range(KT):
                    last = nc.tensor.transpose(PS[0:wd, 2 * n + f // 4, (f % 4) * P:(f % 4 + 1) * P],
                                               src[:, f, t0:t0 + wd], ident)
                last.then_inc(s_vt, 1)

        def values_act(act, m):
            for n, (t0, wd) in enumerate(CHUNKS):
                act.wait_ge(s_vt, 3 * m + n + 1)
                nc.scalar.copy(VT[0:wd, n, :].rearrange("p (a t) -> p a t", a=2),
                               PS[0:wd, 2 * n:2 * n + 2, :]).then_inc(s_vc, 1)

        def rope_pe(pe, rot, first, n):
            for u in range(n):
                if first + u >= 2:
                    pe.wait_ge(s_rope1, first + u - 1)
                nc.tensor.matmul(PS[:, 6 + u % 2, 0:T2], rot, MI[:, u, :], start=True, stop=True).then_inc(s_rot, 1)

        def rope_dve(dve, cos, sin, first, n):
            for u in range(n):
                dve.wait_ge(s_rot, first + u + 1)
                nc.vector.tensor_tensor(SX[:, u % 2, 0, :], PS[:, 6 + u % 2, 0:T2], sin, ALU.mult).then_inc(s_rope1, 1)
                nc.vector.tensor_tensor(MI[:, u, :], MI[:, u, :], cos, ALU.mult).then_inc(s_rope2, 1)
                dve.wait_ge(s_rope1, first + u + 1)
                dve.wait_ge(s_rope2, 2 * (first + u) + 1)
                nc.vector.tensor_tensor(MI[:, u, :], MI[:, u, :], SX[:, u % 2, 0, :], ALU.add).then_inc(s_rope2, 1)

        def ret_pe(pe, layer, G_end):
            pe.wait_ge(s_free, 2 * G_end + 4)
            u0, hh0 = 3 * RH * layer, tail_first(layer, 0)
            values_pe(pe, MI[:, 8:16, :], 3 * layer)
            rope_pe(pe, cc("rot_r", P), 24 * layer, 8)
            pe.wait_ge(s_rope2, 2 * (24 * layer + 8))
            pe.wait_ge(s_vc, 3 * (3 * layer + 1))

            def scores(h):
                for n, (t0, wd) in enumerate(CHUNKS):
                    u = 3 * h + n
                    if u >= 2:
                        pe.wait_ge(s_rd, u0 + u - 1)
                    nc.tensor.matmul(PS[0:wd, u % 2, 0:T2 - t0], MI[:, 4 + h, t0:t0 + wd], MI[:, h, t0:T2],
                                     start=True, stop=True).then_inc(s_rs, 1)

            scores(0)
            for h in range(RH):
                if h + 1 < RH:
                    scores(h + 1)
                pe.wait_ge(s_rd, u0 + 3 * h + 3)
                if h >= 2:
                    pe.wait_ge(s_ot, hh0 + h - 1)
                for e in range(2):
                    for n, (t0, wd) in enumerate(CHUNKS):
                        last = nc.tensor.matmul(PS[:, out_bank(0, h) + e, t0:T2],
                                                VT[0:wd, n, h * 256 + e * P:h * 256 + (e + 1) * P],
                                                MJ[0:wd, 3 * (h % 2) + n, t0:T2], start=(n == 0), stop=(n == 2))
                last.then_inc(s_o, 1)
                if h:
                    tail_pe(pe, 0, hh0 + h - 1, h - 1)
            tail_pe(pe, 0, hh0 + RH - 1, RH - 1)

        def ret_act(act, layer, G_end):
            hh0 = tail_first(layer, 0)
            values_act(act, 3 * layer)
            for h in range(RH + 1):
                if h < RH:
                    log_g = math.log1p(-2.0 ** (-5.0 - h))
                    if h >= 2:
                        act.wait_ge(s_rd, 3 * RH * layer + 3 * (h - 1))
                    act.wait_ge(s_free, 2 * G_end + 4)
                    nc.scalar.activation(MG[:, 3 * (h % 2):3 * (h % 2) + 3, :],
                                         cc("gap", 3 * T2).rearrange("p (n t) -> p n t", n=3), ACT.Exp,
                                         scale=log_g).then_inc(s_dec, 1)
                if h >= 2:
                    tail_act_rdev(act, 0, hh0 + h - 2, h - 2)
                    tail_act_high(act, 0, hh0 + h - 2, h - 2)
                if h >= 1:
                    tail_act_square(act, 0, hh0 + h - 1, h - 1)
            tail_act_rdev(act, 0, hh0 + RH - 1, RH - 1)
            tail_act_high(act, 0, hh0 + RH - 1, RH - 1)

        def ret_dve(dve, link, layer, G_end):
            u0, hh0 = 3 * RH * layer, tail_first(layer, 0)
            rope_dve(dve, cc("cos_r"), cc("sin_r"), 24 * layer, 8)
            for h in range(RH + 1):
                if h < RH:
                    dve.wait_ge(s_dec, RH * layer + h + 1)
                    if h >= 2:
                        dve.wait_ge(s_o, hh0 + h - 1)
                    for n, (t0, wd) in enumerate(CHUNKS):
                        dve.wait_ge(s_rs, u0 + 3 * h + n + 1)
                        nc.vector.scalar_tensor_tensor(MJ[0:wd, 3 * (h % 2) + n, t0:T2],
                                                       PS[0:wd, (3 * h + n) % 2, 0:T2 - t0], P ** -0.5,
                                                       MG[0:wd, 3 * (h % 2) + n, t0:T2],
                                                       ALU.mult, ALU.mult).then_inc(s_rd, 1)
                if h >= 2:
                    tail_dve(dve, link, 0, hh0 + h - 2, h - 2)
            tail_dve(dve, link, 0, hh0 + RH - 1, RH - 1)

        DU = 3 * DH

        def da_pe(pe, layer, G_end):
            pe.wait_ge(s_free, 2 * G_end + 4)
            u0, hh0 = DU * layer, tail_first(layer, 2)
            pe.wait_ge(s_lamp, layer + 1)
            values_pe(pe, MI[:, 16:24, :], 3 * layer + 2)
            nc.tensor.matmul(PS[:, 6, 0:2], ones[:], sm("t0")[:, 0:2], start=True, stop=True).then_inc(s_lams, 1)
            pe.wait_ge(s_lame, layer + 1)
            rope_pe(pe, cc("rot_d", P), 24 * layer + 8, 16)
            pe.wait_ge(s_rope2, 2 * (24 * layer + 24))
            pe.wait_ge(s_vc, 3 * (3 * layer + 3))
            for t in range(DU + 7):
                if t < DU:
                    h, n = divmod(t, 3)
                    t0, wd = CHUNKS[n]
                    if t >= 2:
                        pe.wait_ge(s_dm, u0 + t - 1)
                    for m in range(2):
                        r = slice(64 * m, 64 * m + 64)
                        last = nc.tensor.matmul(PS[0:wd, 2 * (t % 2) + m, 0:t0 + wd], MI[r, h, t0:t0 + wd],
                                                MI[r, 8 + h, 0:t0 + wd], start=True, stop=True)
                    last.then_inc(s_ds, 1)
                if 6 <= t < DU + 6:
                    u = t - 6
                    h, n = divmod(u, 3)
                    t0, wd = CHUNKS[n]
                    pe.wait_ge(s_dc, u0 + u + 1)
                    if n == 0 and h >= 2:
                        pe.wait_ge(s_ot, hh0 + h - 1)
                    for c in range(n + 1):
                        k0, kw = CHUNKS[c]
                        last = nc.tensor.matmul(PS[:, out_bank(2, h), t0:t0 + wd], VT[0:kw, c, h * P:(h + 1) * P],
                                                flat(MG[0:kw, 2 + 2 * (u % 2):4 + 2 * (u % 2), :])[:, c * P:c * P + wd],
                                                start=(c == 0), stop=(c == n))
                    if n == 2:
                        last.then_inc(s_o, 1)
                    if n != 2:
                        last.then_inc(s_dp, 1)
                if 4 <= t < DU + 4:
                    u = t - 4
                    h, n = divmod(u, 3)
                    t0, wd = CHUNKS[n]
                    pe.wait_ge(s_dw, u0 + u + 1)
                    if u:
                        pe.wait_ge(s_dc, u0 + u)
                    for c in range(n + 1):
                        k0, kw = CHUNKS[c]
                        last = nc.tensor.transpose(PS[0:kw, 4, c * P:c * P + wd], MG[0:wd, u % 2, k0:k0 + kw],
                                                   con1[0:wd, 0:wd])
                    last.then_inc(s_dt, 1)
                if t >= 7 and (t - 7) % 3 == 2:
                    h = (t - 7) // 3
                    tail_pe(pe, 2, hh0 + h, h)

        def da_act(act, layer, G_end):
            u0, hh0 = DU * layer, tail_first(layer, 2)
            values_act(act, 3 * layer + 2)
            act.wait_ge(s_lams, layer + 1)
            nc.scalar.activation(sm("t1")[:, 0:2], PS[:, 6, 0:2], ACT.Exp).then_inc(s_lame, 1)
            for t in range(DU + 9):
                if 5 <= t < DU + 5:
                    u = t - 5
                    h, n = divmod(u, 3)
                    t0, wd = CHUNKS[n]
                    act.wait_ge(s_dt, u0 + u + 1)
                    if u >= 2:
                        hu, nu = divmod(u - 2, 3)
                        if nu == 2:
                            act.wait_ge(s_o, hh0 + hu + 1)
                        else:
                            act.wait_ge(s_dp, 2 * (DH * layer + hu) + nu + 1)
                    wt = flat(MG[:, 2 + 2 * (u % 2):4 + 2 * (u % 2), :])
                    full = min(n + 1, 2)
                    last = nc.scalar.copy(wt[:, 0:full * P].rearrange("p (c t) -> p c t", c=full)[:, :, 0:wd],
                                          PS[:, 4, 0:full * P].rearrange("p (c t) -> p c t", c=full)[:, :, 0:wd])
                    if n == 2:
                        last = nc.scalar.copy(wt[0:N_META, 2 * P:2 * P + wd], PS[0:N_META, 4, 2 * P:2 * P + wd])
                    last.then_inc(s_dc, 1)
                if 2 <= t < DU + 2:
                    u = t - 2
                    h, n = divmod(u, 3)
                    t0, wd = CHUNKS[n]
                    act.wait_ge(s_dx, u0 + u + 1)
                    for m in range(2):
                        e = MJ[0:wd, 2 * (u % 4) + m, 0:t0 + wd]
                        last = nc.scalar.activation(e, e, ACT.Exp, bias=dst[0:wd, u % 4, m:m + 1],
                                                    accum_out=dst[0:wd, u % 4, 2 + m:3 + m])
                    last.then_inc(s_de, 1)
                if t >= 7 and (t - 7) % 3 == 2 and t < DU + 7:
                    tail_act_square(act, 2, hh0 + (t - 7) // 3, (t - 7) // 3)
                if t >= 8 and (t - 8) % 3 == 2:
                    tail_act_rdev(act, 2, hh0 + (t - 8) // 3, (t - 8) // 3)
                if t >= 9 and (t - 9) % 3 == 2:
                    tail_act_high(act, 2, hh0 + (t - 9) // 3, (t - 9) // 3)

        def da_dve(dve, link, layer, G_end):
            u0, hh0 = DU * layer, tail_first(layer, 2)
            lambda_init = 0.8 - 0.6 * math.exp(-0.3 * layer)
            lp = COLS["lam"] + 4 * layer
            nc.vector.tensor_tensor(sm("t0")[:, 0:2], cols[:, lp:lp + 4:2], cols[:, lp + 1:lp + 4:2],
                                    ALU.mult).then_inc(s_lamp, 1)
            dve.wait_ge(s_lame, layer + 1)
            link(nc.vector.scalar_tensor_tensor(sm("lam")[:, 0:1], sm("t1")[:, 1:2], -lambda_init, sm("t1")[:, 0:1],
                                                ALU.add, ALU.subtract))
            link(nc.vector.tensor_scalar(sm("sub")[:, 0:1], col("subln", layer), 1.0 - lambda_init, None, ALU.mult))
            rope_dve(dve, cc("cos_d"), cc("sin_d"), 24 * layer + 8, 16)
            for t in range(DU + 11):
                if 3 <= t < DU + 3:
                    u = t - 3
                    h, n = divmod(u, 3)
                    t0, wd = CHUNKS[n]
                    dve.wait_ge(s_de, u0 + u + 1)
                    st = dst[0:wd, u % 4, :]
                    link(nc.vector.reciprocal(st[:, 2:4], st[:, 2:4]))
                    if u >= 2:
                        dve.wait_ge(s_dt, u0 + u - 1)
                    wgt = MG[0:wd, u % 2, 0:t0 + wd]
                    nc.vector.tensor_tensor(st[:, 3:4], st[:, 3:4], sm("lam")[0:wd, 0:1], ALU.mult)
                    link(nc.vector.tensor_scalar(wgt, MJ[0:wd, 2 * (u % 4), 0:t0 + wd], st[:, 2:3], None, ALU.mult))
                    nc.vector.scalar_tensor_tensor(wgt, MJ[0:wd, 2 * (u % 4) + 1, 0:t0 + wd], st[:, 3:4], wgt,
                                                   ALU.mult, ALU.add).then_inc(s_dw, 1)
                if 1 <= t <= DU:
                    u = t - 1
                    h, n = divmod(u, 3)
                    t0, wd = CHUNKS[n]
                    dve.wait_ge(s_ds, u0 + u + 1)
                    b = 2 * (u % 2)
                    c = 2 * (u % 4)
                    s = MJ[0:wd, c:c + 2, 0:t0 + wd]
                    if u >= 4:
                        dve.wait_ge(s_dw, u0 + u - 3)
                    mask = bc(con2[0:wd, C2["dmask"] + n * T2:C2["dmask"] + n * T2 + t0 + wd], 2)
                    nc.vector.scalar_tensor_tensor(s, PS[0:wd, b:b + 2, 0:t0 + wd], 64 ** -0.5, mask,
                                                   ALU.mult, ALU.add).then_inc(s_dm, 1)
                    dve.wait_ge(s_dm, u0 + u + 1)
                    nc.vector.tensor_reduce(dst[0:wd, u % 4, 0:2], s, AX.X, ALU.max, negate=True).then_inc(s_dx, 1)
                if t >= 10 and (t - 10) % 3 == 2:
                    tail_dve_low(dve, 2, hh0 + (t - 10) // 3, (t - 10) // 3)
                if t >= 9 and (t - 9) % 3 == 2:
                    tail_dve_gate(dve, link, 2, hh0 + (t - 9) // 3, (t - 9) // 3)

        NL = len(LEVELS)
        Q_, CBT, K_ = MI[:, 0:8, :], MI[:, 8:16, :], MI[:, 16:24, :]
        KDT = flat(QB[:])[:, 0:2 * D].rearrange("p (n f) -> p n f", n=2)
        ST = flat(CBT)[:, 0:2 * D].rearrange("p (n f) -> p n f", n=2)
        LEVEL_PE = 1 + NL
        HT = LEVEL_PE + 4

        def halves(ap, s):
            if s <= 8:
                v = flat(ap).rearrange("p (b w t) -> p b w t", w=2, t=s)
                nb = KT * T2 // (2 * s)
                pitch = 2 * s
                left, right, ref = v[:, :, 0, :], v[:, :, 1, :], v[:, :, 0, s - 1:s]
                ref = bass.AP(ref.tensor, ref.offset, [ref.ap[0], [pitch, nb], [0, s]])
                return left, right, ref
            v = ap[:, :, 0:2 * P].rearrange("p h (b w t) -> p h b w t", w=2, t=s)
            left, right, ref = v[:, :, :, 0, :], v[:, :, :, 1, :], v[:, :, :, 0, s - 1:s]
            ref = bass.AP(ref.tensor, ref.offset, [ref.ap[0], [T2, KT], [2 * s, 2 * P // (2 * s)], [0, s]])
            return left, right, ref

        def hg_scores(lhs, rhs, with_last):
            for h in range(HH):
                for n, (t0, wd) in enumerate(CHUNKS):
                    if n == 2 and not with_last:
                        continue
                    out = PS[:, 2 * n + h // 4, (h % 4) * P:(h % 4 + 1) * P] if n < 2 else PS[0:wd, 4, h * wd:(h + 1) * wd]
                    last = nc.tensor.matmul(out, lhs[:, h, t0:t0 + wd], rhs[:, h, t0:t0 + wd], start=True, stop=True)
            return last

        def hg_pe(pe, layer, G_end):
            pe.wait_ge(s_free, 2 * G_end + 4)
            t, d, a, p = HT * layer, HDV * layer, HAC * layer, HPO * layer
            values_pe(pe, MJ, 3 * layer + 1)
            pe.wait_ge(s_vc, 3 * (3 * layer + 2))
            pe.wait_ge(s_hp, p + 1)
            hg_scores(K_, Q_, True).then_inc(s_ht, 1)
            for n, s in enumerate(LEVELS):
                pe.wait_ge(s_hd, d + HD_PRED + 3 * n)
                pe.wait_ge(s_hd, d + HD_PRED + 3 * n + 1)
                hg_scores(QB, QB, s <= 8).then_inc(s_ht, 1)
            pe.wait_ge(s_hd, d + HD_END + 2)
            for n in range(2):
                for h in range(HH):
                    last = nc.tensor.transpose(PS[:, 2 * n + h // 4, (h % 4) * P:(h % 4 + 1) * P],
                                               K_[:, h, n * P:(n + 1) * P], ident)
                last.then_inc(s_ht, 1)
            for n in range(2):
                pe.wait_ge(s_ha, a + HA_KT + n + 1)
                for h in range(HH):
                    f = slice(h * P, (h + 1) * P)
                    last = nc.tensor.matmul(PS[:, 4 + 2 * n + h // 4, (h % 4) * P:(h % 4 + 1) * P],
                                            KDT[:, n, f], VT[:, n, f], start=True, stop=True)
                last.then_inc(s_ht, 1)
            pe.wait_ge(s_hd, d + HDV)
            hh0 = tail_first(layer, 1)
            for h in range(HH):
                if h >= 2:
                    pe.wait_ge(s_ot, hh0 + h - 1)
                f = slice(h * P, (h + 1) * P)
                for n, (t0, wd) in enumerate(CHUNKS):
                    out = PS[:, out_bank(1, h), t0:t0 + wd]
                    last = nc.tensor.matmul(out, VT[0:wd, n, f], AM[0:wd, h, t0:t0 + wd], start=True, stop=(n == 0))
                    if n:
                        last = nc.tensor.matmul(out, ST[:, n - 1, f], Q_[:, h, t0:t0 + wd], start=False, stop=True)
                last.then_inc(s_o, 1)
                if h:
                    tail_pe(pe, 1, hh0 + h - 1, h - 1)
            tail_pe(pe, 1, hh0 + HH - 1, HH - 1)

        HD_LOG = 3
        HD_PRED = HD_LOG + 3
        HD_END = HD_LOG + 1 + 3 * NL
        HDV = HD_END + 4
        HA_LEVEL = 2
        HA_KT = HA_LEVEL + NL + 2
        HAC = HA_KT + 2
        HPO = 1 + NL

        def hg_act(act, layer, G_end):
            t, d, a, p = HT * layer, HDV * layer, HAC * layer, HPO * layer
            values_act(act, 3 * layer + 1)
            act.wait_ge(s_hd, d + 1)
            e = small[:, 15 * KT:17 * KT]
            nc.scalar.activation(e, e, ACT.Exp).then_inc(s_ha, 1)
            act.wait_ge(s_hd, d + 3)
            nc.scalar.activation(MJ[:], MJ[:], ACT.Ln)
            nc.scalar.activation(CBT, CBT, ACT.Ln).then_inc(s_ha, 1)
            for n, s in enumerate(LEVELS):
                act.wait_ge(s_hd, d + HD_LOG + 2 + 3 * n)
                act.wait_ge(s_hp, p + 2 + n)
                e = MJ[:] if s <= 8 else MJ[:, :, 0:2 * P]
                nc.scalar.activation(e, e, ACT.Exp).then_inc(s_ha, 1)
            act.wait_ge(s_hd, d + HD_PRED + 3 * (NL - 1) + 1)
            nc.scalar.activation(MJ[:], CBT, ACT.Exp)
            nc.scalar.activation(sm("t0"), CBT[:, :, 2 * P - 1], ACT.Exp).then_inc(s_ha, 1)
            act.wait_ge(s_hd, d + HD_END + 1)
            nc.scalar.activation(MJ[:, :, 0:2 * P], MJ[:, :, 0:2 * P], ACT.Exp).then_inc(s_ha, 1)
            for n in range(2):
                act.wait_ge(s_ht, t + LEVEL_PE + n + 1)
                nc.scalar.copy(KDT[:, n, :].rearrange("p (a t) -> p a t", a=2),
                               PS[:, 2 * n:2 * n + 2, :]).then_inc(s_ha, 1)
            hh0 = tail_first(layer, 1)
            for h in range(HH + 1):
                if h >= 2:
                    tail_act_rdev(act, 1, hh0 + h - 2, h - 2)
                    tail_act_high(act, 1, hh0 + h - 2, h - 2)
                if h >= 1:
                    tail_act_square(act, 1, hh0 + h - 1, h - 1)
            tail_act_rdev(act, 1, hh0 + HH - 1, HH - 1)
            tail_act_high(act, 1, hh0 + HH - 1, HH - 1)

        def hg_pool(pool, layer, G_end):
            d, a, p = HDV * layer, HAC * layer, HPO * layer
            pool.wait_ge(s_free, 2 * G_end + 4)
            nc.gpsimd.memset(AM[:], 0.0)
            pool.wait_ge(s_hd, d + 2)
            for h in range(HH):
                last = nc.gpsimd.tensor_scalar(K_[:, h, :], K_[:, h, :], sm(f"olb{layer}")[:, h:h + 1], None, ALU.mult)
            last.then_inc(s_hp, 1)
            for n, s in enumerate(LEVELS):
                pool.wait_ge(s_hd, d + HD_LOG + 1 + 3 * n)
                left, _, _ = halves(MJ[:], s)
                cl, _, ref = halves(CBT, s)
                nc.gpsimd.tensor_tensor(left, ref, cl, ALU.subtract).then_inc(s_hp, 1)

        def hg_dve(dve, link, layer, G_end):
            t, d, a, p = HT * layer, HDV * layer, HAC * layer, HPO * layer
            a0 = col("hg_lb", 0, KT)
            a1 = col("hg_lb", KT, KT)
            link(nc.vector.tensor_tensor(sm("t0"), a0, a1, ALU.max))
            link(nc.vector.tensor_tensor(sm("t1"), a0, sm("t0"), ALU.subtract))
            nc.vector.tensor_tensor(sm("t2"), a1, sm("t0"), ALU.subtract).then_inc(s_hd, 1)
            dve.wait_ge(s_ha, a + 1)
            lbm, olb = sm(f"lbm{layer}"), sm(f"olb{layer}")
            link(nc.vector.tensor_tensor(sm("t3"), sm("t1"), sm("t2"), ALU.add))
            link(nc.vector.reciprocal(sm("t3"), sm("t3")))
            link(nc.vector.tensor_tensor(sm("t1"), sm("t1"), sm("t3"), ALU.mult))
            link(nc.vector.tensor_tensor(sm("t2"), sm("t2"), sm("t3"), ALU.mult))
            if layer == 0:
                link(nc.vector.tensor_tensor(sm("t3"), sm("t1"), sm("t1"), ALU.subtract))
            else:
                link(nc.vector.tensor_tensor(sm("t3"), sm("t1"), sm("t2"), ALU.add))
                link(nc.vector.tensor_tensor(sm("t3"), sm("t3"), sm("t1"), ALU.subtract))
            link(nc.vector.tensor_scalar(lbm, sm("t3"), 1e-30, None, ALU.max))
            nc.vector.tensor_scalar(olb, sm("t3"), -1.0, 1.0, ALU.mult, ALU.add).then_inc(s_hd, 1)
            dve.wait_ge(s_hd, d + 2)
            for h in range(HH):
                last = nc.vector.tensor_scalar(CBT[:, h, :], CBT[:, h, :], olb[:, h:h + 1], lbm[:, h:h + 1],
                                               ALU.mult, ALU.add)
            link(last)
            dve.wait_ge(s_vt, 3 * (3 * layer + 2))
            link(nc.vector.tensor_scalar(MJ[:], CBT, 2.0 ** -60, None, ALU.max))
            nc.vector.tensor_scalar(CBT, CBT, 2.0 ** 60, 1.0, ALU.mult, ALU.min).then_inc(s_hd, 1)
            dve.wait_ge(s_ha, a + 2)
            link(nc.vector.tensor_tensor(CBT, CBT, MJ[:], ALU.add))
            for h in range(HH):
                last = nc.vector.tensor_tensor_scan(CBT[:, h, :], cc("reset"), CBT[:, h, :], 0.0, ALU.mult, ALU.add)
            last.then_inc(s_hd, 1)
            dve.wait_ge(s_hd, d + HD_LOG + 1)

            def pick(n):
                dve.wait_ge(s_ht, t + n + 1)
                if n == 0:
                    dve.wait_ge(s_hp, p + 1)
                m = C2["levels"] + n * P
                for c, (t0, wd) in enumerate(CHUNKS):
                    if c == 2 and n and LEVELS[n - 1] > 8:
                        continue
                    mask = con2[0:wd, m:m + wd].bitcast(I32)
                    if c < 2:
                        for g in range(2):
                            last = nc.vector.copy_predicated(AM[:, 4 * g:4 * g + 4, t0:t0 + wd], bc(mask, 4),
                                                             PS[:, 2 * c + g, :].rearrange("p (h t) -> p h t", h=4))
                    else:
                        last = nc.vector.copy_predicated(AM[0:wd, :, t0:t0 + wd], bc(mask, HH),
                                                         PS[0:wd, 4, 0:HH * wd].rearrange("p (h t) -> p h t", h=HH))
                return last

            for n, s in enumerate(LEVELS):
                el, er, _ = halves(MJ[:], s)
                cl, cr, ref = halves(CBT, s)
                kl, _, _ = halves(K_, s)
                _, qr, _ = halves(Q_, s)
                bl, br, _ = halves(QB[:], s)
                dve.wait_ge(s_hd, d + HD_LOG + 1 + 3 * n)
                nc.vector.tensor_tensor(er, cr, ref, ALU.subtract).then_inc(s_hd, 1)
                pick(n).then_inc(s_hd, 1)
                dve.wait_ge(s_ha, a + HA_LEVEL + n + 1)
                nc.vector.tensor_tensor(bl, el, kl, ALU.mult)
                nc.vector.tensor_tensor(br, er, qr, ALU.mult).then_inc(s_hd, 1)
            link(pick(NL))
            dve.wait_ge(s_ha, a + HA_LEVEL + NL + 1)
            link(nc.vector.tensor_tensor(Q_, Q_, MJ[:], ALU.mult))
            c2 = CBT[:, :, 0:2 * P].rearrange("p h (c t) -> p h c t", c=2)
            ref = bass.AP(c2.tensor, c2.offset + P - 1, [c2.ap[0], [T2, KT], [P, 2], [0, P]])
            e2 = MJ[:, :, 0:2 * P].rearrange("p h (c t) -> p h c t", c=2)
            nc.vector.tensor_tensor(e2, ref, c2, ALU.subtract).then_inc(s_hd, 1)
            dve.wait_ge(s_ha, a + HA_LEVEL + NL + 2)
            k2 = K_[:, :, 0:2 * P]
            nc.vector.tensor_tensor(k2, k2, MJ[:, :, 0:2 * P], ALU.mult).then_inc(s_hd, 1)
            dve.wait_ge(s_ht, t + LEVEL_PE + 3)
            nc.vector.tensor_copy(ST[:, 0, :].rearrange("p (a t) -> p a t", a=2), PS[:, 4:6, :]).then_inc(s_hd, 1)
            dve.wait_ge(s_hd, d + HD_END + 3)
            dve.wait_ge(s_ht, t + LEVEL_PE + 4)
            for h in range(HH):
                f = slice(h * P, (h + 1) * P)
                last = nc.vector.scalar_tensor_tensor(ST[:, 1, f], ST[:, 0, f], sm("t0")[:, h:h + 1],
                                                      PS[:, 6 + h // 4, (h % 4) * P:(h % 4 + 1) * P],
                                                      ALU.mult, ALU.add)
            last.then_inc(s_hd, 1)
            hh0 = tail_first(layer, 1)
            for h in range(HH):
                tail_dve(dve, link, 1, hh0 + h, h)

        NU = 4 * KT

        def na_pe(pe, G_end):
            pe.wait_ge(s_free, 2 * G_end + 4)
            for n in range(4):
                if n >= 2:
                    pe.wait_ge(s_nvc, n - 1)
                for f in range(KT):
                    last = nc.tensor.transpose(PS[:, 2 * (n % 2) + f // 4, (f % 4) * P:(f % 4 + 1) * P],
                                               NVT[:, f, n * P:(n + 1) * P], ident)
                last.then_inc(s_nvt, 1)
            for u in range(2 * KT):
                if u >= 2:
                    pe.wait_ge(s_nr1, u - 1)
                src = NQ if u < KT else NK
                nc.tensor.matmul(PS[:, 6 + u % 2, 0:SEQ], con1[:, C1["rot"]:C1["rot"] + P], src[:, u % KT, 0:SEQ],
                                 start=True, stop=True).then_inc(s_nrot, 1)
            pe.wait_ge(s_nr2, 4 * KT)
            pe.wait_ge(s_nvc, 4)
            for t in range(NU + 6):
                if t < NU:
                    hp, hl, qt = t // 4, t // 2 % 2, t % 2
                    r = slice(64 * hl, 64 * hl + 64)
                    if t >= 2:
                        pe.wait_ge(s_na, t - 1)
                    nc.tensor.matmul(PS[:, t % 2, :], NQ[r, hp, qt * P:(qt + 1) * P], NK[r, hp, :],
                                     start=True, stop=True).then_inc(s_ns, 1)
                if t >= 6:
                    u = t - 6
                    hp, hl, qt = u // 4, u // 2 % 2, u % 2
                    pe.wait_ge(s_nc, u + 1)
                    if u % 4 == 0 and hp >= 2:
                        pe.wait_ge(s_no_low, hp - 1)
                    for c in range(4):
                        last = nc.tensor.matmul(PS[64 * hl:64 * hl + 64, 6 + hp % 2, qt * P:(qt + 1) * P],
                                                NV[:, c, (2 * hp + hl) * HD:(2 * hp + hl + 1) * HD],
                                                PT[:, u % 2, c * P:(c + 1) * P], start=(c == 0), stop=(c == 3))
                    last.then_inc(s_no, 1)
                if 4 <= t < NU + 4:
                    u = t - 4
                    pe.wait_ge(s_nw, u + 1)
                    if u >= 2:
                        pe.wait_ge(s_nc, u - 1)
                    for c in range(4):
                        last = nc.tensor.transpose(PS[:, 2 + u % 2, c * P:(c + 1) * P],
                                                   SB[:, u % 4, c * P:(c + 1) * P], ident)
                    last.then_inc(s_nt, 1)

        def na_act(act, G_end):
            for n in range(4):
                act.wait_ge(s_nvt, n + 1)
                nc.scalar.copy(NV[:, n, :].rearrange("p (a t) -> p a t", a=2),
                               PS[:, 2 * (n % 2):2 * (n % 2) + 2, :]).then_inc(s_nvc, 1)
            for t in range(NU + 8):
                if 5 <= t < NU + 5:
                    u = t - 5
                    act.wait_ge(s_nt, u + 1)
                    if u >= 2:
                        act.wait_ge(s_no, u - 1)
                    nc.scalar.copy(PT[:, u % 2, :], PS[:, 2 + u % 2, :]).then_inc(s_nc, 1)
                if 1 <= t <= NU:
                    u = t - 1
                    act.wait_ge(s_nm, u + 1)
                    nc.scalar.activation(SB[:, u % 4, :], SB[:, u % 4, :], ACT.Exp, bias=nst[:, u % 4, 0:1],
                                         accum_out=nst[:, u % 4, 1:2]).then_inc(s_ne, 1)
                if t >= 7 and (t - 7) % 4 == 3:
                    hp = (t - 7) // 4
                    act.wait_ge(s_no, 4 * hp + 4)
                    nc.scalar.copy(XH[:, hp, 0:SEQ], PS[:, 6 + hp % 2, 0:SEQ]).then_inc(s_no_high, 1)

        def na_dve(dve, link, G_end):
            dve.wait_ge(s_bias, 16 * 12)
            colmask = con1[:, C1["colmask"]:C1["colmask"] + GRID_W]
            nc.vector.tensor_tensor(TB[:].rearrange("p h j c -> p (h j) c"), TB[:].rearrange("p h j c -> p (h j) c"),
                                    bc(colmask, 6 * NH), ALU.add)
            cos, sin = (con1[:, C1[x]:C1[x] + SEQ] for x in ("cos", "sin"))
            for u in range(2 * KT):
                x = (NQ if u < KT else NK)[:, u % KT, 0:SEQ]
                dve.wait_ge(s_nrot, u + 1)
                nc.vector.tensor_tensor(ROT[:, u % 2, :], PS[:, 6 + u % 2, 0:SEQ], sin, ALU.mult).then_inc(s_nr1, 1)
                nc.vector.tensor_tensor(x, x, cos, ALU.mult).then_inc(s_nr2, 1)
                dve.wait_ge(s_nr1, u + 1)
                dve.wait_ge(s_nr2, 2 * u + 1)
                nc.vector.tensor_tensor(x, x, ROT[:, u % 2, :], ALU.add).then_inc(s_nr2, 1)
            dve.wait_ge(s_nvt, 4)
            for t in range(NU + 8):
                if 2 <= t < NU + 2:
                    u = t - 2
                    dve.wait_ge(s_ne, u + 1)
                    nc.vector.reciprocal(nst[:, u % 4, 2:3], nst[:, u % 4, 1:2]).then_inc(s_nr, 1)
                if t < NU:
                    hd, qt = t // 2, t % 2
                    dve.wait_ge(s_ns, t + 1)
                    if t >= 4:
                        dve.wait_ge(s_nt, t - 3)
                    b = TB[:, hd, 2 - 2 * qt:6 - 2 * qt, :].rearrange("p j c -> p (j c)")
                    nc.vector.tensor_tensor(SB[:, t % 4, 0:SEQ], PS[:, t % 2, 0:SEQ], b, ALU.add)
                    nc.vector.tensor_copy(SB[:, t % 4, SEQ:T1], PS[:, t % 2, SEQ:T1]).then_inc(s_na, 1)
                    dve.wait_ge(s_na, t + 1)
                    nc.vector.tensor_reduce(nst[:, t % 4, 0:1], SB[:, t % 4, :], AX.X, ALU.max,
                                            negate=True).then_inc(s_nm, 1)
                if t >= 7 and (t - 7) % 4 == 3:
                    na_low(dve, (t - 7) // 4)

        def na_low(dve, hp):
            dve.wait_ge(s_no_high, hp + 1)
            nc.vector.tensor_tensor(XL[:, hp, 0:SEQ], PS[:, 6 + hp % 2, 0:SEQ], XH[:, hp, 0:SEQ].bitcast(F32),
                                    ALU.subtract).then_inc(s_no_low, 1)

        def na_pool(pool):
            for u in range(NU):
                pool.wait_ge(s_nr, u + 1)
                nc.gpsimd.tensor_scalar(SB[:, u % 4, :], SB[:, u % 4, :], nst[:, u % 4, 2:3], None,
                                        ALU.mult).then_inc(s_nw, 1)

        def rms_pe(pe, m):
            for hf in range(2):
                pe.wait_ge(s_rsq, 2 * m + hf + 1)
                for k in range(4 * hf, 4 * hf + 4):
                    last = nc.tensor.matmul(PS[:, 1, 0:T2], ones[:], TN[:, k, :], start=(k == 0), stop=(k == KT - 1))
            last.then_inc(s_rsum, 1)

        def rms_act(act, m, G_end):
            if m:
                act.wait_ge(s_free, 2 * G_end + 4)
            else:
                act.wait_ge(s_res, 6 * KT + KT)
                act.wait_ge(s_meta, 32)
            for hf in range(2):
                k = slice(4 * hf, 4 * hf + 4)
                nc.scalar.activation(TN[:, k, :], H[:, k, :], ACT.Square).then_inc(s_rsq, 1)
            act.wait_ge(s_rsum, m + 1)
            nc.scalar.activation(RS[:, 0, 0:T2], PS[:, 1, 0:T2], ACT.Ln, bias=epsc[:, 0:1],
                                 scale=1.0 / D).then_inc(s_rln, 1)
            act.wait_ge(s_rln, m + 1)
            nc.scalar.activation(RS[:, 1, 0:T2], RS[:, 0, 0:T2], ACT.Exp, scale=-0.5).then_inc(s_rrd, 1)
            if m < 4:
                for k in range(0, KT, 2):
                    act.wait_ge(s_rmod, KT * m + k + 2)
                    nc.scalar.copy(NHh[:, k:k + 2, :], TN[:, k:k + 2, :]).then_inc(s_rxh, 1)

        def rms_dve(dve, m, name, layer):
            dve.wait_ge(s_rrd, m + 1)
            for k in range(KT):
                out = s_rmod if m < 4 else s_modd_final
                nc.vector.scalar_tensor_tensor(TN[:, k, :], H[:, k, :], col(name, layer * KT + k), RS[:, 1, 0:T2],
                                               ALU.mult, ALU.mult).then_inc(out, 1)
            if m < 4:
                for hf in range(2):
                    k = slice(4 * hf, 4 * hf + 4)
                    dve.wait_ge(s_rxh, 4 * m + 2 * hf + 2)
                    nc.vector.tensor_tensor(NHl[:, k, :], TN[:, k, :], NHh[:, k, :].bitcast(F32),
                                            ALU.subtract).then_inc(s_rxl, 1)

        block = ctx.enter_context(nc.Block())

        @block.sync
        def _(sp):
            for s in steps:
                for i in groups_of(sp, s):
                    for pi, (k0, nk) in enumerate(s["panels"]):
                        g = s["g0"] + len(s["panels"]) * i + pi
                        for q in range(4):
                            n = 2 if q < 3 else nk - 6
                            sp.wait_ge(s_low, 4 * g + q + 1)
                            for x, src in enumerate(s["src"](i, k0 + 2 * q, n)):
                                if n == 2 and not s["halves"]:
                                    dst = raw[:, q, x, :]
                                else:
                                    dst = raw[:, q, 0:n, x * PW // 2:(x + 1) * PW // 2]
                                    if not s["halves"]:
                                        dst = dst.rearrange("p k n -> p (k n)")
                                sp.dma_start(dst, src).then_inc(s_raw[q], 16)
            sp.wait_ge(s_modd_final, KT)
            sp.dma_start(out_d, TN[:, :, N_META:T2]).then_inc(s_out, 16)
            sp.wait_ge(s_out, 16)

        @block.tensor
        def _(pe):
            pe.sem_inc(s_half, 1)
            pe.sem_inc(s_half, 1)
            norms = rmss = 0

            for s in steps:
                name, T, t0 = s["name"], s["T"], s["t0"]
                if name == "ada":
                    pe.wait_ge(s_sc4, 2)
                    pe.wait_ge(s_tokens, 48)
                elif name in ("glu", "q", "cgate"):
                    pe.wait_ge(s_xl, 2 * (norms + 1))
                elif name == "res" and s["layer"] == 0 and s["r"] == 1:
                    pe.wait_ge(s_no_low, KT)
                if name == "res" and not (s["layer"] == 0 and s["r"] == 1):
                    pe.wait_ge(s_hl, s["hid0"] + 2)
                if s.get("after_rms"):
                    pe.wait_ge(s_rxl, 2 * rmss)
                if name == "branch":
                    pe.wait_ge(s_tail_low, tail_count(s["layer"], s["n"]))
                if name == "add":
                    if len(s["panels"]) == 1:
                        pe.wait_ge(s_yl, 2 * (s["layer"] + 1))
                    else:
                        pe.wait_ge(s_hl, s["hid0"] + 2)
                if name in ("glu", "q", "k", "v", "cgate"):
                    mh, ml = XH, XL
                elif name == "res":
                    mh, ml = (XH, XL) if (s["layer"] == 0 and s["r"] == 1) else (GH, GL)
                elif name in ("store", "gate", "forget", "mgate", "conv"):
                    mh, ml = NHh, NHl
                elif name == "branch":
                    mh, ml = OH, OL
                elif name == "add":
                    mh, ml = (NHh, NHl) if len(s["panels"]) == 1 else (G2H, G2L)
                colof = COLOF[s["halves"]]
                def columns_of(i):
                    G = s["G0"] + i
                    pe.wait_ge(s_adarow, G + 1)
                    out = bank(G, 2).rearrange("p a n -> p (a n)")
                    for j in range(4):
                        last = nc.tensor.matmul(out[:, 2 * j:2 * j + 2], adarow[:, j * P:(j + 1) * P],
                                                con1[:, C1["pair"]:C1["pair"] + 2], start=True, stop=True)
                    last.then_inc(s_pair0, 1)

                def ada_group(i, first=False):
                    G, g = s["G0"] + i, s["g0"] + i
                    out = bank(G, 0).rearrange("p a n -> p (a n)")
                    pe.wait_ge(s_free, 2 * G + 1)
                    for hf in range(2):
                        pe.wait_ge(s_low, 4 * g + 2 * hf + 6)
                        for k in range(4 * hf, 4 * hf + 4):
                            nc.tensor.matmul(out, SC4[:, k, :], high[:, k // 2, k % 2, :], start=(k == 0), stop=False)
                            last = nc.tensor.matmul(out, SC4[:, k, :], low[:, k // 2, k % 2, :], start=False,
                                                    stop=(k == KT - 1))
                        last.then_inc(s_half, 1)
                        if hf == 0 and not first:
                            columns_of(i - 1)

                def gemm_group(i):
                    G = s["G0"] + i
                    for pi, (k0, nk) in enumerate(s["panels"]):
                        g = s["g0"] + len(s["panels"]) * i + pi
                        last_panel = pi == len(s["panels"]) - 1
                        for hf in range(2):
                            pe.wait_ge(s_low, 4 * g + 2 * hf + 6)
                            ks = range(4) if hf == 0 else range(4, nk)
                            for j in range(4):
                                if pi == 0 and hf == 0 and j % 2 == 0:
                                    pe.wait_ge(s_free, 2 * G + j // 2 + 1)
                                out = bank(G, j)[:, :, 0:T].rearrange("p a n -> p (a n)")
                                c = colof[j]
                                for k in ks:
                                    wh = high[:, k // 2, k % 2, c:c + P]
                                    wl = low[:, k // 2, k % 2, c:c + P]
                                    xh, xl = mh[:, k0 + k, t0:t0 + T], ml[:, k0 + k, t0:t0 + T]
                                    nc.tensor.matmul(out, wh, xh, start=(k0 + k == 0), stop=False)
                                    nc.tensor.matmul(out, wh, xl, start=False, stop=False)
                                    last = nc.tensor.matmul(out, wl, xh, start=False,
                                                            stop=(last_panel and k == nk - 1))
                                if last_panel and hf == 1 and j == 1:
                                    last.then_inc(s_pair0, 1)
                            last.then_inc(s_half, 1)

                if name == "ada":
                    ada_group(0, first=True)
                    with pe.Fori(1, s["groups"]) as i:
                        ada_group(i)
                    columns_of(s["groups"] - 1)
                else:
                    for i in groups_of(pe, s):
                        gemm_group(i)
                G_end = s["G0"] + s["groups"]
                if s.get("norm"):
                    pe.wait_ge(s_free, 2 * G_end + 4)
                    if norms == 0:
                        pe.wait_ge(s_ones, 1)
                    ones_sum(PS[:, 0, 0:T], X[:, :, 0:T], KT).then_inc(s_sum, 1)
                    for hf in range(2):
                        pe.wait_ge(s_sq, 2 * norms + hf + 1)
                        for k in range(4 * hf, 4 * hf + 4):
                            last = nc.tensor.matmul(PS[:, 1, 0:T], ones[:], TQ[:, k, 0:T], start=(k == 0),
                                                    stop=(k == KT - 1))
                    last.then_inc(s_var, 1)
                    norms += 1
                    if norms == 6:
                        rms_pe(pe, rmss)
                        rmss += 1
                if s.get("rms"):
                    rms_pe(pe, rmss)
                    rmss += 1
                if name == "v":
                    na_pe(pe, G_end)
                if "mixer" in s:
                    (ret_pe, hg_pe, da_pe)[s["mixer"]](pe, s["layer"], G_end)
                    pe.wait_ge(s_ot, tail_count(s["layer"], s["mixer"]))

        @block.scalar
        def _(act):
            norms = rmss = 0

            def split_high(g, q, n):
                act.wait_ge(s_raw[q], 32 * (g + 1))
                act.wait_ge(s_half, 2 * g + q // 2 + 1)
                nc.scalar.copy(high[:, q, 0:n, :], raw[:, q, 0:n, :]).then_inc(s_high, 1)

            def split_x_high(m):
                for k in range(0, KT, 2):
                    act.wait_ge(s_modd, KT * m + k + 2)
                    T = T1 if m < 2 else SEQ
                    nc.scalar.copy(XH[:, k:k + 2, 0:T], TQ[:, k:k + 2, 0:T]).then_inc(s_xh, 1)

            act.wait_ge(s_tokens, 48)
            cin = cols[:, COLS["c"]:COLS["c"] + 2 * KT]
            nc.scalar.activation(scf[:, 0:2 * KT], cin, ACT.Sigmoid).then_inc(s_silu, 1)
            act.wait_ge(s_sc4, 1)
            scv = scf[:, 2 * KT:4 * KT].rearrange("p (c k) -> p c k", c=2)
            for c in range(2):
                last = nc.scalar.copy(SC4[:, :, 2 * c], scv[:, c, :])
            last.then_inc(s_silu, 1)
            split_high(0, 0, 2)
            split_high(0, 1, 2)
            first_mod = True
            for s in steps:
                name, T, np_ = s["name"], s["T"], len(s["panels"])
                if name == "glu" and first_mod:
                    first_mod = False
                    split_x_high(0)
                def splits(i):
                    for pi, (k0, nk) in enumerate(s["panels"]):
                        g = s["g0"] + np_ * i + pi
                        split_high(g, 2, 2)
                        split_high(g, 3, nk - 6)
                        if not is_last(s, i, pi):
                            split_high(g + 1, 0, 2)
                            split_high(g + 1, 1, 2)

                def epilogue(i):
                    G = s["G0"] + i
                    g_last = s["g0"] + np_ * (i + 1)

                    def pair_ready(p):
                        if p == 0:
                            act.wait_ge(s_pair0, G + 1)
                        else:
                            act.wait_ge(s_half, 2 * g_last + 2)

                    if name == "glu":
                        for p in range(2):
                            pair_ready(p)
                            nc.scalar.activation(SG[:, p:p + 1, 0:T], bank(G, 2 * p)[:, :, 0:T],
                                                 ACT.Sigmoid).then_inc(s_act, 1)
                        for p in range(2):
                            act.wait_ge(s_free, 2 * G + p + 5)
                            nc.scalar.copy(GH[:, bass.ds(2 * i + p, 1), 0:T], GB[:, p:p + 1, 0:T]).then_inc(s_hh, 1)
                    elif name == "cgate":
                        for p in range(2):
                            pair_ready(p)
                            act.wait_ge(s_free, 2 * G + p + 3)
                            nc.scalar.copy(SG[:, p:p + 1, 0:T], bank(G, 2 * p)[:, :, 0:T]).then_inc(s_act, 1)
                    elif name == "bgate":
                        for p in range(2):
                            act.wait_ge(s_free, 2 * G + p + 5)
                            nc.scalar.copy(GH[:, bass.ds(4 * i + 2 * p, 2), 0:T],
                                           GB[:, p, :].rearrange("p (a t) -> p a t", a=2)).then_inc(s_hh, 1)
                    elif name in ("gate", "mgate"):
                        for p in range(2):
                            pair_ready(p)
                            nc.scalar.activation(gate_room(s, 4 * i + 2 * p), bank(G, 2 * p, 2)[:, :, 0:T],
                                                 ACT.Sigmoid).then_inc(s_act, 1)
                    elif name == "forget":
                        for p in range(2):
                            pair_ready(p)
                            ps = bank(G, 2 * p, 2)[:, :, 0:T]
                            nc.scalar.activation(MI[:, bass.ds(8 + 4 * i + 2 * p, 2), :], ps,
                                                 ACT.Sigmoid).then_inc(s_act, 1)
                            nc.scalar.activation(MI[:, bass.ds(16 + 4 * i + 2 * p, 2), :], ps, ACT.Sigmoid,
                                                 scale=-1.0).then_inc(s_act, 1)
                    elif name == "conv":
                        for j in range(4):
                            if j % 2 == 0:
                                pair_ready(j // 2)
                            ft = FT * (j % 2) + 2 * i + j // 2
                            nc.scalar.activation(CB[:, j:j + 1, :], bank(G, j)[:, :, 0:T], ACT.Identity,
                                                 bias=col("conv_b", s["layer"] * 2 * FT + ft),
                                                 scale=col("conv_w", (3 * s["layer"] + 2) * 2 * FT + ft)
                                                 ).then_inc(s_act, 1)
                        for p in range(2):
                            act.wait_ge(s_free, 2 * G + p + 5)
                            nc.scalar.activation(SG2[:, p:p + 1, :], CB[:, 2 * p:2 * p + 1, :],
                                                 ACT.Sigmoid).then_inc(s_act, 1)
                        for p in range(2):
                            act.wait_ge(s_gb, s["gb0"] + 2 * i + p + 1)
                            nc.scalar.copy(G2H[:, bass.ds(2 * i + p, 1), :], SG2[:, 2 + p:3 + p, :]).then_inc(s_hh, 1)

                groups_behind(act, s, splits, epilogue)
                G_end = s["G0"] + s["groups"]
                if s.get("norm"):
                    m = norms
                    for hf in range(2):
                        k = slice(4 * hf, 4 * hf + 4)
                        act.wait_ge(s_cen, 2 * m + hf + 1)
                        nc.scalar.activation(TQ[:, k, 0:T], TC[:, k, 0:T], ACT.Square).then_inc(s_sq, 1)
                    act.wait_ge(s_var, m + 1)
                    nc.scalar.activation(RS[:, 0, 0:T], PS[:, 1, 0:T], ACT.Ln, bias=epsc[:, 0:1],
                                         scale=1.0 / D).then_inc(s_ln, 1)
                    act.wait_ge(s_ln, m + 1)
                    nc.scalar.activation(RS[:, 1, 0:T], RS[:, 0, 0:T], ACT.Exp, scale=-0.5).then_inc(s_rdev, 1)
                    if m < 5:
                        split_x_high(m + 1)
                    else:
                        act.wait_ge(s_modd, KT * 6 + 1)
                    for k in range(KT):
                        dst = X[:, k, 0:T] if m < 5 else H[:, k, N_META:T2]
                        nc.scalar.activation(dst, TC[:, k, 0:T], ACT.Identity, bias=sm("xb")[:, k:k + 1],
                                             scale=sm("xg")[:, k:k + 1]).then_inc(s_res, 1)
                    norms += 1
                    if norms == 6:
                        rms_act(act, 0, G_end)
                        rmss = 1
                if s.get("rms"):
                    rms_act(act, rmss, G_end)
                    rmss += 1
                if name == "v":
                    na_act(act, G_end)
                if "mixer" in s:
                    (ret_act, hg_act, da_act)[s["mixer"]](act, s["layer"], G_end)
                if name == "branch" and s["n"] == 2:
                    act.wait_ge(s_yadd, 8 * (s["layer"] + 1))
                    for hf in range(2):
                        k = slice(4 * hf, 4 * hf + 4)
                        nc.scalar.copy(NHh[:, k, :], Y[:, k, :]).then_inc(s_yh, 1)

        @block.vector
        def _(dve):
            chain = [0]

            def link(ins):
                chain[0] += 1
                ins.then_inc(s_chain, 1)
                dve.wait_ge(s_chain, chain[0])

            norms = rmss = 0
            for _ in range(4):
                dve.sem_inc(s_low, 1)
                dve.sem_inc(s_free, 1)

            def split_low(g, q, n):
                dve.wait_ge(s_high, 4 * g + q + 1)
                nc.vector.tensor_tensor(low[:, q, 0:n, :], raw[:, q, 0:n, :], high[:, q, 0:n, :].bitcast(F32),
                                        ALU.subtract).then_inc(s_low, 1)

            def columns(m):
                layer, r = divmod(m, 3)
                ng = (layer * 3 + r - 1) if m else None
                for c in range(2 if m < 2 else 1):
                    v = mod[:, layer, c, :]
                    shift, scale, gate = (v[:, (3 * r + x) * KT:(3 * r + x + 1) * KT] for x in range(3))
                    link(nc.vector.tensor_scalar(sm("ag", c), scale, 1.0, None, ALU.add))
                    if m:
                        link(nc.vector.tensor_tensor(sm("ab", c), sm("ag", c), col("ln_b", ng * KT, KT), ALU.mult))
                        link(nc.vector.tensor_tensor(sm("ab", c), sm("ab", c), shift, ALU.add))
                        link(nc.vector.tensor_tensor(sm("ag", c), sm("ag", c), col("ln_g", ng * KT, KT), ALU.mult))
                    else:
                        link(nc.vector.tensor_copy(sm("ab", c), shift))
                    link(nc.vector.tensor_scalar(sm("gate", c), gate, 0.5 if r != 1 else 1.0, None, ALU.mult))

            def modulate(m, src, T):
                for k in range(KT):
                    for c in range(T // SEQ):
                        t = slice(c * SEQ, (c + 1) * SEQ)
                        last = nc.vector.tensor_scalar(TQ[:, k, t], src[:, k, t], sm("ag", c)[:, k:k + 1],
                                                       sm("ab", c)[:, k:k + 1], ALU.mult, ALU.add)
                    last.then_inc(s_modd, 1)
                for hf in range(2):
                    k = slice(4 * hf, 4 * hf + 4)
                    dve.wait_ge(s_xh, 4 * m + 2 * hf + 2)
                    nc.vector.tensor_tensor(XL[:, k, 0:T], TQ[:, k, 0:T], XH[:, k, 0:T].bitcast(F32),
                                            ALU.subtract).then_inc(s_xl, 1)

            nc.vector.memset(epsc[:], EPS)
            nc.vector.memset(ones[:], 1.0).then_inc(s_ones, 1)
            link(nc.vector.memset(SC4[:].bitcast(I32), 0))
            dve.wait_ge(s_silu, 1)
            cin = cols[:, COLS["c"]:COLS["c"] + 2 * KT]
            nc.vector.tensor_tensor(scf[:, 2 * KT:4 * KT], cin, scf[:, 0:2 * KT], ALU.mult).then_inc(s_sc4, 1)
            dve.wait_ge(s_silu, 2)
            scv = scf[:, 2 * KT:4 * KT].rearrange("p (c k) -> p c k", c=2)
            for c in range(2):
                last = nc.vector.tensor_tensor(SC4[:, :, 2 * c + 1], scv[:, c, :], SC4[:, :, 2 * c].bitcast(F32),
                                               ALU.subtract)
            last.then_inc(s_sc4, 1)
            split_low(0, 0, 2)
            split_low(0, 1, 2)
            first_mod = True
            for s in steps:
                name, T, np_ = s["name"], s["T"], len(s["panels"])
                if name == "glu" and first_mod:
                    first_mod = False
                    columns(0)
                    modulate(0, X, T1)
                if name == "cgate":
                    nc.vector.memset(UP[:, :, 0:SEQ + 2:SEQ + 1], 0.0)

                def splits(i):
                    for pi, (k0, nk) in enumerate(s["panels"]):
                        g = s["g0"] + np_ * i + pi
                        split_low(g, 2, 2)
                        split_low(g, 3, nk - 6)
                        if not is_last(s, i, pi):
                            split_low(g + 1, 0, 2)
                            split_low(g + 1, 1, 2)

                def epilogue(i):
                    G = s["G0"] + i
                    g_last = s["g0"] + np_ * (i + 1)

                    def pair_ready(p):
                        if p == 0:
                            dve.wait_ge(s_pair0, G + 1)
                        else:
                            dve.wait_ge(s_half, 2 * g_last + 2)

                    if name == "ada":
                        dve.wait_ge(s_half, 2 * g_last + 2)
                        nc.vector.tensor_copy(adarow[:], bank(G, 0).rearrange("p a n -> p (a n)")).then_inc(s_adarow, 1)
                        dve.wait_ge(s_pair0, G + 1)
                        for c in range(2):
                            ps = bank(G, 2)[:, 0, c:8:2]
                            nc.vector.tensor_tensor(mod[:, s["layer"], c, bass.ds(4 * i, 4)], ps,
                                                    col("ada_b", 9 * KT * s["layer"] + 4 * i, 4),
                                                    ALU.add).then_inc(s_free, 1)
                    elif name == "glu":
                        for p in range(2):
                            u = 2 * i + p
                            dve.wait_ge(s_act, s["act0"] + u + 1)
                            nc.vector.tensor_tensor(SG[:, p:p + 1, 0:T], SG[:, p:p + 1, 0:T],
                                                    bank(G, 2 * p)[:, :, 0:T], ALU.mult).then_inc(s_mid, 1)
                            dve.wait_ge(s_mid, s["mid0"] + u + 1)
                            dve.wait_ge(s_hl, s["hid0"] + u + 1)
                            nc.vector.tensor_tensor(GB[:, p:p + 1, 0:T], SG[:, p:p + 1, 0:T],
                                                    bank(G, 2 * p + 1)[:, :, 0:T], ALU.mult).then_inc(s_free, 1)
                    elif name == "res":
                        gate = "gate"
                        for j in range(4):
                            if j % 2 == 0:
                                pair_ready(j // 2)
                            dve.wait_ge(s_res, KT * (norms + 1)) if j == 0 else None
                            for c in range(T // SEQ):
                                t = slice(c * SEQ, (c + 1) * SEQ)
                                x = X[:, bass.ds(4 * i + j, 1), t]
                                last = nc.vector.scalar_tensor_tensor(x, bank(G, j)[:, :, t],
                                                                      smcol("gate", 4 * i + j, c), x,
                                                                      ALU.mult, ALU.add)
                            if j % 2:
                                last.then_inc(s_free, 1)
                    elif name in ("q", "k", "v"):
                        for p in range(2):
                            pair_ready(p)
                            ps = bank(G, 2 * p, 2)[:, :, 0:T]
                            tiles = bass.ds(4 * i + 2 * p, 2)
                            if name == "q":
                                nc.vector.tensor_scalar(NQ[:, tiles, :], ps, HD ** -0.5, None,
                                                        ALU.mult).then_inc(s_free, 1)
                            else:
                                nc.vector.tensor_copy((NK if name == "k" else NVT)[:, tiles, :],
                                                      ps).then_inc(s_free, 1)
                    elif name == "cgate":
                        for p in range(2):
                            u = 2 * i + p
                            f = bass.ds(u, 1)
                            dve.wait_ge(s_act, s["act0"] + u + 1)
                            nc.vector.tensor_tensor(UP[:, f, 1:SEQ + 1], SG[:, p:p + 1, 0:T],
                                                    bank(G, 2 * p + 1)[:, :, 0:T], ALU.mult).then_inc(s_free, 1)
                            dve.wait_ge(s_free, 2 * G + p + 5)
                            for tap in range(3):
                                w_tap = col("sc_w", tap * KT + u)
                                x = UP[:, f, tap:tap + SEQ]
                                if tap == 0:
                                    ins = nc.vector.tensor_scalar(CV[:, f, :], x, w_tap, None, ALU.mult)
                                else:
                                    ins = nc.vector.scalar_tensor_tensor(CV[:, f, :], x, w_tap, CV[:, f, :],
                                                                         ALU.mult, ALU.add)
                                ins.then_inc(s_mid, 1)
                                dve.wait_ge(s_mid, s["mid0"] + 6 * i + 3 * p + tap + 1)
                    elif name == "bgate":
                        for p in range(2):
                            pair_ready(p)
                            dve.wait_ge(s_hl, s["hid0"] + 2 * i + p + 1)
                            nc.vector.tensor_tensor(GB[:, p, :].rearrange("p (a t) -> p a t", a=2),
                                                    CV[:, bass.ds(4 * i + 2 * p, 2), :],
                                                    bank(G, 2 * p, 2)[:, :, 0:T], ALU.mult).then_inc(s_free, 1)
                    elif name == "store":
                        for p in range(2):
                            pair_ready(p)
                            n = 4 * i + 2 * p
                            dst = MJ[:, bass.ds(n, 2), :] if s["tile"] == 24 else MI[:, bass.ds(s["tile"] + n, 2), :]
                            nc.vector.tensor_copy(dst, bank(G, 2 * p, 2)[:, :, 0:T]).then_inc(s_free, 1)
                    elif name == "gate":
                        for p in range(2):
                            dve.wait_ge(s_act, s["act0"] + 2 * i + p + 1)
                            d = gate_room(s, 4 * i + 2 * p)
                            nc.vector.tensor_tensor(d, d, bank(G, 2 * p, 2)[:, :, 0:T], ALU.mult).then_inc(s_free, 1)
                    elif name in ("forget", "mgate"):
                        n = 2 if name == "forget" else 1
                        for p in range(2):
                            dve.wait_ge(s_act, s["act0"] + n * (2 * i + p + 1))
                            dve.sem_inc(s_free, 1)
                    elif name == "branch":
                        for p in range(2):
                            pair_ready(p)
                            f = bass.ds(4 * i + 2 * p, 2)
                            ps = bank(G, 2 * p, 2)[:, :, 0:T]
                            dst = Y if s["n"] == 0 else MG
                            nc.vector.tensor_tensor(dst[:, f, :], MG[:, f, :], ps, ALU.mult).then_inc(s_free, 1)
                            if s["n"]:
                                dve.wait_ge(s_free, 2 * G + p + 5)
                                nc.vector.tensor_tensor(Y[:, f, :], Y[:, f, :], MG[:, f, :],
                                                        ALU.add).then_inc(s_yadd, 1)
                    elif name == "add":
                        for p in range(2):
                            pair_ready(p)
                            f = bass.ds(4 * i + 2 * p, 2)
                            nc.vector.tensor_tensor(H[:, f, :], H[:, f, :], bank(G, 2 * p, 2)[:, :, 0:T],
                                                    ALU.add).then_inc(s_free, 1)
                    elif name == "conv":
                        for j in range(4):
                            ft = FT * (j % 2) + 2 * i + j // 2
                            ps = bank(G, j)
                            dve.wait_ge(s_act, s["act0"] + 6 * i + j + 1)
                            for tap in (1, 0):
                                sh = 2 - tap
                                c = CB[:, j:j + 1, sh:T2]
                                ins = nc.vector.scalar_tensor_tensor(
                                    c, ps[:, :, 0:T2 - sh], col("conv_w", (3 * s["layer"] + tap) * 2 * FT + ft), c,
                                    ALU.mult, ALU.add)
                                if tap == 1:
                                    ins.then_inc(s_mid, 1)
                                    dve.wait_ge(s_mid, s["mid0"] + 8 * i + (1, 3, 4, 6)[j])
                                else:
                                    ins.then_inc(s_mid if j % 2 == 0 else s_free, 1)
                        for p in range(2):
                            dve.wait_ge(s_act, s["act0"] + 6 * i + 5 + p)
                            nc.vector.tensor_tensor(SG2[:, p:p + 1, :], SG2[:, p:p + 1, :], CB[:, 2 * p:2 * p + 1, :],
                                                    ALU.mult).then_inc(s_mid, 1)
                            dve.wait_ge(s_mid, s["mid0"] + 8 * i + 7 + p)
                            dve.wait_ge(s_hl, s["hid0"] + 2 * i + p + 1)
                            nc.vector.tensor_tensor(SG2[:, 2 + p:3 + p, :], SG2[:, p:p + 1, :],
                                                    CB[:, 2 * p + 1:2 * p + 2, :], ALU.mult).then_inc(s_gb, 1)

                groups_behind(dve, s, splits, epilogue)
                G_end = s["G0"] + s["groups"]
                if s.get("norm"):
                    m = norms
                    dve.wait_ge(s_sum, m + 1)
                    if m < 5:
                        columns(m + 1)
                        al = ALPHA
                    else:
                        al = 1.0
                    link(nc.vector.tensor_scalar(sm("xg"), col("ln_g", m * KT, KT), al, None, ALU.mult))
                    link(nc.vector.tensor_scalar(sm("xb"), col("ln_b", m * KT, KT), al, None, ALU.mult))
                    for hf in range(2):
                        k = slice(4 * hf, 4 * hf + 4)
                        nc.vector.scalar_tensor_tensor(TC[:, k, 0:T], bc(PS[:, 0, 0:T], 4), -1.0 / D, X[:, k, 0:T],
                                                       ALU.mult, ALU.add).then_inc(s_cen, 1)
                    dve.wait_ge(s_rdev, m + 1)
                    for hf in range(2):
                        k = slice(4 * hf, 4 * hf + 4)
                        last = nc.vector.tensor_tensor(TC[:, k, 0:T], TC[:, k, 0:T], bc(RS[:, 1, 0:T], 4), ALU.mult)
                    if m < 5:
                        link(last)
                        modulate(m + 1, TC, T)
                    else:
                        last.then_inc(s_modd, 1)
                    norms += 1
                    if norms == 6:
                        rms_dve(dve, 0, "mix_g", 0)
                        rmss = 1
                if s.get("rms"):
                    rms_dve(dve, rmss, *s["rms"])
                    rmss += 1
                if name == "v":
                    na_dve(dve, link, G_end)
                if "mixer" in s:
                    (ret_dve, hg_dve, da_dve)[s["mixer"]](dve, link, s["layer"], G_end)
                if name == "branch" and s["n"] == 2:
                    for hf in range(2):
                        k = slice(4 * hf, 4 * hf + 4)
                        dve.wait_ge(s_yh, 2 * s["layer"] + hf + 1)
                        nc.vector.tensor_tensor(NHl[:, k, :], Y[:, k, :], NHh[:, k, :].bitcast(F32),
                                                ALU.subtract).then_inc(s_yl, 1)

        @block.gpsimd
        def _(pool):
            pool.sem_inc(s_hl, 1)
            pool.sem_inc(s_hl, 1)
            pool.dma_start(cols[:], cols_d).then_inc(s_tokens, 16)
            pool.dma_start(con1[:], const1_d).then_inc(s_tokens, 16)
            pool.dma_start(X[:], tokens).then_inc(s_tokens, 16)
            pool.dma_start(rpb_skew, bass.AP(rpb_d.tensor, 0, [[0, GRID_W], [RPB_W, NH * 7], [1, RPB_W]])
                           ).then_inc(s_skew_out, 16)
            first_mod = True
            for s in steps:
                if s["name"] == "glu" and first_mod:
                    first_mod = False
                    pool.wait_ge(s_tokens, 48)
                    pool.wait_ge(s_modd, KT)
                    for k in range(KT):
                        nc.gpsimd.tensor_scalar(X[:, k, :], X[:, k, :], ALPHA, None, ALU.mult).then_inc(s_res, 1)
                if s["name"] in HIDS:
                    name, T = s["name"], s["T"]
                    for i in groups_of(pool, s):
                        for p in range(2):
                            u = 2 * i + p
                            pool.wait_ge(s_hh, s["hid0"] + u + 1)
                            if name == "glu":
                                f = bass.ds(u, 1)
                                out, x, h = GL[:, f, 0:T], GB[:, p:p + 1, 0:T], GH[:, f, 0:T]
                            elif name == "bgate":
                                f = bass.ds(2 * u, 2)
                                out, h = GL[:, f, 0:T], GH[:, f, 0:T]
                                x = GB[:, p, :].rearrange("p (a t) -> p a t", a=2)
                            else:
                                f = bass.ds(u, 1)
                                out, x, h = G2L[:, f, :], SG2[:, 2 + p:3 + p, :], G2H[:, f, :]
                            nc.gpsimd.tensor_tensor(out, x, h.bitcast(F32), ALU.subtract).then_inc(s_hl, 1)
                G_end = s["G0"] + s["groups"]
                if s["name"] == "res" and s["layer"] == 0 and s["r"] == 0:
                    pool.wait_ge(s_free, 2 * G_end + 4)
                    pool.wait_ge(s_xl, 4)
                    pool.wait_ge(s_skew_out, 16)
                    for rp in range(2):
                        for j in range(6):
                            src = bass.AP(rpb_skew.tensor, (1 - rp + j) * RPB_W + GRID_W - 1,
                                          [[NH * 7 * RPB_W - 1, GRID_W], [7 * RPB_W, NH], [1, GRID_W]])
                            pool.dma_start(TB[64 * rp:64 * rp + 64, :, j, :], src).then_inc(s_bias, 16)
                if s["name"] == "v":
                    na_pool(pool)
                if s["name"] == "res" and s["layer"] == 1 and s["r"] == 2:
                    pool.wait_ge(s_free, 2 * G_end + 4)
                    pool.dma_start(H[:, :, 0:N_META], meta).then_inc(s_meta, 16)
                    pool.dma_start(con2[:], const2_d).then_inc(s_meta, 16)
                if s.get("mixer") == 1:
                    hg_pool(pool, s["layer"], G_end)


_WEIGHTS = ["ada_w", "ffn_w_in", "ffn_w_out", "na_w_qkv", "na_w_out", "sc_w_in", "sc_w_out", "w_in_2",
            "w_branch_2", "w_out_2", "w_ffn_in_2", "w_ffn_out_2"]


def kernel(**inputs):
    import concourse.bacc as bacc
    from concourse.bass_utils import run_bass_kernel_spmd

    a = {k: np.asarray(v) for k, v in inputs.items()}

    def columns(x):
        return np.ascontiguousarray(x).reshape(-1, P).T

    def rows(x):
        return np.ascontiguousarray(x.T.reshape(KT, P, -1).transpose(1, 0, 2))

    lam = np.zeros((P, DEPTH * 4), np.float32)
    lam[0:64] = a["da_lambda_2"][:, [0, 1, 2, 3]].reshape(DEPTH * 4, 64).T
    cols = np.concatenate([
        columns(a["c"]), columns(a["c_ctx"]), columns(a["ada_b"]), columns(a["ln_g"]), columns(a["ln_b"]),
        columns(a["norm_mix_g_2"]), columns(a["norm_ffn_g_2"]), columns(a["norm_final_g_2"]),
        columns(a["sc_conv"]), columns(a["ffn_conv_w_2"]), columns(a["ffn_conv_b_2"]), columns(a["hg_lb_2"]),
        columns(a["da_subln_g_2"]), lam], axis=1)
    rpb = np.zeros((NH, 7, RPB_W), np.float32)
    rpb[:, :, 48:48 + 31] = a["na_rpb"][0][:, 4:11]
    arrays = {name: np.ascontiguousarray(a[name]) for name in _WEIGHTS}
    arrays |= {"tokens": rows(np.concatenate([a["x"][0], a["ctx"][0]])), "meta": rows(a["meta_2"]),
               "cols": np.ascontiguousarray(cols), "const1": first_constants(), "const2": second_constants(),
               "rpb": rpb}
    nc = bacc.Bacc("TRN2", target_bir_lowering=False, num_devices=1)
    ap = {k: nc.dram_tensor(k + "_dram", v.shape, F32, kind="ExternalInput").ap() for k, v in arrays.items()}
    skew = nc.dram_tensor("rpb_skew", (GRID_W, NH * 7, RPB_W), F32, kind="Internal").ap()
    out = nc.dram_tensor("out_dram", (P, KT, SEQ), F32, kind="ExternalOutput").ap()
    two_block_kernel(nc, {k: ap[k] for k in _WEIGHTS}, ap["tokens"], ap["meta"], ap["cols"], ap["const1"],
                     ap["const2"], ap["rpb"], skew, out)
    r = run_bass_kernel_spmd(nc, [{k + "_dram": v for k, v in arrays.items()}], core_ids=[0])
    got = r.results[0]["out_dram"]
    return np.ascontiguousarray(got.transpose(2, 1, 0).reshape(1, SEQ, D))
```

```python
from contextlib import ExitStack
import math

import numpy as np

import concourse.bass as bass
from concourse import mybir

F32 = mybir.dt.float32
F32R = mybir.dt.float32r
I32 = mybir.dt.int32
ALU = mybir.AluOpType
ACT = mybir.ActivationFunctionType
AX = mybir.AxisListType

P = 128
D = 1024
KT = D // P
F = 2816
FT = F // P
SEQ = 256
CTX = 256
N_META = 16
T1 = SEQ + CTX
T2 = N_META + SEQ
DEPTH = 2
PW = 512
NH, HD = 16, 64
GRID_W, GRID_H = 64, SEQ // 64
RH = 4
HH = 8
DH = 8
ALPHA = (2.0 * DEPTH) ** 0.25
EPS = 1e-6
IN_W = 13312
TURN = 6
CHUNKS = ((0, 128), (128, 128), (256, 16))
LEVELS = (1, 2, 4, 8, 16, 32, 64)
NEG = -1e30

COLS = {}
_at = 0
for _name, _n in (("c", 2 * KT), ("ada_b", DEPTH * 9 * KT), ("ln_g", DEPTH * 3 * KT), ("ln_b", DEPTH * 3 * KT),
                  ("mix_g", DEPTH * KT), ("ffn_g", DEPTH * KT), ("final_g", KT), ("sc_w", 3 * KT),
                  ("conv_w", DEPTH * 3 * 2 * FT), ("conv_b", DEPTH * 2 * FT), ("hg_lb", DEPTH * KT),
                  ("subln", DEPTH), ("lam", DEPTH * 4)):
    COLS[_name] = _at
    _at += _n
NCOL = _at

C1 = {"ident": 0, "rot": 128, "cos": 256, "sin": 512, "colmask": 768}
NC1 = 832
C2 = {"rot_r": 0, "rot_d": 128, "cos_r": 256, "sin_r": 528, "cos_d": 800, "sin_d": 1072,
      "gap": 1344, "dmask": 2160, "reset": 2976, "levels": 3248}
NC2 = 3248 + 8 * 128


def rotation(half, width):
    r = np.zeros((P, P), np.float32)
    for base in range(0, P, width):
        for d in range(half):
            r[base + half + d, base + d] = -1.0
            r[base + d, base + half + d] = 1.0
    return r


def first_constants():
    out = np.zeros((P, NC1), np.float32)
    out[:, 0:128] = np.eye(P)
    out[:, C1["rot"]:C1["rot"] + P] = rotation(HD // 4, HD // 2)
    t = np.arange(SEQ)
    inv = 10000.0 ** (-np.arange(HD // 4) / (HD // 4))
    for p in range(P):
        d = p % HD
        pos = (t // GRID_W) if d < HD // 2 else (t % GRID_W)
        ang = pos * inv[d % (HD // 4)]
        out[p, C1["cos"]:C1["cos"] + SEQ] = np.cos(ang)
        out[p, C1["sin"]:C1["sin"] + SEQ] = np.sin(ang)
    for p in range(P):
        start = min(max(p % GRID_W - 8, 0), GRID_W - 16)
        row = np.full(GRID_W, NEG, np.float32)
        row[start:start + 16] = 0.0
        out[p, C1["colmask"]:] = row
    return out


def second_constants():
    out = np.zeros((P, NC2), np.float32)
    out[:, 0:P] = rotation(64, 128)
    out[:, P:2 * P] = rotation(32, 64)
    pos = np.arange(T2, dtype=np.float32)
    for key, dim in (("_r", 128), ("_d", 64)):
        inv = (np.float32(10000.0) ** (-np.arange(0, dim, 2, dtype=np.float32) / np.float32(dim))).astype(np.float32)
        ang = inv[np.arange(P) % (dim // 2)][:, None] * pos[None, :]
        out[:, C2["cos" + key]:C2["cos" + key] + T2] = np.cos(ang)
        out[:, C2["sin" + key]:C2["sin" + key] + T2] = np.sin(ang)
    for n, (t0, w) in enumerate(CHUNKS):
        k = t0 + np.arange(w)
        gap = pos[None, :] - k[:, None]
        out[:w, C2["gap"] + n * T2:C2["gap"] + (n + 1) * T2] = np.where(gap >= 0, gap, 1e6)
        out[:w, C2["dmask"] + n * T2:C2["dmask"] + (n + 1) * T2] = np.where(-gap >= 0, 0.0, NEG)
    reset = np.ones(T2, np.float32)
    reset[[t0 for t0, _ in CHUNKS]] = 0.0
    out[:, C2["reset"]:C2["reset"] + T2] = reset
    i = np.arange(P)
    masks = [i[:, None] == i[None, :]]
    for s in LEVELS:
        same = (i[:, None] // (2 * s)) == (i[None, :] // (2 * s))
        masks.append(same & (i[:, None] % (2 * s) < s) & (i[None, :] % (2 * s) >= s))
    for n, m in enumerate(masks):
        out[:, C2["levels"] + n * P:C2["levels"] + (n + 1) * P] = m
    return out


def gemm_steps(w):
    steps = []

    def add(name, groups, src, layer=0, t0=0, T=SEQ, panels=((0, 8),), halves=False, unroll=False):
        steps.append(dict(name=name, groups=groups, src=src, layer=layer, t0=t0, T=T, panels=panels,
                          halves=halves, unroll=unroll))

    def plain(ap, col0=0):
        v = ap.rearrange("(k p) n -> p k n", p=P)

        def src(i, k0, nk):
            if nk == 2:
                return [v[:, k0 + x, bass.ds(col0 + PW * i, PW)] for x in range(2)]
            return [v[:, k0, bass.ds(col0 + PW * i + x * PW // 2, PW // 2)] for x in range(2)]
        return src

    def paired(ap, first, second):
        v = ap.rearrange("(k p) n -> p k n", p=P)

        def src(i, k0, nk):
            return [v[:, k0:k0 + nk, bass.ds(at + 256 * i, 256)] for at in (first, second)]
        return src

    deep = ((0, 7), (7, 7), (14, 8))
    for layer in range(DEPTH):
        add("ada", 9 * D // PW, plain(w["ada_w"][layer]), layer)
    for layer in range(DEPTH):
        for r in range(3):
            T = T1 if (layer, r) == (0, 0) else SEQ
            if r != 1:
                half = 0 if r == 0 else 1
                add("glu", FT // 2, paired(w["ffn_w_in"][layer, half], 0, F), layer, T=T, halves=True)
                add("res", 2, plain(w["ffn_w_out"][layer, half]), layer, T=T, panels=deep)
                steps[-1]["r"] = r
            elif layer == 0:
                add("q", 2, plain(w["na_w_qkv"][0], 0), layer)
                add("k", 2, plain(w["na_w_qkv"][0], D), layer, T=T1)
                add("v", 2, plain(w["na_w_qkv"][0], 2 * D), layer, T=T1)
                add("res", 2, plain(w["na_w_out"][0]), layer)
                steps[-1]["r"] = r
            else:
                add("cgate", 4, paired(w["sc_w_in"][0], D, 2 * D), layer, halves=True)
                add("bgate", 2, plain(w["sc_w_in"][0], 0), layer)
                add("res", 2, plain(w["sc_w_out"][0]), layer)
                steps[-1]["r"] = r
            steps[-1]["norm"] = True
    for layer in range(DEPTH):
        w_in = w["w_in_2"][layer]
        for n, kinds in enumerate(((("store", 4, 0, 0), ("gate", 2, 2048, 16)),
                                   (("store", 2, 3072, 0), ("forget", 2, 4096, 8), ("store", 2, 5120, 24),
                                    ("gate", 2, 6144, 32)),
                                   (("store", 6, 7168, 0),))):
            for kind, groups, col, tile in kinds:
                add(kind, groups, plain(w_in, col), layer, T=T2)
                steps[-1]["tile"] = tile
                steps[-1]["after_rms"] = col == 0
            steps[-1]["mixer"] = n
            add("mgate", 2, plain(w_in, 10240 + n * D), layer, T=T2)
            add("branch", 2, plain(w["w_branch_2"][layer, n]), layer, T=T2)
            steps[-1]["n"] = n
        add("add", 2, plain(w["w_out_2"][layer]), layer, T=T2)
        steps[-1]["rms"] = ("ffn_g", layer)
        add("conv", FT // 2, paired(w["w_ffn_in_2"][layer], 0, F), layer, T=T2, halves=True)
        steps[-1]["after_rms"] = True
        add("add", 2, plain(w["w_ffn_out_2"][layer]), layer, T=T2, panels=deep, unroll=(layer == DEPTH - 1))
        steps[-1]["rms"] = ("mix_g", layer + 1) if layer + 1 < DEPTH else ("final_g", 0)
    g = G = 0
    for s in steps:
        s["g0"], s["G0"] = g, G
        g += s["groups"] * len(s["panels"])
        G += s["groups"] // TURN if s["name"] == "ada" else s["groups"]
    steps[-1]["last"] = True
    return steps


RPB_W = 128


def two_block_kernel(nc, w, tokens, meta, cols_d, const1_d, const2_d, rpb_d, rpb_skew, out_d):
    steps = gemm_steps(w)
    ctx = ExitStack()
    with ctx:
        def sem(name):
            return ctx.enter_context(nc.semaphore(name))

        base = 16512
        arena = nc.sbuf_usable_end - 64

        class Region:
            def __init__(self, at):
                self.at = at

            def take(self, name, shape, dt=F32):
                off = (self.at + 31) // 32 * 32
                size = 4 * int(np.prod(shape[1:]))
                self.at = off + size
                assert self.at <= arena, (name, self.at, arena)
                return nc.alloc_sbuf_tensor_at(name, shape, dt, offset=off)

        R = Region(base)
        raw = R.take("raw", [P, 4, 2, PW])
        high = R.take("high", [P, 4, 2, PW], F32R)
        low = R.take("low", [P, 4, 2, PW], F32R)
        x_at = R.at
        X = R.take("X", [P, KT, T1])
        cols = R.take("cols", [P, NCOL])
        con1 = R.take("con1", [P, NC1])
        ones = R.take("ones", [P, P])
        mod = R.take("mod", [P, DEPTH, 2, 9 * KT])
        small = R.take("small", [P, 40 * KT])
        RS = R.take("RS", [P, 2, T1])
        epsc = R.take("epsc", [P, 2])
        dst = R.take("dst", [P, 4, 4])
        common_end = R.at

        A = Region(common_end)
        XH = A.take("XH", [P, KT, T1], F32R)
        XL = A.take("XL", [P, KT, T1], F32R)
        inner = A.at
        GH = A.take("GH", [P, FT, T1], F32R)
        GL = A.take("GL", [P, FT, T1], F32R)
        A2 = Region(inner)
        TC = A2.take("TC", [P, KT, T1])
        TQ = A2.take("TQ", [P, KT, T1])
        E1 = Region(A.at)
        SG = E1.take("SG", [P, 2, T1])
        GB = E1.take("GB", [P, 2, T1])
        e1_end = E1.at
        A3 = Region(inner)
        ADA = 9 * D // PW
        SC0 = 4 * (TURN - 1)
        SC4 = A3.take("SC4", [P, KT, SC0 + P], F32R)
        adarow = A3.take("adarow", [P, PW])
        scf = A3.take("scf", [P, 4 * 2 * KT])
        raw_odd = A3.take("raw_odd", [P, 4, 2, PW])
        A4 = Region(inner)
        NQ = A4.take("NQ", [P, KT, SEQ])
        NK = A4.take("NK", [P, KT, T1])
        NV = A4.take("NV", [P, 4, D])
        NVT = A4.take("NVT", [P, KT, T1])
        TB = A4.take("TB", [P, NH, 6, GRID_W])
        NT = Region(A4.at - 4 * NH * 6 * GRID_W - 4 * KT * T1)
        SB = NT.take("SB", [P, 4, T1])
        PT = NT.take("PT", [P, 2, T1])
        ROT = A4.take("ROT", [P, 2, SEQ])
        nst = A4.take("nst", [P, 4, 4])
        A5 = Region(inner + 2 * 4 * FT * T1 // 2)
        UP = A5.take("UP", [P, KT, SEQ + 2])
        CV = A5.take("CV", [P, KT, SEQ])
        A5.at = max(A5.at, e1_end)

        con2 = Region(arena // 32 * 32 - 4 * NC2 - 32).take("con2", [P, NC2])
        B = Region(common_end)
        H = B.take("H", [P, KT, T2])
        NHh = B.take("NHh", [P, KT, T2], F32R)
        nhl_at = B.at
        NHl = B.take("NHl", [P, KT, T2], F32R)
        SQ = Region(nhl_at).take("SQ", [P, KT, T2])
        b_inner = B.at
        Y = B.take("Y", [P, KT, T2])
        oh_at = B.at
        OH = B.take("OH", [P, KT, T2], F32R)
        ol_at = B.at
        OL = B.take("OL", [P, KT, T2], F32R)
        VT = B.take("VT", [P, 3, D])
        sx_at = B.at
        SX = B.take("SX", [P, 2, 2, T2])
        SY = B.take("SY", [P, 2, 2, T2])
        MI = B.take("MI", [P, 24, T2])
        MJ = B.take("MJ", [P, 8, T2])
        MG = B.take("MG", [P, 8, T2])
        assert B.at <= arena - 4 * NC2 - 96
        QB = Region(oh_at).take("QB", [P, KT, T2])
        QB1 = Region(x_at).take("QB1", [P, KT, T2])
        DEC = Region(x_at).take("DEC", [P, 3 * RH, T2])
        EX = Region(sx_at).take("EX", [P, KT, T2])
        AM = Region(ol_at).take("AM", [P, KT, T2])
        B2 = Region(b_inner)
        G2H = B2.take("G2H", [P, FT, T2], F32R)
        G2L = B2.take("G2L", [P, FT, T2], F32R)
        CB = B2.take("CB", [P, 4, T2])
        SG2 = B2.take("SG2", [P, 4, T2])
        assert B2.at <= arena - 4 * NC2 - 96
        TN = Region(b_inner).take("TN", [P, KT, T2])

        PS = ctx.enter_context(nc.psum_tensor("PS", [P, 8, PW], F32))

        s_tokens = sem("tokens_loaded")
        s_out = sem("output_written")
        s_skew_out = sem("bias_skew_written")
        s_bias = sem("bias_loaded")
        s_ones = sem("ones_set")
        s_raw = [sem(f"raw_quarter{q}_loaded") for q in range(4)]
        s_raw_odd = [sem(f"raw_odd_quarter{q}_loaded") for q in range(4)]
        s_high = sem("high_quarters")
        s_low = sem("low_quarters")
        s_half = sem("panel_halves_multiplied")
        s_pair0 = sem("first_pair_multiplied")
        s_free = sem("pairs_evacuated")
        s_act = sem("act_epilogue")
        s_mid = sem("dve_epilogue_steps")
        s_gb = sem("conv_hidden_ready")
        s_hh = sem("hidden_high")
        s_hl = sem("hidden_low")
        s_adarow = sem("ada_row_ready")
        s_adacol = sem("ada_columns_ready")
        s_silu = sem("silu_c_steps")
        s_sc4 = sem("silu_c_ready")
        s_sum = sem("row_sums")
        s_cen = sem("centred_halves")
        s_sq = sem("squared_halves")
        s_var = sem("square_sums")
        s_ln = sem("log_taken")
        s_rdev = sem("rdev_ready")
        s_modd = sem("modulated_tiles")
        s_xh = sem("x_high_pairs")
        s_xl = sem("x_low_halves")
        s_res = sem("residual_ready")
        s_chain = sem("dve_chain")

        ACTS = {"glu": 2, "cgate": 2, "gate": 2, "forget": 4, "mgate": 2, "conv": 6}
        MIDS = {"glu": 2, "cgate": 6, "conv": 8}
        HIDS = {"glu": 2, "bgate": 2, "conv": 2}
        act = mid = hid = gb = yad = 0
        for s in steps:
            s["act0"], s["mid0"], s["hid0"], s["gb0"], s["yad0"] = act, mid, hid, gb, yad
            act += ACTS.get(s["name"], 0) * s["groups"]
            mid += MIDS.get(s["name"], 0) * s["groups"]
            hid += HIDS.get(s["name"], 0) * s["groups"]
            gb += (2 if s["name"] == "conv" else 0) * s["groups"]
            yad += 2 * s["groups"] if s["name"] == "branch" and s["n"] else 0

        COLOF = {False: (0, 128, 256, 384), True: (0, 256, 128, 384)}

        def groups_of(eng, s):
            if s["unroll"] or s["groups"] == 2:
                yield from range(s["groups"])
            else:
                with eng.Fori(0, s["groups"]) as i:
                    yield i

        def raw_of(g, odd):
            if odd is None:
                return raw, s_raw, 32 * (g + 1 - DEPTH * ADA // 2)
            return ((raw_odd, s_raw_odd) if odd else (raw, s_raw)) + (16 * (g - odd) + 32,)

        def groups_behind(eng, s, body, epilogue, between=None):
            body(0)
            if between:
                between()
            if s["unroll"] or s["groups"] == 2:
                for i in range(1, s["groups"]):
                    body(i)
                    epilogue(i - 1)
            else:
                with eng.Fori(1, s["groups"]) as i:
                    body(i)
                    epilogue(i - 1)
            epilogue(s["groups"] - 1)

        def is_last(s, i, pi):
            return bool(s.get("last")) and s["unroll"] and i == s["groups"] - 1 and pi == len(s["panels"]) - 1

        def col(name, n=0, w=1):
            return cols[:, bass.ds(COLS[name] + n, w)]

        def flat(ap):
            return ap.rearrange("p a t -> p (a t)")

        def bc(ap, n):
            return bass.AP(ap.tensor, ap.offset, [ap.ap[0], [0, n], *ap.ap[1:]])

        def sm(name, c=0):
            names = ("ag", "ag_", "gate", "gate_", "xg", "xb", "ab", "ab_", "lbm0", "lbm1", "olb0", "olb1",
                     "sub", "lam", "t0", "t1", "t2", "t3")
            at = names.index(name + "_" * c) * KT
            return small[:, at:at + KT]

        def smcol(name, n, c=0, w=1):
            names = ("ag", "ag_", "gate", "gate_", "xg", "xb", "ab", "ab_", "lbm0", "lbm1", "olb0", "olb1",
                     "sub", "lam", "t0", "t1", "t2", "t3")
            return small[:, bass.ds(names.index(name + "_" * c) * KT + n, w)]

        def norm_bank(G_end):
            return 4 * (G_end % 2)

        def bank(G, j, n=1):
            return PS[:, bass.ds((G % 2) * 4 + j, n), :]

        def ones_sum(dst, src, n):
            for k in range(n):
                last = nc.tensor.matmul(dst, ones[:], src[:, k, :], start=(k == 0), stop=(k == n - 1))
            return last

        def gate_room(s, n):
            if s["name"] == "gate" and s["tile"] == 16:
                return MI[:, bass.ds(16 + n, 2), :]
            return MG[:, bass.ds(n, 2), :]

        s_nvt = sem("na_values_transposed")
        s_nvc = sem("na_values_copied")
        s_nrot = sem("na_rotated")
        s_nrc = sem("na_rope_cosine_parts")
        s_nr1 = sem("na_sin_part")
        s_nr2 = sem("na_roped")
        s_ns = sem("na_scores")
        s_na = sem("na_biased")
        s_nm = sem("na_max")
        s_ne = sem("na_exp")
        s_nr = sem("na_sum_inverse")
        s_nw = sem("na_probs")
        s_nt = sem("na_probs_transposed")
        s_nc = sem("na_probs_copied")
        s_no = sem("na_heads_out")
        s_no_high = sem("na_out_high")
        s_no_low = sem("na_out_low")
        s_vt = sem("values_transposed")
        s_vc = sem("values_copied")
        s_rot = sem("rotated")
        s_rope1 = sem("sin_part")
        s_rope2 = sem("roped")
        s_dec = sem("decay_ready")
        s_ropec = sem("rope_cosine_parts")
        s_rs = sem("ret_scores")
        s_rd = sem("ret_scores_decayed")
        s_lamp = sem("lambda_products")
        s_lams = sem("lambda_sums")
        s_lame = sem("lambda_exps")
        s_ds = sem("da_scores")
        s_dm = sem("da_masked")
        s_dx = sem("da_max")
        s_de = sem("da_exp")
        s_dw = sem("da_weights")
        s_dt = sem("da_weights_transposed")
        s_dp = sem("da_values_summed")
        s_dc = sem("da_weights_copied")
        s_hd = sem("hg_dve")
        s_ha = sem("hg_act")
        s_hp = sem("hg_pool")
        s_ht = sem("hg_pe")
        s_lb = sem("hg_bound_logits")
        s_lbe = sem("hg_bound_exps")
        s_hf = sem("hg_forget_pairs")
        s_hr = sem("hg_right_exponents")
        s_hq = sem("hg_operands")
        s_hk = sem("hg_scores_picked")
        s_o = sem("head_out")
        s_osq = sem("head_squared")
        s_oms = sem("head_square_sum")
        s_oln = sem("head_log")
        s_ord = sem("head_rdev")
        s_ot = sem("head_gated")
        s_oth = sem("head_high")
        s_tail_low = sem("head_low")
        s_yadd = sem("y_added")
        s_yh = sem("y_high")
        s_yl = sem("y_low")
        s_rsq = sem("rms_squares")
        s_rsum = sem("rms_sums")
        s_rln = sem("rms_log")
        s_rrd = sem("rms_rdev")
        s_modd_final = sem("rms_scaled_final")
        s_rmod = sem("rms_scaled")
        s_rxh = sem("rms_high_pairs")
        s_rxl = sem("rms_low_halves")
        s_meta = sem("meta_loaded")

        ident = con1[:, 0:P]

        def tail_first(layer, n):
            return layer * 16 + (0, 4, 8)[n]

        def tail_count(layer, n):
            return layer * 16 + (4, 8, 16)[n]

        def cc(name, w=T2, at=0):
            return con2[:, C2[name] + at:C2[name] + at + w]

        def out_bank(n, h):
            return (2, 4, 0)[h % 3] if n == 0 else 5 + h % 2

        def tail_act_square(act, n, hh, h):
            ne = 2 if n == 0 else 1
            act.wait_ge(s_o, hh + 1)
            if hh >= 2:
                act.wait_ge(s_oms, hh - 1)
            b = out_bank(n, h)
            nc.scalar.activation(SX[:, hh % 2, 0:ne, :], PS[:, b:b + ne, 0:T2], ACT.Square).then_inc(s_osq, 1)

        def tail_pe(pe, n, hh, h):
            ne = 2 if n == 0 else 1
            pe.wait_ge(s_osq, hh + 1)
            if hh >= 1:
                pe.wait_ge(s_oln, hh)
            ones_sum(PS[:, 7, 0:T2], SX[:, hh % 2], ne).then_inc(s_oms, 1)

        def tail_act_rdev(act, n, hh, h):
            act.wait_ge(s_oms, hh + 1)
            if hh >= 2:
                act.wait_ge(s_ot, hh - 1)
            rs = RS[:, hh % 2, 0:T2]
            nc.scalar.activation(rs, PS[:, 7, 0:T2], ACT.Ln, bias=epsc[:, 0:1],
                                 scale=1.0 / (256 if n == 0 else 128)).then_inc(s_oln, 1)
            act.wait_ge(s_oln, hh + 1)
            nc.scalar.activation(rs, rs, ACT.Exp, scale=-0.5).then_inc(s_ord, 1)

        def tail_act_high(act, n, hh, h):
            ne = 2 if n == 0 else 1
            act.wait_ge(s_ot, hh + 1)
            nc.scalar.copy(OH[:, h * ne:(h + 1) * ne, :], SY[:, hh % 2, 0:ne, :]).then_inc(s_oth, 1)

        def tail_dve_gate(dve, link, n, hh, h):
            ne = 2 if n == 0 else 1
            b = out_bank(n, h)
            dve.wait_ge(s_ord, hh + 1)
            if h >= 2:
                dve.wait_ge(s_tail_low, hh - 1)
            rs, sy = RS[:, hh % 2, 0:T2], SY[:, hh % 2, 0:ne, :]
            if n == 2:
                nc.vector.scalar_tensor_tensor(sy[:, 0, :], PS[:, b, 0:T2], sm("sub")[:, 0:1], rs,
                                               ALU.mult, ALU.mult).then_inc(s_ot, 1)
            else:
                link(nc.vector.tensor_tensor(sy, PS[:, b:b + ne, 0:T2], bc(rs, ne), ALU.mult))
                gate = MI[:, 16 + 2 * h:18 + 2 * h, :] if n == 0 else MG[:, h:h + 1, :]
                nc.vector.tensor_tensor(sy, sy, gate, ALU.mult).then_inc(s_ot, 1)

        def tail_dve_low(dve, n, hh, h):
            ne = 2 if n == 0 else 1
            sy = SY[:, hh % 2, 0:ne, :]
            dve.wait_ge(s_oth, hh + 1)
            t = slice(h * ne, (h + 1) * ne)
            nc.vector.tensor_tensor(OL[:, t, :], sy, OH[:, t, :].bitcast(F32), ALU.subtract).then_inc(s_tail_low, 1)

        def values_pe(pe, src, m):
            for n, (t0, wd) in enumerate(CHUNKS):
                for f in range(KT):
                    last = nc.tensor.transpose(PS[0:wd, 2 * n + f // 4, (f % 4) * P:(f % 4 + 1) * P],
                                               src[:, f, t0:t0 + wd], ident)
                last.then_inc(s_vt, 1)

        def values_act(act, m):
            for n, (t0, wd) in enumerate(CHUNKS):
                act.wait_ge(s_vt, 3 * m + n + 1)
                nc.scalar.copy(VT[0:wd, n, :].rearrange("p (a t) -> p a t", a=2),
                               PS[0:wd, 2 * n:2 * n + 2, :]).then_inc(s_vc, 1)

        def rope_pe(pe, rot, first, n):
            for u in range(n):
                if first + u >= 2:
                    pe.wait_ge(s_rope1, first + u - 1)
                nc.tensor.matmul(PS[:, 6 + u % 2, 0:T2], rot, MI[:, u, :], start=True, stop=True).then_inc(s_rot, 1)

        def rope_dve(dve, sin, first, n):
            for u in range(n):
                dve.wait_ge(s_rot, first + u + 1)
                if u >= 2:
                    dve.wait_ge(s_rope2, first + u - 1)
                nc.vector.tensor_tensor(SX[:, u % 2, 0, :], PS[:, 6 + u % 2, 0:T2], sin,
                                        ALU.mult).then_inc(s_rope1, 1)
                if u:
                    rope_add(dve, first, u - 1)
            rope_add(dve, first, n - 1)

        def rope_add(dve, first, u):
            dve.wait_ge(s_rope1, first + u + 1)
            dve.wait_ge(s_ropec, first + u + 1)
            nc.vector.tensor_tensor(MI[:, u, :], MI[:, u, :], SX[:, u % 2, 0, :], ALU.add).then_inc(s_rope2, 1)

        def rope_pool(pool, cos, first, n):
            for u in range(n):
                pool.wait_ge(s_rot, first + u + 1)
                nc.gpsimd.tensor_tensor(MI[:, u, :], MI[:, u, :], cos, ALU.mult).then_inc(s_ropec, 1)

        def ret_pe(pe, layer, G_end):
            pe.wait_ge(s_free, 2 * G_end + 4)
            u0, hh0 = 3 * RH * layer, tail_first(layer, 0)
            values_pe(pe, MI[:, 8:16, :], 3 * layer)
            rope_pe(pe, cc("rot_r", P), 24 * layer, 8)
            pe.wait_ge(s_rope2, 24 * layer + 8)
            pe.wait_ge(s_vc, 3 * (3 * layer + 1))

            for u in range(3 * RH):
                h, n = divmod(u, 3)
                t0, wd = CHUNKS[n]
                if u >= 4:
                    pe.wait_ge(s_rd, u0 + u - 3)
                nc.tensor.matmul(PS[0:wd, ret_bank(u), 0:T2 - t0], MI[:, 4 + h, t0:t0 + wd], MI[:, h, t0:T2],
                                 start=True, stop=True).then_inc(s_rs, 1)
            for h in range(RH):
                pe.wait_ge(s_rd, u0 + 3 * (h if h < 2 else RH - 1) + 3)
                if h >= 3:
                    pe.wait_ge(s_ot, hh0 + h - 2)
                for e in range(2):
                    for n, (t0, wd) in enumerate(CHUNKS):
                        last = nc.tensor.matmul(PS[:, out_bank(0, h) + e, t0:T2],
                                                VT[0:wd, n, h * 256 + e * P:h * 256 + (e + 1) * P],
                                                ret_scores(h, n)[0:wd, t0:T2], start=(n == 0), stop=(n == 2))
                last.then_inc(s_o, 1)
                if h:
                    if h == 1:
                        pe.wait_ge(s_rd, u0 + 3 * RH)
                    tail_pe(pe, 0, hh0 + h - 1, h - 1)
            tail_pe(pe, 0, hh0 + RH - 1, RH - 1)

        def ret_bank(u):
            return (0, 1, 6, 7)[u % 4]

        def ret_scores(h, n):
            return (MJ if h < 2 else MG)[:, 3 * (h % 2) + n, :]

        def ret_act(act, layer, G_end):
            hh0 = tail_first(layer, 0)
            values_act(act, 3 * layer)
            for h in range(RH + 2):
                if h < RH:
                    tail_act_square(act, 0, hh0 + h, h)
                if h >= 2:
                    tail_act_high(act, 0, hh0 + h - 2, h - 2)
                if 1 <= h <= RH:
                    tail_act_rdev(act, 0, hh0 + h - 1, h - 1)

        def ret_decays(act, layer):
            for h in range(RH):
                nc.scalar.activation(DEC[:, 3 * h:3 * h + 3, :],
                                     cc("gap", 3 * T2).rearrange("p (n t) -> p n t", n=3), ACT.Exp,
                                     scale=math.log1p(-2.0 ** (-5.0 - h))).then_inc(s_dec, 1)

        def ret_dve(dve, link, layer, G_end):
            u0, hh0 = 3 * RH * layer, tail_first(layer, 0)
            rope_dve(dve, cc("sin_r"), 24 * layer, 8)
            dve.wait_ge(s_dec, RH * (layer + 1))
            for h in range(RH):
                for n, (t0, wd) in enumerate(CHUNKS):
                    dve.wait_ge(s_rs, u0 + 3 * h + n + 1)
                    nc.vector.scalar_tensor_tensor(ret_scores(h, n)[0:wd, t0:T2],
                                                   PS[0:wd, ret_bank(3 * h + n), 0:T2 - t0], P ** -0.5,
                                                   DEC[0:wd, 3 * h + n, t0:T2],
                                                   ALU.mult, ALU.mult).then_inc(s_rd, 1)
            for h in range(RH + 1):
                if h < RH:
                    tail_dve_gate(dve, link, 0, hh0 + h, h)
                if h:
                    tail_dve_low(dve, 0, hh0 + h - 1, h - 1)

        DU = 3 * DH

        def da_pe(pe, layer, G_end):
            pe.wait_ge(s_free, 2 * G_end + 4)
            u0, hh0 = DU * layer, tail_first(layer, 2)
            pe.wait_ge(s_lamp, layer + 1)
            values_pe(pe, MI[:, 16:24, :], 3 * layer + 2)
            nc.tensor.matmul(PS[:, 6, 0:2], ones[:], sm("t0")[:, 0:2], start=True, stop=True).then_inc(s_lams, 1)
            pe.wait_ge(s_lame, layer + 1)
            rope_pe(pe, cc("rot_d", P), 24 * layer + 8, 16)
            pe.wait_ge(s_rope2, 24 * layer + 24)
            pe.wait_ge(s_vc, 3 * (3 * layer + 3))
            for t in range(DU + 7):
                if t < DU:
                    h, n = divmod(t, 3)
                    t0, wd = CHUNKS[n]
                    if t >= 2:
                        pe.wait_ge(s_dm, u0 + t - 1)
                    for m in range(2):
                        r = slice(64 * m, 64 * m + 64)
                        last = nc.tensor.matmul(PS[0:wd, 2 * (t % 2) + m, 0:t0 + wd], MI[r, h, t0:t0 + wd],
                                                MI[r, 8 + h, 0:t0 + wd], start=True, stop=True)
                    last.then_inc(s_ds, 1)
                if 6 <= t < DU + 6:
                    u = t - 6
                    h, n = divmod(u, 3)
                    t0, wd = CHUNKS[n]
                    pe.wait_ge(s_dc, u0 + u + 1)
                    if n == 0 and h >= 2:
                        pe.wait_ge(s_ot, hh0 + h - 1)
                    for c in range(n + 1):
                        k0, kw = CHUNKS[c]
                        last = nc.tensor.matmul(PS[:, out_bank(2, h), t0:t0 + wd], VT[0:kw, c, h * P:(h + 1) * P],
                                                flat(MG[0:kw, 2 + 2 * (u % 2):4 + 2 * (u % 2), :])[:, c * P:c * P + wd],
                                                start=(c == 0), stop=(c == n))
                    if n == 2:
                        last.then_inc(s_o, 1)
                    if n != 2:
                        last.then_inc(s_dp, 1)
                if 4 <= t < DU + 4:
                    u = t - 4
                    h, n = divmod(u, 3)
                    t0, wd = CHUNKS[n]
                    pe.wait_ge(s_dw, u0 + u + 1)
                    if u:
                        pe.wait_ge(s_dc, u0 + u)
                    for c in range(n + 1):
                        k0, kw = CHUNKS[c]
                        last = nc.tensor.transpose(PS[0:kw, 4, c * P:c * P + wd], MG[0:wd, u % 2, k0:k0 + kw],
                                                   con1[0:wd, 0:wd])
                    last.then_inc(s_dt, 1)
                if t >= 7 and (t - 7) % 3 == 2:
                    h = (t - 7) // 3
                    tail_pe(pe, 2, hh0 + h, h)

        def da_act(act, layer, G_end):
            u0, hh0 = DU * layer, tail_first(layer, 2)
            values_act(act, 3 * layer + 2)
            act.wait_ge(s_lams, layer + 1)
            nc.scalar.activation(sm("t1")[:, 0:2], PS[:, 6, 0:2], ACT.Exp).then_inc(s_lame, 1)
            for t in range(DU + 9):
                if 5 <= t < DU + 5:
                    u = t - 5
                    h, n = divmod(u, 3)
                    t0, wd = CHUNKS[n]
                    act.wait_ge(s_dt, u0 + u + 1)
                    if u >= 2:
                        hu, nu = divmod(u - 2, 3)
                        if nu == 2:
                            act.wait_ge(s_o, hh0 + hu + 1)
                        else:
                            act.wait_ge(s_dp, 2 * (DH * layer + hu) + nu + 1)
                    wt = flat(MG[:, 2 + 2 * (u % 2):4 + 2 * (u % 2), :])
                    full = min(n + 1, 2)
                    last = nc.scalar.copy(wt[:, 0:full * P].rearrange("p (c t) -> p c t", c=full)[:, :, 0:wd],
                                          PS[:, 4, 0:full * P].rearrange("p (c t) -> p c t", c=full)[:, :, 0:wd])
                    if n == 2:
                        last = nc.scalar.copy(wt[0:N_META, 2 * P:2 * P + wd], PS[0:N_META, 4, 2 * P:2 * P + wd])
                    last.then_inc(s_dc, 1)
                if 2 <= t < DU + 2:
                    u = t - 2
                    h, n = divmod(u, 3)
                    t0, wd = CHUNKS[n]
                    act.wait_ge(s_dx, u0 + u + 1)
                    for m in range(2):
                        e = MJ[0:wd, 2 * (u % 4) + m, 0:t0 + wd]
                        last = nc.scalar.activation(e, e, ACT.Exp, bias=dst[0:wd, u % 4, m:m + 1],
                                                    accum_out=dst[0:wd, u % 4, 2 + m:3 + m])
                    last.then_inc(s_de, 1)
                if t >= 7 and (t - 7) % 3 == 2 and t < DU + 7:
                    tail_act_square(act, 2, hh0 + (t - 7) // 3, (t - 7) // 3)
                if t >= 8 and (t - 8) % 3 == 2:
                    tail_act_rdev(act, 2, hh0 + (t - 8) // 3, (t - 8) // 3)
                if t >= 9 and (t - 9) % 3 == 2:
                    tail_act_high(act, 2, hh0 + (t - 9) // 3, (t - 9) // 3)

        def da_dve(dve, link, layer, G_end):
            u0, hh0 = DU * layer, tail_first(layer, 2)
            lambda_init = 0.8 - 0.6 * math.exp(-0.3 * layer)
            lp = COLS["lam"] + 4 * layer
            nc.vector.tensor_tensor(sm("t0")[:, 0:2], cols[:, lp:lp + 4:2], cols[:, lp + 1:lp + 4:2],
                                    ALU.mult).then_inc(s_lamp, 1)
            dve.wait_ge(s_lame, layer + 1)
            link(nc.vector.scalar_tensor_tensor(sm("lam")[:, 0:1], sm("t1")[:, 1:2], -lambda_init, sm("t1")[:, 0:1],
                                                ALU.add, ALU.subtract))
            link(nc.vector.tensor_scalar(sm("sub")[:, 0:1], col("subln", layer), 1.0 - lambda_init, None, ALU.mult))
            rope_dve(dve, cc("sin_d"), 24 * layer + 8, 16)
            for t in range(DU + 11):
                if 3 <= t < DU + 3:
                    u = t - 3
                    h, n = divmod(u, 3)
                    t0, wd = CHUNKS[n]
                    dve.wait_ge(s_de, u0 + u + 1)
                    st = dst[0:wd, u % 4, :]
                    link(nc.vector.reciprocal(st[:, 2:4], st[:, 2:4]))
                    if u >= 2:
                        dve.wait_ge(s_dt, u0 + u - 1)
                    wgt = MG[0:wd, u % 2, 0:t0 + wd]
                    nc.vector.tensor_tensor(st[:, 3:4], st[:, 3:4], sm("lam")[0:wd, 0:1], ALU.mult)
                    link(nc.vector.tensor_scalar(wgt, MJ[0:wd, 2 * (u % 4), 0:t0 + wd], st[:, 2:3], None, ALU.mult))
                    nc.vector.scalar_tensor_tensor(wgt, MJ[0:wd, 2 * (u % 4) + 1, 0:t0 + wd], st[:, 3:4], wgt,
                                                   ALU.mult, ALU.add).then_inc(s_dw, 1)
                if 1 <= t <= DU:
                    u = t - 1
                    h, n = divmod(u, 3)
                    t0, wd = CHUNKS[n]
                    dve.wait_ge(s_ds, u0 + u + 1)
                    b = 2 * (u % 2)
                    c = 2 * (u % 4)
                    s = MJ[0:wd, c:c + 2, 0:t0 + wd]
                    if u >= 4:
                        dve.wait_ge(s_dw, u0 + u - 3)
                    mask = bc(con2[0:wd, C2["dmask"] + n * T2:C2["dmask"] + n * T2 + t0 + wd], 2)
                    nc.vector.scalar_tensor_tensor(s, PS[0:wd, b:b + 2, 0:t0 + wd], 64 ** -0.5, mask,
                                                   ALU.mult, ALU.add).then_inc(s_dm, 1)
                    dve.wait_ge(s_dm, u0 + u + 1)
                    nc.vector.tensor_reduce(dst[0:wd, u % 4, 0:2], s, AX.X, ALU.max, negate=True).then_inc(s_dx, 1)
                if t >= 10 and (t - 10) % 3 == 2:
                    tail_dve_low(dve, 2, hh0 + (t - 10) // 3, (t - 10) // 3)
                if t >= 9 and (t - 9) % 3 == 2:
                    tail_dve_gate(dve, link, 2, hh0 + (t - 9) // 3, (t - 9) // 3)

        NL = len(LEVELS)
        Q_, CBT, K_ = MI[:, 0:8, :], MI[:, 8:16, :], MI[:, 16:24, :]
        KDT = flat(QB[:])[:, 0:2 * D].rearrange("p (n f) -> p n f", n=2)
        ST = flat(CBT)[:, 0:2 * D].rearrange("p (n f) -> p n f", n=2)
        LEVEL_PE = 1 + NL
        HT = LEVEL_PE + 4

        def halves(ap, s):
            if s <= 8:
                v = flat(ap).rearrange("p (b w t) -> p b w t", w=2, t=s)
                nb = KT * T2 // (2 * s)
                pitch = 2 * s
                left, right, ref = v[:, :, 0, :], v[:, :, 1, :], v[:, :, 0, s - 1:s]
                ref = bass.AP(ref.tensor, ref.offset, [ref.ap[0], [pitch, nb], [0, s]])
                return left, right, ref
            v = ap[:, :, 0:2 * P].rearrange("p h (b w t) -> p h b w t", w=2, t=s)
            left, right, ref = v[:, :, :, 0, :], v[:, :, :, 1, :], v[:, :, :, 0, s - 1:s]
            ref = bass.AP(ref.tensor, ref.offset, [ref.ap[0], [T2, KT], [2 * s, 2 * P // (2 * s)], [0, s]])
            return left, right, ref

        def hg_scores(lhs, rhs):
            for h in range(HH):
                for n, (t0, wd) in enumerate(CHUNKS):
                    if n < 2:
                        out = PS[:, 2 * n + h // 4, (h % 4) * P:(h % 4 + 1) * P]
                    else:
                        out = PS[0:wd, 4, h * wd:(h + 1) * wd]
                    last = nc.tensor.matmul(out, lhs[:, h, t0:t0 + wd], rhs[:, h, t0:t0 + wd], start=True, stop=True)
            return last

        def hg_level(n, s):
            q = (QB, QB1)[n % 2]
            for c, (t0, wd) in enumerate(CHUNKS):
                if c == 2 and s > 8:
                    continue
                for h in range(HH):
                    out = PS[0:wd, level_bank(n) + c, h * wd // 2:(h + 1) * wd // 2]
                    out = out.rearrange("p (b t) -> p b t", t=s)
                    last = nc.tensor.matmul(out, q[:, h, t0:t0 + wd], right_half(q[:, h, t0:t0 + wd], s),
                                            start=True, stop=True)
            return last

        def level_bank(n):
            return 0 if n % 2 else 5

        def right_half(ap, s):
            if len(ap.shape) == 2:
                return ap.rearrange("p (b w t) -> p b w t", w=2, t=s)[:, :, 1, :]
            return ap.rearrange("p h (b w t) -> p h b w t", w=2, t=s)[:, :, :, 1, :]

        def hg_pe(pe, layer, G_end):
            pe.wait_ge(s_free, 2 * G_end + 4)
            t, d, a, p = HT * layer, HDV * layer, HAC * layer, HPO * layer
            values_pe(pe, MJ, 3 * layer + 1)
            pe.wait_ge(s_vc, 3 * (3 * layer + 2))
            pe.wait_ge(s_hf, 4 * (layer + 1))
            hg_scores(K_, Q_).then_inc(s_ht, 1)
            for n, s in enumerate(LEVELS):
                pe.wait_ge(s_hq, NL * layer + n + 1)
                if n:
                    pe.wait_ge(s_hk, (NL + 1) * layer + n)
                hg_level(n, s).then_inc(s_ht, 1)
            pe.wait_ge(s_hk, (NL + 1) * (layer + 1) - 1)
            pe.wait_ge(s_hd, d + HD_END + 2)
            for n in range(2):
                for h in range(HH):
                    last = nc.tensor.transpose(PS[:, 2 * n + h // 4, (h % 4) * P:(h % 4 + 1) * P],
                                               K_[:, h, n * P:(n + 1) * P], ident)
                last.then_inc(s_ht, 1)
            pe.wait_ge(s_hk, (NL + 1) * (layer + 1))
            for n in range(2):
                pe.wait_ge(s_ha, a + HA_KT + n + 1)
                for h in range(HH):
                    f = slice(h * P, (h + 1) * P)
                    last = nc.tensor.matmul(PS[:, 4 + 2 * n + h // 4, (h % 4) * P:(h % 4 + 1) * P],
                                            KDT[:, n, f], VT[:, n, f], start=True, stop=True)
                last.then_inc(s_ht, 1)
            pe.wait_ge(s_hd, d + HDV)
            pe.wait_ge(s_hp, p + HPO)
            u0 = tail_first(layer, 1)
            for u in range(HH // 2 + 2):
                if u < HH // 2:
                    if u >= 3:
                        pe.wait_ge(s_ot, u0 + u - 2)
                    for h in (2 * u, 2 * u + 1):
                        f = slice(h * P, (h + 1) * P)
                        for n, (t0, wd) in enumerate(CHUNKS):
                            out = PS[:, 2 * (u % 3) + h % 2, t0:t0 + wd]
                            last = nc.tensor.matmul(out, VT[0:wd, n, f], AM[0:wd, h, t0:t0 + wd], start=True,
                                                    stop=(n == 0))
                            if n:
                                last = nc.tensor.matmul(out, ST[:, n - 1, f], Q_[:, h, t0:t0 + wd], start=False,
                                                        stop=True)
                    last.then_inc(s_o, 1)
                if 1 <= u <= HH // 2:
                    v = u - 1
                    pe.wait_ge(s_osq, u0 + v + 1)
                    if v:
                        pe.wait_ge(s_oln, u0 + v)
                    for x in range(2):
                        last = nc.tensor.matmul(PS[:, 6 + x, 0:T2], ones[:], SX[:, v % 2, x, :],
                                                start=True, stop=True)
                    last.then_inc(s_oms, 1)

        HD_CB = 1
        HD_END = HD_CB
        HDV = HD_END + 4
        HA_LEVEL = 1
        HA_KT = HA_LEVEL + NL + 2
        HAC = HA_KT + 2
        HPO = 2 + NL

        def hg_logs(act, layer):
            act.wait_ge(s_hf, 4 * (layer + 1))
            nc.scalar.activation(EX[:], EX[:], ACT.Ln)
            nc.scalar.activation(CBT, CBT, ACT.Ln).then_inc(s_ha, 1)

        def level_exps(act, layer, n):
            act.wait_ge(s_hr, NL * layer + n + 1)
            act.wait_ge(s_hp, HPO * layer + 2 + n)
            e = (EX, MJ)[n % 2]
            e = e[:] if LEVELS[n] <= 8 else e[:, :, 0:2 * P]
            nc.scalar.activation(e, e, ACT.Exp).then_inc(s_ha, 1)

        def hg_act(act, layer, G_end):
            t, d, a, p = HT * layer, HDV * layer, HAC * layer, HPO * layer
            values_act(act, 3 * layer + 1)
            for n in range(1, NL):
                level_exps(act, layer, n)
            act.wait_ge(s_hq, NL * (layer + 1) - 1)
            nc.scalar.activation(MJ[:], CBT, ACT.Exp)
            nc.scalar.activation(sm("t0"), CBT[:, :, 2 * P - 1], ACT.Exp).then_inc(s_ha, 1)
            act.wait_ge(s_hd, d + HD_END + 1)
            nc.scalar.activation(EX[:, :, 0:2 * P], EX[:, :, 0:2 * P], ACT.Exp).then_inc(s_ha, 1)
            for n in range(2):
                act.wait_ge(s_ht, t + LEVEL_PE + n + 1)
                nc.scalar.copy(KDT[:, n, :].rearrange("p (a t) -> p a t", a=2),
                               PS[:, 2 * n:2 * n + 2, :]).then_inc(s_ha, 1)
            u0 = tail_first(layer, 1)
            for u in range(HH // 2 + 2):
                if u < HH // 2:
                    act.wait_ge(s_o, u0 + u + 1)
                    if u >= 2:
                        act.wait_ge(s_oms, u0 + u - 1)
                    b = 2 * (u % 3)
                    nc.scalar.activation(SX[:, u % 2, :, :], PS[:, b:b + 2, 0:T2], ACT.Square).then_inc(s_osq, 1)
                if u >= 2:
                    v = u - 2
                    act.wait_ge(s_ot, u0 + v + 1)
                    nc.scalar.copy(OH[:, 2 * v:2 * v + 2, :], SY[:, v % 2, :, :]).then_inc(s_oth, 1)
                if 1 <= u <= HH // 2:
                    v = u - 1
                    act.wait_ge(s_oms, u0 + v + 1)
                    if v >= 2:
                        act.wait_ge(s_ot, u0 + v - 1)
                    rs = MJ[:, 2 * (v % 2):2 * (v % 2) + 2, :]
                    nc.scalar.activation(rs, PS[:, 6:8, 0:T2], ACT.Ln, bias=epsc[:, 0:1],
                                         scale=1.0 / P).then_inc(s_oln, 1)
                    act.wait_ge(s_oln, u0 + v + 1)
                    nc.scalar.activation(rs, rs, ACT.Exp, scale=-0.5).then_inc(s_ord, 1)

        def hg_pool_first(pool, layer, G_end):
            pool.wait_ge(s_free, 2 * G_end + 4)
            nc.gpsimd.memset(AM[:], 0.0).then_inc(s_hp, 1)
            left_exponents(pool, layer, 0)

        def left_exponents(pool, layer, n):
            if n == 0:
                pool.wait_ge(s_hd, HDV * layer + HD_CB)
            elif n == 1:
                pool.wait_ge(s_vt, 3 * (3 * layer + 2))
            else:
                pool.wait_ge(s_hq, NL * layer + n - 1)
            left, _, _ = halves((EX, MJ)[n % 2][:], LEVELS[n])
            cl, _, ref = halves(CBT, LEVELS[n])
            nc.gpsimd.tensor_tensor(left, ref, cl, ALU.subtract).then_inc(s_hp, 1)

        def hg_pool(pool, layer):
            for n in range(1, NL):
                left_exponents(pool, layer, n)
            pool.wait_ge(s_ha, HAC * layer + HA_LEVEL + NL + 1)
            pool.wait_ge(s_hq, NL * (layer + 1))
            pool.wait_ge(s_ht, HT * layer + 1)
            nc.gpsimd.tensor_tensor(Q_, Q_, MJ[:], ALU.mult).then_inc(s_hp, 1)

        def hg_bounds(dve, link):
            dve.wait_ge(s_lbe, 1)
            link(nc.vector.tensor_tensor(sm("t3"), sm("t1"), sm("t2"), ALU.add))
            link(nc.vector.reciprocal(sm("t3"), sm("t3")))
            link(nc.vector.tensor_tensor(sm("t1"), sm("t1"), sm("t3"), ALU.mult))
            link(nc.vector.tensor_tensor(sm("t2"), sm("t2"), sm("t3"), ALU.mult))
            for layer in range(DEPTH):
                lbm, olb = sm(f"lbm{layer}"), sm(f"olb{layer}")
                if layer == 0:
                    link(nc.vector.tensor_tensor(sm("t3"), sm("t1"), sm("t1"), ALU.subtract))
                else:
                    link(nc.vector.tensor_tensor(sm("t3"), sm("t1"), sm("t2"), ALU.add))
                    link(nc.vector.tensor_tensor(sm("t3"), sm("t3"), sm("t1"), ALU.subtract))
                link(nc.vector.tensor_scalar(lbm, sm("t3"), 1e-30, None, ALU.max))
                link(nc.vector.tensor_scalar(olb, sm("t3"), -1.0, 1.0, ALU.mult, ALU.add))

        def hg_gates(dve, link, layer, n):
            lbm, olb = sm(f"lbm{layer}"), sm(f"olb{layer}")
            for h in (n, n + 1):
                nc.vector.tensor_scalar(K_[:, h, :], K_[:, h, :], olb[:, h:h + 1], None, ALU.mult)
                last = nc.vector.tensor_scalar(CBT[:, h, :], CBT[:, h, :], olb[:, h:h + 1], lbm[:, h:h + 1],
                                               ALU.mult, ALU.add)
            link(last)
            f = CBT[:, n:n + 2, :]
            link(nc.vector.tensor_scalar(EX[:, n:n + 2, :], f, 2.0 ** -60, None, ALU.max))
            nc.vector.tensor_scalar(f, f, 2.0 ** 60, 1.0, ALU.mult, ALU.min).then_inc(s_hf, 1)

        def hg_cumulate(dve, link, layer):
            dve.wait_ge(s_ha, HAC * layer + 1)
            link(nc.vector.tensor_tensor(CBT, CBT, EX[:], ALU.add))
            for h in range(HH):
                last = nc.vector.tensor_tensor_scan(CBT[:, h, :], cc("reset"), CBT[:, h, :], 0.0, ALU.mult, ALU.add)
            last.then_inc(s_hd, 1)

        def right_exponents(dve, layer, n):
            if n == 0:
                dve.wait_ge(s_hd, HDV * layer + HD_CB)
            elif n == 1:
                dve.wait_ge(s_vt, 3 * (3 * layer + 2))
            else:
                dve.wait_ge(s_hq, NL * layer + n - 1)
            _, er, _ = halves((EX, MJ)[n % 2][:], LEVELS[n])
            _, cr, ref = halves(CBT, LEVELS[n])
            nc.vector.tensor_tensor(er, cr, ref, ALU.subtract).then_inc(s_hr, 1)

        def level_operands(dve, layer, n):
            s = LEVELS[n]
            el, er, _ = halves((EX, MJ)[n % 2][:], s)
            kl, _, _ = halves(K_, s)
            _, qr, _ = halves(Q_, s)
            bl, br, _ = halves((QB, QB1)[n % 2][:], s)
            dve.wait_ge(s_ha, HAC * layer + HA_LEVEL + n + 1)
            if n >= 2:
                dve.wait_ge(s_ht, HT * layer + n)
            nc.vector.tensor_tensor(bl, el, kl, ALU.mult)
            nc.vector.tensor_tensor(br, er, qr, ALU.mult).then_inc(s_hq, 1)

        def hg_dve(dve, link, layer, G_end):
            t, d, a, p = HT * layer, HDV * layer, HAC * layer, HPO * layer
            def pick(n):
                dve.wait_ge(s_ht, t + n + 1)
                if n == 0:
                    dve.wait_ge(s_hp, p + 1)
                else:
                    dve.wait_ge(s_hk, (NL + 1) * layer + n)
                m = C2["levels"] + n * P
                for c, (t0, wd) in enumerate(CHUNKS):
                    mask = con2[0:wd, m:m + wd].bitcast(I32)
                    if n:
                        s = LEVELS[n - 1]
                        if c == 2 and s > 8:
                            continue
                        src = PS[0:wd, level_bank(n - 1) + c, 0:HH * wd // 2]
                        last = nc.vector.copy_predicated(right_half(AM[0:wd, :, t0:t0 + wd], s),
                                                         bc(right_half(mask, s), HH),
                                                         src.rearrange("p (h b t) -> p h b t", h=HH, t=s))
                    elif c < 2:
                        for g in range(2):
                            last = nc.vector.copy_predicated(AM[:, 4 * g:4 * g + 4, t0:t0 + wd], bc(mask, 4),
                                                             PS[:, 2 * c + g, :].rearrange("p (h t) -> p h t", h=4))
                    else:
                        last = nc.vector.copy_predicated(AM[0:wd, :, t0:t0 + wd], bc(mask, HH),
                                                         PS[0:wd, 4, 0:HH * wd].rearrange("p (h t) -> p h t", h=HH))
                last.then_inc(s_hk, 1)

            def end_exponents():
                c2 = CBT[:, :, 0:2 * P].rearrange("p h (c t) -> p h c t", c=2)
                ref = bass.AP(c2.tensor, c2.offset + P - 1, [c2.ap[0], [T2, KT], [P, 2], [0, P]])
                e2 = EX[:, :, 0:2 * P].rearrange("p h (c t) -> p h c t", c=2)
                dve.wait_ge(s_hq, NL * (layer + 1))
                nc.vector.tensor_tensor(e2, ref, c2, ALU.subtract).then_inc(s_hd, 1)

            right_exponents(dve, layer, 1)
            for n in range(NL):
                if n:
                    level_operands(dve, layer, n)
                if n + 2 < NL:
                    right_exponents(dve, layer, n + 2)
                if n == NL - 1:
                    end_exponents()
                pick(n)
            dve.wait_ge(s_ha, a + HA_LEVEL + NL + 2)
            k2 = K_[:, :, 0:2 * P]
            nc.vector.tensor_tensor(k2, k2, EX[:, :, 0:2 * P], ALU.mult).then_inc(s_hd, 1)
            pick(NL)
            dve.wait_ge(s_ht, t + LEVEL_PE + 3)
            nc.vector.tensor_copy(ST[:, 0, :].rearrange("p (a t) -> p a t", a=2), PS[:, 4:6, :]).then_inc(s_hd, 1)
            dve.wait_ge(s_hd, d + HD_END + 3)
            dve.wait_ge(s_ht, t + LEVEL_PE + 4)
            for h in range(HH):
                f = slice(h * P, (h + 1) * P)
                last = nc.vector.scalar_tensor_tensor(ST[:, 1, f], ST[:, 0, f], sm("t0")[:, h:h + 1],
                                                      PS[:, 6 + h // 4, (h % 4) * P:(h % 4 + 1) * P],
                                                      ALU.mult, ALU.add)
            last.then_inc(s_hd, 1)
            u0 = tail_first(layer, 1)
            for u in range(HH // 2 + 1):
                if u < HH // 2:
                    dve.wait_ge(s_ord, u0 + u + 1)
                    if u >= 2:
                        dve.wait_ge(s_tail_low, u0 + u - 1)
                    b, x, sy = 2 * (u % 3), 2 * (u % 2), SY[:, u % 2, :, :]
                    link(nc.vector.tensor_tensor(sy, PS[:, b:b + 2, 0:T2], MJ[:, x:x + 2, :], ALU.mult))
                    nc.vector.tensor_tensor(sy, sy, MG[:, 2 * u:2 * u + 2, :], ALU.mult).then_inc(s_ot, 1)
                if u:
                    v = u - 1
                    dve.wait_ge(s_oth, u0 + v + 1)
                    nc.vector.tensor_tensor(OL[:, 2 * v:2 * v + 2, :], SY[:, v % 2, :, :],
                                            OH[:, 2 * v:2 * v + 2, :].bitcast(F32),
                                            ALU.subtract).then_inc(s_tail_low, 1)

        NU = 4 * KT

        def na_pe(pe, G_end):
            pe.wait_ge(s_free, 2 * G_end + 4)
            for n in range(4):
                if n >= 2:
                    pe.wait_ge(s_nvc, n - 1)
                for f in range(KT):
                    last = nc.tensor.transpose(PS[:, 2 * (n % 2) + f // 4, (f % 4) * P:(f % 4 + 1) * P],
                                               NVT[:, f, n * P:(n + 1) * P], ident)
                last.then_inc(s_nvt, 1)
            for u in range(2 * KT):
                if u >= 2:
                    pe.wait_ge(s_nr1, u - 1)
                src = NQ if u < KT else NK
                nc.tensor.matmul(PS[:, 6 + u % 2, 0:SEQ], con1[:, C1["rot"]:C1["rot"] + P], src[:, u % KT, 0:SEQ],
                                 start=True, stop=True).then_inc(s_nrot, 1)
            pe.wait_ge(s_nr2, 2 * KT)
            pe.wait_ge(s_nvc, 4)
            for t in range(NU + 6):
                if t < NU:
                    hp, hl, qt = t // 4, t // 2 % 2, t % 2
                    r = slice(64 * hl, 64 * hl + 64)
                    if t >= 2:
                        pe.wait_ge(s_na, t - 1)
                    nc.tensor.matmul(PS[:, t % 2, :], NQ[r, hp, qt * P:(qt + 1) * P], NK[r, hp, :],
                                     start=True, stop=True).then_inc(s_ns, 1)
                if t >= 6:
                    u = t - 6
                    hp, hl, qt = u // 4, u // 2 % 2, u % 2
                    pe.wait_ge(s_nc, u + 1)
                    if u % 4 == 0 and hp >= 2:
                        pe.wait_ge(s_no_low, hp - 1)
                    for c in range(4):
                        last = nc.tensor.matmul(PS[64 * hl:64 * hl + 64, 6 + hp % 2, qt * P:(qt + 1) * P],
                                                NV[:, c, (2 * hp + hl) * HD:(2 * hp + hl + 1) * HD],
                                                PT[:, u % 2, c * P:(c + 1) * P], start=(c == 0), stop=(c == 3))
                    last.then_inc(s_no, 1)
                if 4 <= t < NU + 4:
                    u = t - 4
                    pe.wait_ge(s_nw, u + 1)
                    if u >= 2:
                        pe.wait_ge(s_nc, u - 1)
                    for c in range(4):
                        last = nc.tensor.transpose(PS[:, 2 + u % 2, c * P:(c + 1) * P],
                                                   SB[:, u % 4, c * P:(c + 1) * P], ident)
                    last.then_inc(s_nt, 1)

        def na_act(act, G_end):
            for n in range(4):
                act.wait_ge(s_nvt, n + 1)
                nc.scalar.copy(NV[:, n, :].rearrange("p (a t) -> p a t", a=2),
                               PS[:, 2 * (n % 2):2 * (n % 2) + 2, :]).then_inc(s_nvc, 1)
            act.wait_ge(s_lb, 1)
            e = small[:, 15 * KT:17 * KT]
            nc.scalar.activation(e, e, ACT.Exp).then_inc(s_lbe, 1)
            for t in range(NU + 8):
                if 5 <= t < NU + 5:
                    u = t - 5
                    act.wait_ge(s_nt, u + 1)
                    if u >= 2:
                        act.wait_ge(s_no, u - 1)
                    nc.scalar.copy(PT[:, u % 2, :], PS[:, 2 + u % 2, :]).then_inc(s_nc, 1)
                if 1 <= t <= NU:
                    u = t - 1
                    act.wait_ge(s_nm, u + 1)
                    nc.scalar.activation(SB[:, u % 4, :], SB[:, u % 4, :], ACT.Exp, bias=nst[:, u % 4, 0:1],
                                         accum_out=nst[:, u % 4, 1:2]).then_inc(s_ne, 1)
                if t >= 7 and (t - 7) % 4 == 3:
                    hp = (t - 7) // 4
                    act.wait_ge(s_no, 4 * hp + 4)
                    nc.scalar.copy(XH[:, hp, 0:SEQ], PS[:, 6 + hp % 2, 0:SEQ]).then_inc(s_no_high, 1)

        def na_dve(dve, link, G_end):
            a0, a1 = col("hg_lb", 0, KT), col("hg_lb", KT, KT)
            link(nc.vector.tensor_tensor(sm("t0"), a0, a1, ALU.max))
            link(nc.vector.tensor_tensor(sm("t1"), a0, sm("t0"), ALU.subtract))
            nc.vector.tensor_tensor(sm("t2"), a1, sm("t0"), ALU.subtract).then_inc(s_lb, 1)
            dve.wait_ge(s_bias, 16 * 12)
            colmask = con1[:, C1["colmask"]:C1["colmask"] + GRID_W]
            nc.vector.tensor_tensor(TB[:].rearrange("p h j c -> p (h j) c"), TB[:].rearrange("p h j c -> p (h j) c"),
                                    bc(colmask, 6 * NH), ALU.add)
            sin = con1[:, C1["sin"]:C1["sin"] + SEQ]
            for u in range(2 * KT):
                x = (NQ if u < KT else NK)[:, u % KT, 0:SEQ]
                dve.wait_ge(s_nrot, u + 1)
                nc.vector.tensor_tensor(ROT[:, u % 2, :], PS[:, 6 + u % 2, 0:SEQ], sin, ALU.mult).then_inc(s_nr1, 1)
                dve.wait_ge(s_nr1, u + 1)
                dve.wait_ge(s_nrc, u + 1)
                nc.vector.tensor_tensor(x, x, ROT[:, u % 2, :], ALU.add).then_inc(s_nr2, 1)
            hg_bounds(dve, link)
            dve.wait_ge(s_nvt, 4)
            for t in range(NU + 8):
                if 2 <= t < NU + 2:
                    u = t - 2
                    dve.wait_ge(s_ne, u + 1)
                    nc.vector.reciprocal(nst[:, u % 4, 2:3], nst[:, u % 4, 1:2]).then_inc(s_nr, 1)
                if t < NU:
                    hd, qt = t // 2, t % 2
                    dve.wait_ge(s_ns, t + 1)
                    if t >= 4:
                        dve.wait_ge(s_nt, t - 3)
                    b = TB[:, hd, 2 - 2 * qt:6 - 2 * qt, :].rearrange("p j c -> p (j c)")
                    nc.vector.tensor_tensor(SB[:, t % 4, 0:SEQ], PS[:, t % 2, 0:SEQ], b, ALU.add)
                    nc.vector.tensor_copy(SB[:, t % 4, SEQ:T1], PS[:, t % 2, SEQ:T1]).then_inc(s_na, 1)
                    dve.wait_ge(s_na, t + 1)
                    nc.vector.tensor_reduce(nst[:, t % 4, 0:1], SB[:, t % 4, :], AX.X, ALU.max,
                                            negate=True).then_inc(s_nm, 1)
                if t >= 7 and (t - 7) % 4 == 3:
                    na_low(dve, (t - 7) // 4)

        def na_low(dve, hp):
            dve.wait_ge(s_no_high, hp + 1)
            nc.vector.tensor_tensor(XL[:, hp, 0:SEQ], PS[:, 6 + hp % 2, 0:SEQ], XH[:, hp, 0:SEQ].bitcast(F32),
                                    ALU.subtract).then_inc(s_no_low, 1)

        def na_pool(pool):
            for u in range(2 * KT):
                x = (NQ if u < KT else NK)[:, u % KT, 0:SEQ]
                pool.wait_ge(s_nrot, u + 1)
                nc.gpsimd.tensor_tensor(x, x, con1[:, C1["cos"]:C1["cos"] + SEQ], ALU.mult).then_inc(s_nrc, 1)
            for u in range(NU):
                pool.wait_ge(s_nr, u + 1)
                nc.gpsimd.tensor_scalar(SB[:, u % 4, :], SB[:, u % 4, :], nst[:, u % 4, 2:3], None,
                                        ALU.mult).then_inc(s_nw, 1)

        def rms_squares(m):
            return SQ if m and m % 2 == 0 else TN

        def rms_pe(pe, m, G_end):
            for hf in range(2):
                pe.wait_ge(s_rsq, 2 * m + hf + 1)
                for k in range(4 * hf, 4 * hf + 4):
                    last = nc.tensor.matmul(PS[:, norm_bank(G_end) + 1, 0:T2], ones[:], rms_squares(m)[:, k, :],
                                            start=(k == 0), stop=(k == KT - 1))
            last.then_inc(s_rsum, 1)

        def rms_act(act, m, G_end):
            if not m:
                act.wait_ge(s_res, 6 * KT + KT)
                act.wait_ge(s_meta, 32)
            for hf in range(2):
                k = slice(4 * hf, 4 * hf + 4)
                if m:
                    act.wait_ge(s_free, 2 * G_end + 2 + 2 * hf)
                nc.scalar.activation(rms_squares(m)[:, k, :], H[:, k, :], ACT.Square).then_inc(s_rsq, 1)
            act.wait_ge(s_rsum, m + 1)
            nc.scalar.activation(RS[:, 0, 0:T2], PS[:, norm_bank(G_end) + 1, 0:T2], ACT.Ln, bias=epsc[:, 0:1],
                                 scale=1.0 / D).then_inc(s_rln, 1)
            act.wait_ge(s_rln, m + 1)
            nc.scalar.activation(RS[:, 1, 0:T2], RS[:, 0, 0:T2], ACT.Exp, scale=-0.5).then_inc(s_rrd, 1)
            if m < 4:
                for k in range(0, KT, 2):
                    act.wait_ge(s_rmod, KT * m + k + 2)
                    nc.scalar.copy(NHh[:, k:k + 2, :], TN[:, k:k + 2, :]).then_inc(s_rxh, 1)

        def rms_dve(dve, m, name, layer):
            dve.wait_ge(s_rrd, m + 1)
            for k in range(KT):
                out = s_rmod if m < 4 else s_modd_final
                nc.vector.scalar_tensor_tensor(TN[:, k, :], H[:, k, :], col(name, layer * KT + k), RS[:, 1, 0:T2],
                                               ALU.mult, ALU.mult).then_inc(out, 1)
            if m < 4:
                for hf in range(2):
                    k = slice(4 * hf, 4 * hf + 4)
                    dve.wait_ge(s_rxh, 4 * m + 2 * hf + 2)
                    nc.vector.tensor_tensor(NHl[:, k, :], TN[:, k, :], NHh[:, k, :].bitcast(F32),
                                            ALU.subtract).then_inc(s_rxl, 1)

        block = ctx.enter_context(nc.Block())

        @block.sync
        def _(sp):
            for s in steps:
                if s["name"] == "ada":
                    with sp.Fori(0, ADA // 2) as h:
                        for odd in range(2):
                            i = 2 * h + odd
                            g = s["g0"] + i
                            for q in range(4):
                                if s["layer"] or odd:
                                    sp.wait_ge(s_low, 4 * g + q - 3)
                                else:
                                    sp.wait_ge(s_low, 4 * g + q + 1)
                                dst, loaded, _ = raw_of(g, odd)
                                for x, src in enumerate(s["src"](i, 2 * q, 2)):
                                    sp.dma_start(dst[:, q, x, :], src).then_inc(loaded[q], 16)
                    continue
                for i in groups_of(sp, s):
                    for pi, (k0, nk) in enumerate(s["panels"]):
                        g = s["g0"] + len(s["panels"]) * i + pi
                        for q in range(4):
                            n = 2 if q < 3 else nk - 6
                            sp.wait_ge(s_low, 4 * g + q + 1)
                            for x, src in enumerate(s["src"](i, k0 + 2 * q, n)):
                                if n == 2 and not s["halves"]:
                                    dst = raw[:, q, x, :]
                                else:
                                    dst = raw[:, q, 0:n, x * PW // 2:(x + 1) * PW // 2]
                                    if not s["halves"]:
                                        dst = dst.rearrange("p k n -> p (k n)")
                                sp.dma_start(dst, src).then_inc(s_raw[q], 16)
            sp.wait_ge(s_modd_final, KT)
            sp.dma_start(out_d, TN[:, :, N_META:T2]).then_inc(s_out, 16)
            sp.wait_ge(s_out, 16)

        @block.tensor
        def _(pe):
            pe.sem_inc(s_half, 1)
            pe.sem_inc(s_half, 1)
            norms = rmss = 0

            for s in steps:
                name, T, t0 = s["name"], s["T"], s["t0"]
                if name == "ada":
                    pe.wait_ge(s_sc4, 2)
                    pe.wait_ge(s_tokens, 48)
                elif name == "res" and s["layer"] == 0 and s["r"] == 1:
                    pe.wait_ge(s_no_low, KT)
                if name == "branch":
                    pe.wait_ge(s_tail_low, tail_count(s["layer"], s["n"]))
                if name in ("glu", "q", "k", "v", "cgate"):
                    mh, ml = XH, XL
                elif name == "res":
                    mh, ml = (XH, XL) if (s["layer"] == 0 and s["r"] == 1) else (GH, GL)
                elif name in ("store", "gate", "forget", "mgate", "conv"):
                    mh, ml = NHh, NHl
                elif name == "branch":
                    mh, ml = OH, OL
                elif name == "add":
                    mh, ml = (NHh, NHl) if len(s["panels"]) == 1 else (G2H, G2L)
                colof = COLOF[s["halves"]]

                def ada_turn(t, first=False):
                    out = bank(t, 0).rearrange("p a n -> p (a n)")
                    if not first:
                        pe.wait_ge(s_adarow, t)
                    for x in range(TURN):
                        g = TURN * t + x
                        for hf in range(2):
                            pe.wait_ge(s_low, 4 * g + 2 * hf + 6)
                            for k in range(4 * hf, 4 * hf + 4):
                                sc = SC4[:, k, SC0 - 4 * x:SC0 - 4 * x + P]
                                nc.tensor.matmul(out, sc, high[:, k // 2, k % 2, :],
                                                 start=(x == 0 and k == 0), stop=False)
                                last = nc.tensor.matmul(out, sc, low[:, k // 2, k % 2, :], start=False,
                                                        stop=(x == TURN - 1 and k == KT - 1))
                            last.then_inc(s_half, 1)
                            if x == 1 and hf == 0 and not first:
                                ada_columns(t - 1)

                def ada_columns(t):
                    pe.wait_ge(s_adarow, t + 2)
                    out = bank(t, 2).rearrange("p a n -> p (a n)")
                    for j in range(4):
                        last = nc.tensor.matmul(out[:, j * P:j * P + 4 * TURN], adarow[:, j * P:(j + 1) * P],
                                                con1[:, 0:4 * TURN], start=True, stop=True)
                    last.then_inc(s_pair0, 1)

                def rows_ready(i, pi, hf, k_end):
                    if s["groups"] == 2 and i:
                        return
                    if name in ("glu", "q", "cgate") and pi == 0:
                        pe.wait_ge(s_xl, 2 * norms + hf + 1)
                    if s.get("after_rms") and pi == 0:
                        pe.wait_ge(s_rxl, 2 * rmss + hf - 1)
                    if len(s["panels"]) > 1:
                        pe.wait_ge(s_hl, s["hid0"] + 2 - FT + k_end)
                    if name == "add" and len(s["panels"]) == 1:
                        pe.wait_ge(s_yl, 2 * s["layer"] + hf + 1)
                    if name == "res" and s["r"] == 1 and s["layer"]:
                        pe.wait_ge(s_hl, s["hid0"] + 2 * hf)

                def gemm_group(i):
                    G = s["G0"] + i
                    for pi, (k0, nk) in enumerate(s["panels"]):
                        g = s["g0"] + len(s["panels"]) * i + pi
                        last_panel = pi == len(s["panels"]) - 1
                        for hf in range(2):
                            pe.wait_ge(s_low, 4 * g + 2 * hf + 6)
                            ks = range(4) if hf == 0 else range(4, nk)
                            rows_ready(i, pi, hf, k0 + ks[-1] + 1)
                            for j in range(4):
                                if pi == 0 and hf == 0 and j % 2 == 0:
                                    pe.wait_ge(s_free, 2 * G + j // 2 + 1)
                                out = bank(G, j)[:, :, 0:T].rearrange("p a n -> p (a n)")
                                c = colof[j]
                                for k in ks:
                                    wh = high[:, k // 2, k % 2, c:c + P]
                                    wl = low[:, k // 2, k % 2, c:c + P]
                                    xh, xl = mh[:, k0 + k, t0:t0 + T], ml[:, k0 + k, t0:t0 + T]
                                    nc.tensor.matmul(out, wh, xh, start=(k0 + k == 0), stop=False)
                                    nc.tensor.matmul(out, wh, xl, start=False, stop=False)
                                    last = nc.tensor.matmul(out, wl, xh, start=False,
                                                            stop=(last_panel and k == nk - 1))
                                if last_panel and hf == 1 and j == 1:
                                    last.then_inc(s_pair0, 1)
                            last.then_inc(s_half, 1)

                if name == "ada":
                    if s["layer"] == 0:
                        ada_turn(0, first=True)
                        with pe.Fori(1, DEPTH * ADA // TURN) as t:
                            ada_turn(t)
                        ada_columns(DEPTH * ADA // TURN - 1)
                else:
                    for i in groups_of(pe, s):
                        gemm_group(i)
                G_end = s["G0"] + s["groups"]
                if s.get("norm"):
                    if norms == 0:
                        pe.wait_ge(s_ones, 1)
                    b = norm_bank(G_end)
                    for k in range(KT):
                        if k % 2 == 0:
                            pe.wait_ge(s_free, 2 * G_end + 1 + k // 2)
                        last = nc.tensor.matmul(PS[:, b, 0:T], ones[:], X[:, k, 0:T], start=(k == 0),
                                                stop=(k == KT - 1))
                    last.then_inc(s_sum, 1)
                    for k in range(KT):
                        if k % 2 == 0:
                            pe.wait_ge(s_sq, 4 * norms + k // 2 + 1)
                        last = nc.tensor.matmul(PS[:, b + 1, 0:T], ones[:], TQ[:, k, 0:T], start=(k == 0),
                                                stop=(k == KT - 1))
                    last.then_inc(s_var, 1)
                    norms += 1
                    if norms == 6:
                        rms_pe(pe, rmss, G_end)
                        rmss += 1
                if s.get("rms"):
                    rms_pe(pe, rmss, G_end)
                    rmss += 1
                if name == "v":
                    na_pe(pe, G_end)
                if "mixer" in s:
                    (ret_pe, hg_pe, da_pe)[s["mixer"]](pe, s["layer"], G_end)
                    pe.wait_ge(s_ot, tail_count(s["layer"], s["mixer"]))

        @block.scalar
        def _(act):
            norms = rmss = 0

            def split_high(g, q, n, odd=None):
                src, loaded, count = raw_of(g, odd)
                act.wait_ge(loaded[q], count)
                act.wait_ge(s_half, 2 * g + q // 2 + 1)
                nc.scalar.copy(high[:, q, 0:n, :], src[:, q, 0:n, :]).then_inc(s_high, 1)

            def split_x_high(m):
                for k in range(0, KT, 2):
                    act.wait_ge(s_modd, KT * m + k + 2)
                    T = T1 if m < 2 else SEQ
                    nc.scalar.copy(XH[:, k:k + 2, 0:T], TQ[:, k:k + 2, 0:T]).then_inc(s_xh, 1)

            def residual_rows(m, T):
                for k in range(KT):
                    dst = X[:, k, 0:T] if m < 5 else H[:, k, N_META:T2]
                    nc.scalar.activation(dst, TC[:, k, 0:T], ACT.Identity, bias=sm("xb")[:, k:k + 1],
                                         scale=sm("xg")[:, k:k + 1]).then_inc(s_res, 1)

            rows_due = None
            act.wait_ge(s_tokens, 48)
            cin = cols[:, COLS["c"]:COLS["c"] + 2 * KT]
            nc.scalar.activation(scf[:, 0:2 * KT], cin, ACT.Sigmoid).then_inc(s_silu, 1)
            act.wait_ge(s_sc4, 1)
            scv = scf[:, 2 * KT:4 * KT].rearrange("p (c k) -> p c k", c=2)
            for c in range(2):
                last = nc.scalar.copy(SC4[:, :, SC0 + 2 * c], scv[:, c, :])
            last.then_inc(s_silu, 1)
            split_high(0, 0, 2, 0)
            split_high(0, 1, 2, 0)
            first_mod = True
            for s in steps:
                name, T, np_ = s["name"], s["T"], len(s["panels"])
                if name == "glu" and first_mod:
                    first_mod = False
                    split_x_high(0)

                def splits(i):
                    for pi, (k0, nk) in enumerate(s["panels"]):
                        g = s["g0"] + np_ * i + pi
                        split_high(g, 2, 2)
                        split_high(g, 3, nk - 6)
                        if not is_last(s, i, pi):
                            split_high(g + 1, 0, 2)
                            split_high(g + 1, 1, 2)

                def epilogue(i):
                    G = s["G0"] + i
                    g_last = s["g0"] + np_ * (i + 1)

                    def pair_ready(p):
                        if p == 0:
                            act.wait_ge(s_pair0, G + 1)
                        else:
                            act.wait_ge(s_half, 2 * g_last + 2)

                    if name == "glu":
                        for p in range(2):
                            pair_ready(p)
                            nc.scalar.activation(SG[:, p:p + 1, 0:T], bank(G, 2 * p)[:, :, 0:T],
                                                 ACT.Sigmoid).then_inc(s_act, 1)
                        for p in range(2):
                            act.wait_ge(s_free, 2 * G + p + 5)
                            nc.scalar.copy(GH[:, bass.ds(2 * i + p, 1), 0:T], GB[:, p:p + 1, 0:T]).then_inc(s_hh, 1)
                    elif name == "cgate":
                        for p in range(2):
                            pair_ready(p)
                            act.wait_ge(s_free, 2 * G + p + 3)
                            nc.scalar.copy(SG[:, p:p + 1, 0:T], bank(G, 2 * p)[:, :, 0:T]).then_inc(s_act, 1)
                    elif name == "bgate":
                        for p in range(2):
                            act.wait_ge(s_free, 2 * G + p + 5)
                            nc.scalar.copy(GH[:, bass.ds(4 * i + 2 * p, 2), 0:T],
                                           GB[:, p, :].rearrange("p (a t) -> p a t", a=2)).then_inc(s_hh, 1)
                    elif name in ("gate", "mgate"):
                        for p in range(2):
                            pair_ready(p)
                            nc.scalar.activation(gate_room(s, 4 * i + 2 * p), bank(G, 2 * p, 2)[:, :, 0:T],
                                                 ACT.Sigmoid).then_inc(s_act, 1)
                    elif name == "forget":
                        for p in range(2):
                            pair_ready(p)
                            ps = bank(G, 2 * p, 2)[:, :, 0:T]
                            nc.scalar.activation(MI[:, bass.ds(8 + 4 * i + 2 * p, 2), :], ps,
                                                 ACT.Sigmoid).then_inc(s_act, 1)
                            nc.scalar.activation(MI[:, bass.ds(16 + 4 * i + 2 * p, 2), :], ps, ACT.Sigmoid,
                                                 scale=-1.0).then_inc(s_act, 1)
                    elif name == "conv":
                        for j in range(4):
                            if j % 2 == 0:
                                pair_ready(j // 2)
                            ft = FT * (j % 2) + 2 * i + j // 2
                            nc.scalar.activation(CB[:, j:j + 1, :], bank(G, j)[:, :, 0:T], ACT.Identity,
                                                 bias=col("conv_b", s["layer"] * 2 * FT + ft),
                                                 scale=col("conv_w", (3 * s["layer"] + 2) * 2 * FT + ft)
                                                 ).then_inc(s_act, 1)
                        for p in range(2):
                            act.wait_ge(s_free, 2 * G + p + 5)
                            nc.scalar.activation(SG2[:, p:p + 1, :], CB[:, 2 * p:2 * p + 1, :],
                                                 ACT.Sigmoid).then_inc(s_act, 1)
                        for p in range(2):
                            act.wait_ge(s_gb, s["gb0"] + 2 * i + p + 1)
                            nc.scalar.copy(G2H[:, bass.ds(2 * i + p, 1), :], SG2[:, 2 + p:3 + p, :]).then_inc(s_hh, 1)

                def ada_panels(t, end=False):
                    for x in range(TURN):
                        g = s["g0"] + TURN * t + x
                        after = None if end and x == TURN - 1 else 1 - x % 2
                        for q in range(4):
                            split_high(g + q // 2, (q + 2) % 4, 2, x % 2 if q < 2 else after)

                if name == "ada":
                    turns = ADA // TURN
                    with act.Fori(0, turns - 1) as t:
                        ada_panels(t)
                    ada_panels(turns - 1, end=(s["layer"] == DEPTH - 1))
                    continue
                between = None
                if rows_due is not None:
                    def between(m=rows_due):
                        residual_rows(m, SEQ)
                    rows_due = None
                if name == "gate" and s["tile"] == 16:
                    def between():
                        ret_decays(act, s["layer"])
                if name == "store" and s["tile"] == 24:
                    def between():
                        hg_logs(act, s["layer"])

                groups_behind(act, s, splits, epilogue, between)
                if name == "gate" and s["tile"] == 32:
                    level_exps(act, s["layer"], 0)
                G_end = s["G0"] + s["groups"]
                if s.get("norm"):
                    m = norms
                    for q in range(4):
                        k = slice(2 * q, 2 * q + 2)
                        act.wait_ge(s_cen, 4 * m + q + 1)
                        nc.scalar.activation(TQ[:, k, 0:T], TC[:, k, 0:T], ACT.Square).then_inc(s_sq, 1)
                    act.wait_ge(s_var, m + 1)
                    nc.scalar.activation(RS[:, 0, 0:T], PS[:, norm_bank(G_end) + 1, 0:T], ACT.Ln, bias=epsc[:, 0:1],
                                         scale=1.0 / D).then_inc(s_ln, 1)
                    act.wait_ge(s_ln, m + 1)
                    nc.scalar.activation(RS[:, 1, 0:T], RS[:, 0, 0:T], ACT.Exp, scale=-0.5).then_inc(s_rdev, 1)
                    if m < 5:
                        split_x_high(m + 1)
                    else:
                        act.wait_ge(s_modd, KT * 6 + 1)
                    if m in (0, 5):
                        residual_rows(m, T)
                    else:
                        rows_due = m
                    norms += 1
                    if norms == 6:
                        rms_act(act, 0, G_end)
                        rmss = 1
                if s.get("rms"):
                    rms_act(act, rmss, G_end)
                    rmss += 1
                if name == "v":
                    na_act(act, G_end)
                if "mixer" in s:
                    (ret_act, hg_act, da_act)[s["mixer"]](act, s["layer"], G_end)
                if name == "branch" and s["n"] == 2:
                    for hf in range(2):
                        k = slice(4 * hf, 4 * hf + 4)
                        act.wait_ge(s_yadd, 8 * s["layer"] + 2 * hf + 6)
                        nc.scalar.copy(NHh[:, k, :], Y[:, k, :]).then_inc(s_yh, 1)

        @block.vector
        def _(dve):
            chain = [0]

            def link(ins):
                chain[0] += 1
                ins.then_inc(s_chain, 1)
                dve.wait_ge(s_chain, chain[0])

            norms = rmss = 0
            dve.sem_inc(s_adarow, 1)
            for _ in range(4):
                dve.sem_inc(s_low, 1)
                dve.sem_inc(s_free, 1)

            def split_low(g, q, n, odd=None):
                src = raw_of(g, odd)[0]
                dve.wait_ge(s_high, 4 * g + q + 1)
                nc.vector.tensor_tensor(low[:, q, 0:n, :], src[:, q, 0:n, :], high[:, q, 0:n, :].bitcast(F32),
                                        ALU.subtract).then_inc(s_low, 1)

            def columns(m):
                layer, r = divmod(m, 3)
                ng = (layer * 3 + r - 1) if m else None
                for c in range(2 if m < 2 else 1):
                    v = mod[:, layer, c, :]
                    shift, scale, gate = (v[:, (3 * r + x) * KT:(3 * r + x + 1) * KT] for x in range(3))
                    link(nc.vector.tensor_scalar(sm("ag", c), scale, 1.0, None, ALU.add))
                    if m:
                        link(nc.vector.tensor_tensor(sm("ab", c), sm("ag", c), col("ln_b", ng * KT, KT), ALU.mult))
                        link(nc.vector.tensor_tensor(sm("ab", c), sm("ab", c), shift, ALU.add))
                        link(nc.vector.tensor_tensor(sm("ag", c), sm("ag", c), col("ln_g", ng * KT, KT), ALU.mult))
                    else:
                        link(nc.vector.tensor_copy(sm("ab", c), shift))
                    link(nc.vector.tensor_scalar(sm("gate", c), gate, 0.5 if r != 1 else 1.0, None, ALU.mult))

            def modulate(m, src, T, before=None):
                def rows(hf):
                    if before:
                        before(hf)
                    for k in range(4 * hf, 4 * hf + 4):
                        for c in range(T // SEQ):
                            t = slice(c * SEQ, (c + 1) * SEQ)
                            last = nc.vector.tensor_scalar(TQ[:, k, t], src[:, k, t], sm("ag", c)[:, k:k + 1],
                                                           sm("ab", c)[:, k:k + 1], ALU.mult, ALU.add)
                        last.then_inc(s_modd, 1)

                def x_low(hf):
                    k = slice(4 * hf, 4 * hf + 4)
                    dve.wait_ge(s_xh, 4 * m + 2 * hf + 2)
                    nc.vector.tensor_tensor(XL[:, k, 0:T], TQ[:, k, 0:T], XH[:, k, 0:T].bitcast(F32),
                                            ALU.subtract).then_inc(s_xl, 1)

                rows(0)
                if before:
                    x_low(0)
                    rows(1)
                else:
                    rows(1)
                    x_low(0)
                x_low(1)

            nc.vector.memset(epsc[:], EPS)
            nc.vector.memset(ones[:], 1.0).then_inc(s_ones, 1)
            link(nc.vector.memset(SC4[:].bitcast(I32), 0))
            dve.wait_ge(s_silu, 1)
            cin = cols[:, COLS["c"]:COLS["c"] + 2 * KT]
            nc.vector.tensor_tensor(scf[:, 2 * KT:4 * KT], cin, scf[:, 0:2 * KT], ALU.mult).then_inc(s_sc4, 1)
            dve.wait_ge(s_silu, 2)
            scv = scf[:, 2 * KT:4 * KT].rearrange("p (c k) -> p c k", c=2)
            for c in range(2):
                last = nc.vector.tensor_tensor(SC4[:, :, SC0 + 2 * c + 1], scv[:, c, :],
                                               SC4[:, :, SC0 + 2 * c].bitcast(F32), ALU.subtract)
            last.then_inc(s_sc4, 1)
            split_low(0, 0, 2, 0)
            split_low(0, 1, 2, 0)
            first_mod = True
            for s in steps:
                name, T, np_ = s["name"], s["T"], len(s["panels"])
                if name == "glu" and first_mod:
                    first_mod = False
                    columns(0)
                    modulate(0, X, T1)
                if name == "cgate":
                    nc.vector.memset(UP[:, :, 0:SEQ + 2:SEQ + 1], 0.0)

                def splits(i):
                    for pi, (k0, nk) in enumerate(s["panels"]):
                        g = s["g0"] + np_ * i + pi
                        split_low(g, 2, 2)
                        split_low(g, 3, nk - 6)
                        if not is_last(s, i, pi):
                            split_low(g + 1, 0, 2)
                            split_low(g + 1, 1, 2)

                def epilogue(i):
                    G = s["G0"] + i
                    g_last = s["g0"] + np_ * (i + 1)

                    def pair_ready(p):
                        if p == 0:
                            dve.wait_ge(s_pair0, G + 1)
                        else:
                            dve.wait_ge(s_half, 2 * g_last + 2)

                    if name == "glu":
                        for p in range(2):
                            u = 2 * i + p
                            dve.wait_ge(s_act, s["act0"] + u + 1)
                            nc.vector.tensor_tensor(SG[:, p:p + 1, 0:T], SG[:, p:p + 1, 0:T],
                                                    bank(G, 2 * p)[:, :, 0:T], ALU.mult).then_inc(s_mid, 1)
                            dve.wait_ge(s_mid, s["mid0"] + u + 1)
                            dve.wait_ge(s_hl, s["hid0"] + u + 1)
                            nc.vector.tensor_tensor(GB[:, p:p + 1, 0:T], SG[:, p:p + 1, 0:T],
                                                    bank(G, 2 * p + 1)[:, :, 0:T], ALU.mult).then_inc(s_free, 1)
                    elif name == "res":
                        for j in range(4):
                            if j % 2 == 0:
                                pair_ready(j // 2)
                            if j == 0:
                                dve.wait_ge(s_res, KT * (norms + 1))
                            for c in range(T // SEQ):
                                t = slice(c * SEQ, (c + 1) * SEQ)
                                x = X[:, bass.ds(4 * i + j, 1), t]
                                last = nc.vector.scalar_tensor_tensor(x, bank(G, j)[:, :, t],
                                                                      smcol("gate", 4 * i + j, c), x,
                                                                      ALU.mult, ALU.add)
                            if j % 2:
                                last.then_inc(s_free, 1)
                    elif name in ("q", "k", "v"):
                        for p in range(2):
                            pair_ready(p)
                            ps = bank(G, 2 * p, 2)[:, :, 0:T]
                            tiles = bass.ds(4 * i + 2 * p, 2)
                            if name == "q":
                                nc.vector.tensor_scalar(NQ[:, tiles, :], ps, HD ** -0.5, None,
                                                        ALU.mult).then_inc(s_free, 1)
                            else:
                                nc.vector.tensor_copy((NK if name == "k" else NVT)[:, tiles, :],
                                                      ps).then_inc(s_free, 1)
                    elif name == "cgate":
                        for p in range(2):
                            u = 2 * i + p
                            f = bass.ds(u, 1)
                            dve.wait_ge(s_act, s["act0"] + u + 1)
                            nc.vector.tensor_tensor(UP[:, f, 1:SEQ + 1], SG[:, p:p + 1, 0:T],
                                                    bank(G, 2 * p + 1)[:, :, 0:T], ALU.mult).then_inc(s_free, 1)
                            dve.wait_ge(s_free, 2 * G + p + 5)
                            for tap in range(3):
                                w_tap = col("sc_w", tap * KT + u)
                                x = UP[:, f, tap:tap + SEQ]
                                if tap == 0:
                                    ins = nc.vector.tensor_scalar(CV[:, f, :], x, w_tap, None, ALU.mult)
                                else:
                                    ins = nc.vector.scalar_tensor_tensor(CV[:, f, :], x, w_tap, CV[:, f, :],
                                                                         ALU.mult, ALU.add)
                                ins.then_inc(s_mid, 1)
                                dve.wait_ge(s_mid, s["mid0"] + 6 * i + 3 * p + tap + 1)
                    elif name == "bgate":
                        for p in range(2):
                            pair_ready(p)
                            dve.wait_ge(s_hl, s["hid0"] + 2 * i + p + 1)
                            nc.vector.tensor_tensor(GB[:, p, :].rearrange("p (a t) -> p a t", a=2),
                                                    CV[:, bass.ds(4 * i + 2 * p, 2), :],
                                                    bank(G, 2 * p, 2)[:, :, 0:T], ALU.mult).then_inc(s_free, 1)
                    elif name == "store":
                        for p in range(2):
                            pair_ready(p)
                            n = 4 * i + 2 * p
                            dst = MJ[:, bass.ds(n, 2), :] if s["tile"] == 24 else MI[:, bass.ds(s["tile"] + n, 2), :]
                            nc.vector.tensor_copy(dst, bank(G, 2 * p, 2)[:, :, 0:T]).then_inc(s_free, 1)
                    elif name == "gate":
                        for p in range(2):
                            dve.wait_ge(s_act, s["act0"] + 2 * i + p + 1)
                            d = gate_room(s, 4 * i + 2 * p)
                            nc.vector.tensor_tensor(d, d, bank(G, 2 * p, 2)[:, :, 0:T], ALU.mult).then_inc(s_free, 1)
                    elif name in ("forget", "mgate"):
                        n = 2 if name == "forget" else 1
                        for p in range(2):
                            dve.wait_ge(s_act, s["act0"] + n * (2 * i + p + 1))
                            dve.sem_inc(s_free, 1)
                            if name == "forget":
                                hg_gates(dve, link, s["layer"], 4 * i + 2 * p)
                    elif name == "branch":
                        for p in range(2):
                            pair_ready(p)
                            f = bass.ds(4 * i + 2 * p, 2)
                            ps = bank(G, 2 * p, 2)[:, :, 0:T]
                            dst = Y if s["n"] == 0 else MG
                            nc.vector.tensor_tensor(dst[:, f, :], MG[:, f, :], ps, ALU.mult).then_inc(s_free, 1)
                            if s["n"]:
                                dve.wait_ge(s_free, 2 * G + p + 5)
                                nc.vector.tensor_tensor(Y[:, f, :], Y[:, f, :], MG[:, f, :],
                                                        ALU.add).then_inc(s_yadd, 1)
                    elif name == "add":
                        for p in range(2):
                            pair_ready(p)
                            f = bass.ds(4 * i + 2 * p, 2)
                            nc.vector.tensor_tensor(H[:, f, :], H[:, f, :], bank(G, 2 * p, 2)[:, :, 0:T],
                                                    ALU.add).then_inc(s_free, 1)
                    elif name == "conv":
                        for j in range(4):
                            ft = FT * (j % 2) + 2 * i + j // 2
                            ps = bank(G, j)
                            dve.wait_ge(s_act, s["act0"] + 6 * i + j + 1)
                            for tap in (1, 0):
                                sh = 2 - tap
                                c = CB[:, j:j + 1, sh:T2]
                                ins = nc.vector.scalar_tensor_tensor(
                                    c, ps[:, :, 0:T2 - sh], col("conv_w", (3 * s["layer"] + tap) * 2 * FT + ft), c,
                                    ALU.mult, ALU.add)
                                if tap == 1:
                                    ins.then_inc(s_mid, 1)
                                    dve.wait_ge(s_mid, s["mid0"] + 8 * i + (1, 3, 4, 6)[j])
                                else:
                                    ins.then_inc(s_mid if j % 2 == 0 else s_free, 1)
                        for p in range(2):
                            dve.wait_ge(s_act, s["act0"] + 6 * i + 5 + p)
                            nc.vector.tensor_tensor(SG2[:, p:p + 1, :], SG2[:, p:p + 1, :], CB[:, 2 * p:2 * p + 1, :],
                                                    ALU.mult).then_inc(s_mid, 1)
                            dve.wait_ge(s_mid, s["mid0"] + 8 * i + 7 + p)
                            dve.wait_ge(s_hl, s["hid0"] + 2 * i + p + 1)
                            nc.vector.tensor_tensor(SG2[:, 2 + p:3 + p, :], SG2[:, p:p + 1, :],
                                                    CB[:, 2 * p + 1:2 * p + 2, :], ALU.mult).then_inc(s_gb, 1)

                def ada_panels(t, before, end=False):
                    for x in range(TURN):
                        g = s["g0"] + TURN * t + x
                        after = None if end and x == TURN - 1 else 1 - x % 2
                        for q in range(4):
                            split_low(g + q // 2, (q + 2) % 4, 2, x % 2 if q < 2 else after)
                        if before and x == 0:
                            ada_rows(*before)
                        if before and x == 2:
                            ada_modulation(*before)

                def ada_rows(layer, t):
                    T = ADA // TURN * layer + t
                    dve.wait_ge(s_half, 2 * TURN * (T + 1) + 2)
                    nc.vector.tensor_copy(adarow[:], bank(T, 0).rearrange("p a n -> p (a n)")).then_inc(s_adarow, 1)

                def ada_modulation(layer, t):
                    T = ADA // TURN * layer + t
                    dve.wait_ge(s_pair0, T + 1)
                    parts = bank(T, 2)[:, 0, :].rearrange("p (j i c) -> p c i j", j=4, c=4)
                    bias = col("ada_b", 9 * KT * layer + 4 * TURN * t, 4 * TURN).rearrange("p (i j) -> p i j", j=4)
                    for c in range(2):
                        dst = mod[:, layer, c, bass.ds(4 * TURN * t, 4 * TURN)].rearrange("p (i j) -> p i j", j=4)
                        nc.vector.tensor_tensor(dst, parts[:, 2 * c, 0:TURN, :], bias, ALU.add).then_inc(s_free, 1)
                    for c in range(2):
                        dst = mod[:, layer, c, bass.ds(4 * TURN * t, 4 * TURN)].rearrange("p (i j) -> p i j", j=4)
                        dve.wait_ge(s_free, 2 * T + c + 5)
                        nc.vector.tensor_tensor(dst, dst, parts[:, 2 * c + 1, 0:TURN, :],
                                                ALU.add).then_inc(s_adacol, 1)

                if name == "ada":
                    turns = ADA // TURN
                    ada_panels(0, (s["layer"] - 1, turns - 1) if s["layer"] else None)
                    with dve.Fori(1, turns - 1) as t:
                        ada_panels(t, (s["layer"], t - 1))
                    end = s["layer"] == DEPTH - 1
                    ada_panels(turns - 1, (s["layer"], turns - 2), end=end)
                    if end:
                        ada_rows(s["layer"], turns - 1)
                        ada_modulation(s["layer"], turns - 1)
                        dve.wait_ge(s_adacol, 2 * DEPTH * turns)
                    continue
                between = None
                if name == "gate" and s["tile"] == 32:
                    def between():
                        hg_cumulate(dve, link, s["layer"])
                        right_exponents(dve, s["layer"], 0)

                groups_behind(dve, s, splits, epilogue, between)
                if name == "gate" and s["tile"] == 32:
                    level_operands(dve, s["layer"], 0)
                G_end = s["G0"] + s["groups"]
                if s.get("norm"):
                    m = norms
                    dve.wait_ge(s_sum, m + 1)
                    for q in range(4):
                        k = slice(2 * q, 2 * q + 2)
                        nc.vector.scalar_tensor_tensor(TC[:, k, 0:T], bc(PS[:, norm_bank(G_end), 0:T], 2), -1.0 / D,
                                                       X[:, k, 0:T], ALU.mult, ALU.add).then_inc(s_cen, 1)
                    if m < 5:
                        columns(m + 1)
                    al = ALPHA if m < 5 else 1.0
                    link(nc.vector.tensor_scalar(sm("xg"), col("ln_g", m * KT, KT), al, None, ALU.mult))
                    link(nc.vector.tensor_scalar(sm("xb"), col("ln_b", m * KT, KT), al, None, ALU.mult))
                    dve.wait_ge(s_cen, 4 * (m + 1))
                    dve.wait_ge(s_rdev, m + 1)

                    def standardise(hf):
                        k = slice(4 * hf, 4 * hf + 4)
                        return nc.vector.tensor_tensor(TC[:, k, 0:T], TC[:, k, 0:T], bc(RS[:, 1, 0:T], 4), ALU.mult)

                    if m < 5:
                        modulate(m + 1, TC, T, lambda hf: link(standardise(hf)))
                    else:
                        standardise(0)
                        standardise(1).then_inc(s_modd, 1)
                    norms += 1
                    if norms == 6:
                        rms_dve(dve, 0, "mix_g", 0)
                        rmss = 1
                if s.get("rms"):
                    rms_dve(dve, rmss, *s["rms"])
                    rmss += 1
                if name == "v":
                    na_dve(dve, link, G_end)
                if "mixer" in s:
                    (ret_dve, hg_dve, da_dve)[s["mixer"]](dve, link, s["layer"], G_end)
                if name == "branch" and s["n"] == 2:
                    for hf in range(2):
                        k = slice(4 * hf, 4 * hf + 4)
                        dve.wait_ge(s_yh, 2 * s["layer"] + hf + 1)
                        nc.vector.tensor_tensor(NHl[:, k, :], Y[:, k, :], NHh[:, k, :].bitcast(F32),
                                                ALU.subtract).then_inc(s_yl, 1)

        @block.gpsimd
        def _(pool):
            pool.sem_inc(s_hl, 1)
            pool.sem_inc(s_hl, 1)
            pool.dma_start(cols[:], cols_d).then_inc(s_tokens, 16)
            pool.dma_start(con1[:], const1_d).then_inc(s_tokens, 16)
            pool.dma_start(X[:], tokens).then_inc(s_tokens, 16)
            pool.dma_start(rpb_skew, bass.AP(rpb_d.tensor, 0, [[0, GRID_W], [RPB_W, NH * 7], [1, RPB_W]])
                           ).then_inc(s_skew_out, 16)
            first_mod = True
            for s in steps:
                if s["name"] == "glu" and first_mod:
                    first_mod = False
                    pool.wait_ge(s_tokens, 48)
                    pool.wait_ge(s_modd, KT)
                    for k in range(KT):
                        nc.gpsimd.tensor_scalar(X[:, k, :], X[:, k, :], ALPHA, None, ALU.mult).then_inc(s_res, 1)
                if s["name"] in HIDS:
                    name, T = s["name"], s["T"]
                    for i in groups_of(pool, s):
                        for p in range(2):
                            u = 2 * i + p
                            pool.wait_ge(s_hh, s["hid0"] + u + 1)
                            if name == "glu":
                                f = bass.ds(u, 1)
                                out, x, h = GL[:, f, 0:T], GB[:, p:p + 1, 0:T], GH[:, f, 0:T]
                            elif name == "bgate":
                                f = bass.ds(2 * u, 2)
                                out, h = GL[:, f, 0:T], GH[:, f, 0:T]
                                x = GB[:, p, :].rearrange("p (a t) -> p a t", a=2)
                            else:
                                f = bass.ds(u, 1)
                                out, x, h = G2L[:, f, :], SG2[:, 2 + p:3 + p, :], G2H[:, f, :]
                            nc.gpsimd.tensor_tensor(out, x, h.bitcast(F32), ALU.subtract).then_inc(s_hl, 1)
                G_end = s["G0"] + s["groups"]
                if s["name"] == "res" and s["layer"] == 0 and s["r"] == 0:
                    pool.wait_ge(s_free, 2 * G_end + 4)
                    pool.wait_ge(s_xl, 4)
                    pool.wait_ge(s_skew_out, 16)
                    for rp in range(2):
                        for j in range(6):
                            src = bass.AP(rpb_skew.tensor, (1 - rp + j) * RPB_W + GRID_W - 1,
                                          [[NH * 7 * RPB_W - 1, GRID_W], [7 * RPB_W, NH], [1, GRID_W]])
                            pool.dma_start(TB[64 * rp:64 * rp + 64, :, j, :], src).then_inc(s_bias, 16)
                if s["name"] == "v":
                    na_pool(pool)
                if s["name"] == "res" and s["layer"] == 1 and s["r"] == 2:
                    pool.wait_ge(s_free, 2 * G_end + 4)
                    pool.dma_start(H[:, :, 0:N_META], meta).then_inc(s_meta, 16)
                    pool.dma_start(con2[:], const2_d).then_inc(s_meta, 16)
                if s.get("mixer") == 0:
                    rope_pool(pool, cc("cos_r"), 24 * s["layer"], 8)
                if s.get("mixer") == 2:
                    rope_pool(pool, cc("cos_d"), 24 * s["layer"] + 8, 16)
                if s["name"] == "forget":
                    hg_pool_first(pool, s["layer"], G_end)
                if s.get("mixer") == 1:
                    hg_pool(pool, s["layer"])


_WEIGHTS = ["ada_w", "ffn_w_in", "ffn_w_out", "na_w_qkv", "na_w_out", "sc_w_in", "sc_w_out", "w_in_2",
            "w_branch_2", "w_out_2", "w_ffn_in_2", "w_ffn_out_2"]


def kernel(**inputs):
    import concourse.bacc as bacc
    from concourse.bass_utils import run_bass_kernel_spmd

    a = {k: np.asarray(v) for k, v in inputs.items()}

    def columns(x):
        return np.ascontiguousarray(x).reshape(-1, P).T

    def rows(x):
        return np.ascontiguousarray(x.T.reshape(KT, P, -1).transpose(1, 0, 2))

    lam = np.zeros((P, DEPTH * 4), np.float32)
    lam[0:64] = a["da_lambda_2"][:, [0, 1, 2, 3]].reshape(DEPTH * 4, 64).T
    cols = np.concatenate([
        columns(a["c"]), columns(a["c_ctx"]), columns(a["ada_b"]), columns(a["ln_g"]), columns(a["ln_b"]),
        columns(a["norm_mix_g_2"]), columns(a["norm_ffn_g_2"]), columns(a["norm_final_g_2"]),
        columns(a["sc_conv"]), columns(a["ffn_conv_w_2"]), columns(a["ffn_conv_b_2"]), columns(a["hg_lb_2"]),
        columns(a["da_subln_g_2"]), lam], axis=1)
    rpb = np.zeros((NH, 7, RPB_W), np.float32)
    rpb[:, :, 48:48 + 31] = a["na_rpb"][0][:, 4:11]
    arrays = {name: np.ascontiguousarray(a[name]) for name in _WEIGHTS}
    arrays |= {"tokens": rows(np.concatenate([a["x"][0], a["ctx"][0]])), "meta": rows(a["meta_2"]),
               "cols": np.ascontiguousarray(cols), "const1": first_constants(), "const2": second_constants(),
               "rpb": rpb}
    nc = bacc.Bacc("TRN2", target_bir_lowering=False, num_devices=1)
    ap = {k: nc.dram_tensor(k + "_dram", v.shape, F32, kind="ExternalInput").ap() for k, v in arrays.items()}
    skew = nc.dram_tensor("rpb_skew", (GRID_W, NH * 7, RPB_W), F32, kind="Internal").ap()
    out = nc.dram_tensor("out_dram", (P, KT, SEQ), F32, kind="ExternalOutput").ap()
    two_block_kernel(nc, {k: ap[k] for k in _WEIGHTS}, ap["tokens"], ap["meta"], ap["cols"], ap["const1"],
                     ap["const2"], ap["rpb"], skew, out)
    r = run_bass_kernel_spmd(nc, [{k + "_dram": v for k, v in arrays.items()}], core_ids=[0])
    got = r.results[0]["out_dram"]
    return np.ascontiguousarray(got.transpose(2, 1, 0).reshape(1, SEQ, D))
```
